# Optimizing a Trainium2 kernel written in Bass

```python
import math
import jax
import jax.numpy as jnp
from jax import lax
import numpy as np
import jax, jax.numpy as jnp

D_MODEL = 1024
BATCH = 1
SEQ = 256
DEPTH = 1

BLOCK = 128
EPS = 1e-6

MLA_HEADS = 8
MLA_NOPE = 64
MLA_ROPE = 32
MLA_V = 64
MLA_KV_RANK = 256
ROPE_THETA = 10000.0

DIL_PATTERNS = ((128, 1), (512, 4), (2048, 16))
N_DIL_GROUPS = 3
DIL_HEADS = 8
DIL_HEAD_DIM = 64

N_EXPERT_GROUPS = 4
EXPERTS_PER_GROUP = 8
N_EXPERTS = N_EXPERT_GROUPS * EXPERTS_PER_GROUP
TOP_K_EXPERT = 2
D_FF_EXPERT = 256

MLA_Q_COLS = MLA_HEADS * (MLA_NOPE + MLA_ROPE)
DIL_COLS = 3 * N_DIL_GROUPS * DIL_HEADS * DIL_HEAD_DIM
GATE_COLS = 2 * D_MODEL
IN_COLS = MLA_Q_COLS + MLA_KV_RANK + MLA_ROPE + DIL_COLS + GATE_COLS


def rms_norm(x, g):
    xf = x.astype(jnp.float32)
    y = xf * lax.rsqrt(jnp.mean(xf * xf, axis=-1, keepdims=True) + EPS)
    return (y * g.astype(jnp.float32)).astype(x.dtype)

def alibi_slopes(n):
    return jnp.exp2(-8.0 * (jnp.arange(n, dtype=jnp.float32) + 1.0) / n)

def rope(t, positions):
    half = t.shape[-1] // 2
    freqs = ROPE_THETA ** (-jnp.arange(half, dtype=jnp.float32) / half)
    ang = positions.astype(jnp.float32)[:, :, None] * freqs
    cos = jnp.cos(ang)[:, :, None, :]
    sin = jnp.sin(ang)[:, :, None, :]
    t1 = t[..., :half].astype(jnp.float32)
    t2 = t[..., half:].astype(jnp.float32)
    return jnp.concatenate([t1 * cos - t2 * sin, t2 * cos + t1 * sin], axis=-1).astype(t.dtype)

def causal_block_attention(q, k, v, scale):
    B, S, H, dq = q.shape
    nb = S // BLOCK
    q_blocks = jnp.moveaxis(q.reshape(B, nb, BLOCK, H, dq), 1, 0)
    kpos = jnp.arange(S)

    def one_block(args):
        qb, bi = args
        s = jnp.einsum('bqhd,bkhd->bhqk', qb, k).astype(jnp.float32) * scale
        qpos = bi * BLOCK + jnp.arange(BLOCK)
        s = jnp.where(kpos[None, :] <= qpos[:, None], s, -jnp.inf)
        p = jax.nn.softmax(s, axis=-1)
        return jnp.einsum('bhqk,bkhd->bqhd', p.astype(v.dtype), v)

    o = lax.map(one_block, (q_blocks, jnp.arange(nb)))
    return jnp.moveaxis(o, 0, 1).reshape(B, S, H, v.shape[-1])

def banded_attention(q, k, v, n_back, stride, slopes, scale):
    assert n_back <= BLOCK
    N, L, H, dh = q.shape
    nb = -(-L // BLOCK)
    Lp = nb * BLOCK
    qb = jnp.pad(q, ((0, 0), (0, Lp - L), (0, 0), (0, 0))).reshape(N, nb, BLOCK, H, dh)

    def key_blocks(t):
        tp = jnp.pad(t, ((0, 0), (BLOCK, Lp - L), (0, 0), (0, 0)))
        prev = tp[:, :Lp].reshape(N, nb, BLOCK, H, dh)
        cur = tp[:, BLOCK:].reshape(N, nb, BLOCK, H, dh)
        return jnp.concatenate([prev, cur], axis=2)

    kb = key_blocks(k)
    vb = key_blocks(v)
    s = jnp.einsum('nbqhd,nbkhd->nbhqk', qb, kb).astype(jnp.float32) * scale
    i = jnp.arange(BLOCK)[:, None]
    j = jnp.arange(2 * BLOCK)[None, :]
    delta = i + BLOCK - j
    kpos = jnp.arange(nb)[:, None, None] * BLOCK - BLOCK + j[None]
    valid = (delta >= 0) & (delta <= n_back) & (kpos >= 0)
    bias = -slopes[:, None, None] * (delta * stride).astype(jnp.float32)
    s = jnp.where(valid[None, :, None], s + bias, -jnp.inf)
    m = jnp.max(s, axis=-1, keepdims=True)
    p = jnp.exp(s - m)
    den = jnp.sum(p, axis=-1, keepdims=True)
    o = jnp.einsum('nbhqk,nbkhd->nbqhd', (p / den).astype(v.dtype), vb)
    o = o.reshape(N, Lp, H, dh)[:, :L]
    lse = jnp.transpose((m + jnp.log(den))[..., 0], (0, 1, 3, 2)).reshape(N, Lp, H)[:, :L]
    return o, lse

def mla_branch(q_cols, ckv, k_rope, positions, norm_ckv, w_ukv, q_norm, k_norm):
    B, S, _ = q_cols.shape
    q = q_cols.reshape(B, S, MLA_HEADS, MLA_NOPE + MLA_ROPE)
    kv = (rms_norm(ckv, norm_ckv) @ w_ukv).reshape(B, S, MLA_HEADS, MLA_NOPE + MLA_V)
    k_nope, v = kv[..., :MLA_NOPE], kv[..., MLA_NOPE:]
    k = jnp.concatenate([k_nope, jnp.broadcast_to(k_rope[:, :, None, :], (B, S, MLA_HEADS, MLA_ROPE))], axis=-1)
    q = rms_norm(q, q_norm)
    k = rms_norm(k, k_norm)
    q = jnp.concatenate([q[..., :MLA_NOPE], rope(q[..., MLA_NOPE:], positions)], axis=-1)
    k = jnp.concatenate([k[..., :MLA_NOPE], rope(k[..., MLA_NOPE:], positions)], axis=-1)
    o = causal_block_attention(q, k, v, (MLA_NOPE + MLA_ROPE) ** -0.5)
    return o.reshape(B, S, MLA_HEADS * MLA_V)

def dilated_branch(qkv_cols, q_norm, k_norm):
    B, S, _ = qkv_cols.shape
    H, dh = DIL_HEADS, DIL_HEAD_DIM
    qkv = qkv_cols.reshape(B, S, 3, N_DIL_GROUPS, H, dh)
    q = rms_norm(qkv[:, :, 0], q_norm[:, None, :])
    k = rms_norm(qkv[:, :, 1], k_norm[:, None, :])
    v = qkv[:, :, 2]
    slopes = alibi_slopes(H)
    outs, lses = [], []
    for g, (window, dil) in enumerate(DIL_PATTERNS):
        L = S // dil
        def fold(t):
            return t[:, :, g].reshape(B, L, dil, H, dh).transpose(0, 2, 1, 3, 4).reshape(B * dil, L, H, dh)
        o, lse = banded_attention(fold(q), fold(k), fold(v), window // dil, dil, slopes, dh ** -0.5)
        outs.append(o.reshape(B, dil, L, H, dh).transpose(0, 2, 1, 3, 4).reshape(B, S, H, dh))
        lses.append(lse.reshape(B, dil, L, H).transpose(0, 2, 1, 3).reshape(B, S, H))
    w = jax.nn.softmax(jnp.stack(lses, axis=0), axis=0)
    o = jnp.sum(w[..., None] * jnp.stack(outs, axis=0).astype(jnp.float32), axis=0)
    return o.astype(qkv_cols.dtype).reshape(B, S, H * dh)

def hier_moe(h, w_rg, b_rg, w_re, b_re, w_gate, w_up, w_down):
    B, S, D = h.shape
    T = B * S
    hf = h.reshape(T, D)
    gp = jax.nn.softmax((hf @ w_rg + b_rg).astype(jnp.float32), axis=-1)
    g_p, g_i = lax.top_k(gp, 1)
    g_p, g_i = g_p[:, 0], g_i[:, 0]
    el = (hf @ w_re + b_re).astype(jnp.float32).reshape(T, N_EXPERT_GROUPS, EXPERTS_PER_GROUP)
    el_sel = el[jnp.arange(T), g_i]
    ep = jax.nn.softmax(el_sel, axis=-1)
    e_p, e_i = lax.top_k(ep, TOP_K_EXPERT)
    e_p = e_p / jnp.sum(e_p, axis=-1, keepdims=True)
    weights = g_p[:, None] * e_p
    expert_idx = g_i[:, None] * EXPERTS_PER_GROUP + e_i
    combine = jnp.sum(jax.nn.one_hot(expert_idx, N_EXPERTS, dtype=jnp.float32) * weights[..., None], axis=1)
    combine = combine.astype(hf.dtype)
    y = jnp.zeros_like(hf)
    for e in range(N_EXPERTS):
        he = jax.nn.silu(hf @ w_gate[e]) * (hf @ w_up[e])
        y = y + combine[:, e:e + 1] * (he @ w_down[e])
    return y.reshape(B, S, D)

def first_inputs(seed: int = 0) -> dict:
    key = jax.random.key(seed)
    ks = jax.random.split(key, 24)

    def nrm(k, shape, fan_in):
        return jax.random.normal(k, shape, jnp.float32) * (fan_in ** -0.5)

    def gain(k, shape):
        return 1.0 + 0.02 * jax.random.normal(k, shape, jnp.float32)

    def bias(k, shape, scale):
        return scale * jax.random.normal(k, shape, jnp.float32)

    Ld = DEPTH
    return {
        'x': jax.random.normal(ks[0], (BATCH, SEQ, D_MODEL), jnp.float32),
        'positions': jnp.broadcast_to(jnp.arange(SEQ, dtype=jnp.int32), (BATCH, SEQ)),
        'norm_attn': gain(ks[1], (Ld, D_MODEL)),
        'w_in': nrm(ks[2], (Ld, D_MODEL, IN_COLS), D_MODEL),
        'b_gate': bias(ks[3], (Ld, 2, D_MODEL), 0.02),
        'norm_ckv': gain(ks[4], (Ld, MLA_KV_RANK)),
        'w_ukv': nrm(ks[5], (Ld, MLA_KV_RANK, MLA_HEADS * (MLA_NOPE + MLA_V)), MLA_KV_RANK),
        'q_norm_mla': gain(ks[6], (Ld, MLA_NOPE + MLA_ROPE)),
        'k_norm_mla': gain(ks[7], (Ld, MLA_NOPE + MLA_ROPE)),
        'q_norm_dil': gain(ks[8], (Ld, N_DIL_GROUPS, DIL_HEAD_DIM)),
        'k_norm_dil': gain(ks[9], (Ld, N_DIL_GROUPS, DIL_HEAD_DIM)),
        'w_o_mla': nrm(ks[10], (Ld, MLA_HEADS * MLA_V, D_MODEL), MLA_HEADS * MLA_V),
        'w_o_dil': nrm(ks[11], (Ld, DIL_HEADS * DIL_HEAD_DIM, D_MODEL), DIL_HEADS * DIL_HEAD_DIM),
        'w_out': nrm(ks[12], (Ld, D_MODEL, D_MODEL), D_MODEL),
        'norm_ffn': gain(ks[13], (Ld, D_MODEL)),
        'w_router_group': nrm(ks[14], (Ld, D_MODEL, N_EXPERT_GROUPS), D_MODEL),
        'b_router_group': bias(ks[15], (Ld, N_EXPERT_GROUPS), 0.01),
        'w_router_expert': nrm(ks[16], (Ld, D_MODEL, N_EXPERTS), D_MODEL),
        'b_router_expert': bias(ks[17], (Ld, N_EXPERTS), 0.01),
        'w_gate': nrm(ks[18], (Ld, N_EXPERTS, D_MODEL, D_FF_EXPERT), D_MODEL),
        'w_up': nrm(ks[19], (Ld, N_EXPERTS, D_MODEL, D_FF_EXPERT), D_MODEL),
        'w_down': nrm(ks[20], (Ld, N_EXPERTS, D_FF_EXPERT, D_MODEL), D_FF_EXPERT),
    }

def first_block(x, positions, norm_attn, w_in, b_gate, norm_ckv, w_ukv, q_norm_mla, k_norm_mla,
              q_norm_dil, k_norm_dil, w_o_mla, w_o_dil, w_out, norm_ffn, w_router_group,
              b_router_group, w_router_expert, b_router_expert, w_gate, w_up, w_down):
    B, S, D = x.shape
    splits = [MLA_Q_COLS, MLA_Q_COLS + MLA_KV_RANK, MLA_Q_COLS + MLA_KV_RANK + MLA_ROPE,
              MLA_Q_COLS + MLA_KV_RANK + MLA_ROPE + DIL_COLS]
    for l in range(DEPTH):
        h = rms_norm(x, norm_attn[l])
        proj = h @ w_in[l]
        q_mla, ckv, k_rope, qkv_dil, gate_pre = jnp.split(proj, splits, axis=-1)
        o_mla = mla_branch(q_mla, ckv, k_rope, positions, norm_ckv[l], w_ukv[l],
                           q_norm_mla[l], k_norm_mla[l])
        o_dil = dilated_branch(qkv_dil, q_norm_dil[l], k_norm_dil[l])
        gates = jax.nn.sigmoid(gate_pre.reshape(B, S, 2, D) + b_gate[l])
        merged = gates[:, :, 0] * (o_mla @ w_o_mla[l]) + gates[:, :, 1] * (o_dil @ w_o_dil[l])
        x = x + merged @ w_out[l]
        h2 = rms_norm(x, norm_ffn[l])
        x = x + hier_moe(h2, w_router_group[l], b_router_group[l], w_router_expert[l],
                         b_router_expert[l], w_gate[l], w_up[l], w_down[l])
    return x


DEPTH_2 = 2

HEAD_DIM = 128
MOBA_HEADS = 4
RET_HEADS = 4
MOBA_BLOCK = 256
MOBA_TOPK = 3
MOBA_QCHUNK = 32
RET_CHUNK = 128
CONV_WIDTH = 3
PEER_HEADS = 8
PEER_NKEYS = 128
PEER_NEXPERTS = PEER_NKEYS * PEER_NKEYS
PEER_TOPK = 16
PEER_DKEY = 256
PEER_TOKCHUNK = 128
N_EVEN = (DEPTH_2 + 1) // 2
N_ODD = DEPTH_2 // 2
MOBA_W = MOBA_HEADS * HEAD_DIM
RET_W = RET_HEADS * HEAD_DIM
EVEN_SPLITS = (MOBA_W, MOBA_W, MOBA_W, RET_W, RET_W, RET_W, RET_W)
EVEN_IN = sum(EVEN_SPLITS)
EVEN_OUT_IN = MOBA_W + RET_W


def rmsnorm(x, g):
    xf = x.astype(jnp.float32)
    y = xf * lax.rsqrt(jnp.mean(xf * xf, axis=-1, keepdims=True) + EPS)
    return (y * g.astype(jnp.float32)).astype(x.dtype)

def rope_2(t):
    s, dh = t.shape[2], t.shape[3]
    half = dh // 2
    inv = ROPE_THETA ** (-jnp.arange(half, dtype=jnp.float32) / half)
    ang = jnp.arange(s, dtype=jnp.float32)[:, None] * inv[None, :]
    cos = jnp.cos(ang).astype(t.dtype)
    sin = jnp.sin(ang).astype(t.dtype)
    t1, t2 = t[..., :half], t[..., half:]
    return jnp.concatenate([t1 * cos - t2 * sin, t2 * cos + t1 * sin], axis=-1)

def split_heads(t, n):
    b, s, _ = t.shape
    return t.reshape(b, s, n, HEAD_DIM).transpose(0, 2, 1, 3)

def merge_heads(t):
    b, h, s, dh = t.shape
    return t.transpose(0, 2, 1, 3).reshape(b, s, h * dh)

def moba_attention(q, k, v):
    b, h, s, dh = q.shape
    nb = -(-s // MOBA_BLOCK)
    pad = nb * MOBA_BLOCK - s
    kb = jnp.pad(k, ((0, 0), (0, 0), (0, pad), (0, 0))).reshape(b, h, nb, MOBA_BLOCK, dh)
    vb = jnp.pad(v, ((0, 0), (0, 0), (0, pad), (0, 0))).reshape(b, h, nb, MOBA_BLOCK, dh)
    counts = jnp.minimum(MOBA_BLOCK, s - jnp.arange(nb) * MOBA_BLOCK).astype(jnp.float32)
    kmean = kb.astype(jnp.float32).sum(axis=3) / counts[None, None, :, None]
    gate = jnp.einsum('bhsd,bhnd->bhsn', q.astype(jnp.float32), kmean)
    qblk = jnp.arange(s) // MOBA_BLOCK
    past = jnp.arange(nb)[None, :] < qblk[:, None]
    gate = jnp.where(past, gate, -jnp.inf)
    kk = min(MOBA_TOPK, nb)
    _, sel = lax.top_k(gate, kk)
    valid = sel < qblk[:, None]
    nq = s // MOBA_QCHUNK
    def chunked(t):
        return t.reshape(b, h, nq, MOBA_QCHUNK, *t.shape[3:]).transpose(2, 0, 1, 3, *range(4, t.ndim + 1))
    qs, sels, valids = chunked(q), chunked(sel), chunked(valid)
    scale = dh ** -0.5
    bi = jnp.arange(b)[:, None, None, None]
    hi = jnp.arange(h)[None, :, None, None]

    def step(args):
        ci, qc, selc, validc = args
        tpos = ci * MOBA_QCHUNK + jnp.arange(MOBA_QCHUNK)
        ob = (ci * MOBA_QCHUNK) // MOBA_BLOCK
        k_own = lax.dynamic_index_in_dim(kb, ob, axis=2, keepdims=False)
        v_own = lax.dynamic_index_in_dim(vb, ob, axis=2, keepdims=False)
        kpos = ob * MOBA_BLOCK + jnp.arange(MOBA_BLOCK)
        s_own = jnp.einsum('bhqd,bhkd->bhqk', qc, k_own).astype(jnp.float32) * scale
        s_own = jnp.where(kpos[None, :] <= tpos[:, None], s_own, -jnp.inf)
        kg = kb[bi, hi, selc]
        vg = vb[bi, hi, selc]
        s_sel = jnp.einsum('bhqd,bhqjkd->bhqjk', qc, kg).astype(jnp.float32) * scale
        s_sel = jnp.where(validc[..., None], s_sel, -jnp.inf)
        scores = jnp.concatenate([s_sel.reshape(b, h, MOBA_QCHUNK, kk * MOBA_BLOCK), s_own], axis=-1)
        p = jax.nn.softmax(scores, axis=-1).astype(v.dtype)
        p_sel = p[..., :kk * MOBA_BLOCK].reshape(b, h, MOBA_QCHUNK, kk, MOBA_BLOCK)
        p_own = p[..., kk * MOBA_BLOCK:]
        return (jnp.einsum('bhqjk,bhqjkd->bhqd', p_sel, vg)
                + jnp.einsum('bhqk,bhkd->bhqd', p_own, v_own))

    out = lax.map(step, (jnp.arange(nq), qs, sels, valids))
    return out.transpose(1, 2, 0, 3, 4).reshape(b, h, s, dh)

def retention(q, k, v):
    b, h, s, dh = q.shape
    c = RET_CHUNK
    nc = s // c
    log_g = jnp.log(1.0 - 2.0 ** (-5.0 - jnp.arange(h, dtype=jnp.float32)))
    idx = jnp.arange(c, dtype=jnp.float32)
    diff = idx[:, None] - idx[None, :]
    dmask = jnp.where(diff >= 0, jnp.exp(log_g[:, None, None] * jnp.maximum(diff, 0.0)), 0.0)
    xi = jnp.exp(log_g[:, None] * (idx + 1.0))[..., None]
    zeta = jnp.exp(log_g[:, None] * (c - 1.0 - idx))[..., None]
    gc = jnp.exp(log_g * c)[:, None, None]
    def chunked(t):
        return t.astype(jnp.float32).reshape(b, h, nc, c, dh).transpose(2, 0, 1, 3, 4)
    qs, ks, vs = chunked(q), chunked(k * (dh ** -0.5)), chunked(v)

    def step(state, inp):
        qc, kc, vc = inp
        inner = jnp.einsum('bhnd,bhmd->bhnm', qc, kc) * dmask
        o = jnp.einsum('bhnm,bhmd->bhnd', inner, vc) + jnp.einsum('bhnd,bhde->bhne', qc, state) * xi
        state = state * gc + jnp.einsum('bhmd,bhme->bhde', kc * zeta, vc)
        return state, o

    state0 = jnp.zeros((b, h, dh, dh), jnp.float32)
    _, outs = lax.scan(step, state0, (qs, ks, vs))
    return outs.transpose(1, 2, 0, 3, 4).reshape(b, h, s, dh)

def attn_retention_mixer(xn, w_in, w_out):
    proj = xn @ w_in
    cuts = list(np.cumsum(EVEN_SPLITS)[:-1])
    mq, mk, mv, rq, rk, rv, rg = jnp.split(proj, cuts, axis=-1)
    mq, mk, mv = split_heads(mq, MOBA_HEADS), split_heads(mk, MOBA_HEADS), split_heads(mv, MOBA_HEADS)
    rq, rk, rv = split_heads(rq, RET_HEADS), split_heads(rk, RET_HEADS), split_heads(rv, RET_HEADS)
    mo = merge_heads(moba_attention(rope_2(mq), rope_2(mk), mv))
    ro = retention(rope_2(rq), rope_2(rk), rv)
    ro = ro * lax.rsqrt(jnp.mean(ro * ro, axis=-1, keepdims=True) + EPS)
    ro = merge_heads(ro).astype(xn.dtype) * jax.nn.silu(rg)
    return jnp.concatenate([mo, ro], axis=-1) @ w_out

def short_conv_mixer(xn, w_in, conv_w, w_out):
    d = xn.shape[-1]
    bg, cg, hx = jnp.split(xn @ w_in, 3, axis=-1)
    u = cg * hx
    y = lax.conv_general_dilated(u, conv_w[:, None, :], window_strides=(1,),
                                 padding=[(CONV_WIDTH - 1, 0)],
                                 dimension_numbers=('NWC', 'WIO', 'NWC'),
                                 feature_group_count=d)
    return (bg * y) @ w_out

def peer(xn, w_q, sub_keys, u, v):
    b, s, d = xn.shape
    t = xn.reshape(b * s, d)
    n_tok = b * s
    q = (t @ w_q).reshape(n_tok, PEER_HEADS, 2, PEER_DKEY // 2)
    sc = jnp.einsum('thpd,hpnd->thpn', q, sub_keys).astype(jnp.float32)
    s1, i1 = lax.top_k(sc[:, :, 0], PEER_TOPK)
    s2, i2 = lax.top_k(sc[:, :, 1], PEER_TOPK)
    cand = (s1[..., :, None] + s2[..., None, :]).reshape(n_tok, PEER_HEADS, PEER_TOPK * PEER_TOPK)
    cidx = (i1[..., :, None] * PEER_NKEYS + i2[..., None, :]).reshape(n_tok, PEER_HEADS, PEER_TOPK * PEER_TOPK)
    top_s, pos = lax.top_k(cand, PEER_TOPK)
    eidx = jnp.take_along_axis(cidx, pos, axis=-1)
    gate = jax.nn.softmax(top_s, axis=-1).astype(xn.dtype)
    nt = n_tok // PEER_TOKCHUNK

    def step(args):
        tc, ec, gc = args
        hid = jax.nn.gelu(jnp.einsum('td,thkd->thk', tc, u[ec]), approximate=False)
        return jnp.einsum('thk,thkd->td', gc * hid, v[ec])

    out = lax.map(step, (t.reshape(nt, PEER_TOKCHUNK, d),
                         eidx.reshape(nt, PEER_TOKCHUNK, PEER_HEADS, PEER_TOPK),
                         gate.reshape(nt, PEER_TOKCHUNK, PEER_HEADS, PEER_TOPK)))
    return out.reshape(b, s, d)

def second_inputs(seed: int = 0) -> dict:
    key = jax.random.key(seed)
    ks = jax.random.split(key, 16)
    f32 = jnp.float32
    nrm = lambda k, shape, sc: jax.random.normal(k, shape, f32) * sc
    return {
        "x": nrm(ks[0], (BATCH, SEQ, D_MODEL), 1.0),
        "norm_mix": 1.0 + nrm(ks[1], (DEPTH_2, D_MODEL), 0.02),
        "norm_ffn": 1.0 + nrm(ks[2], (DEPTH_2, D_MODEL), 0.02),
        "even_w_in": nrm(ks[3], (N_EVEN, D_MODEL, EVEN_IN), D_MODEL ** -0.5),
        "even_w_out": nrm(ks[4], (N_EVEN, EVEN_OUT_IN, D_MODEL), EVEN_OUT_IN ** -0.5),
        "odd_w_in": nrm(ks[5], (N_ODD, D_MODEL, 3 * D_MODEL), D_MODEL ** -0.5),
        "odd_conv": nrm(ks[6], (N_ODD, CONV_WIDTH, D_MODEL), CONV_WIDTH ** -0.5),
        "odd_w_out": nrm(ks[7], (N_ODD, D_MODEL, D_MODEL), D_MODEL ** -0.5),
        "peer_w_q": nrm(ks[8], (DEPTH_2, D_MODEL, PEER_HEADS * PEER_DKEY), D_MODEL ** -0.5),
        "peer_sub_keys": nrm(ks[9], (DEPTH_2, PEER_HEADS, 2, PEER_NKEYS, PEER_DKEY // 2), (PEER_DKEY // 2) ** -0.5),
        "peer_u": nrm(ks[10], (DEPTH_2, PEER_NEXPERTS, D_MODEL), D_MODEL ** -0.5),
        "peer_v": nrm(ks[11], (DEPTH_2, PEER_NEXPERTS, D_MODEL), 0.1),
        "final_norm": 1.0 + nrm(ks[12], (D_MODEL,), 0.02),
    }

def second_block(x, norm_mix, norm_ffn, even_w_in, even_w_out, odd_w_in, odd_conv, odd_w_out,
              peer_w_q, peer_sub_keys, peer_u, peer_v, final_norm):
    h = x
    for layer in range(DEPTH_2):
        xn = rmsnorm(h, norm_mix[layer])
        i = layer // 2
        if layer % 2 == 0:
            h = h + attn_retention_mixer(xn, even_w_in[i], even_w_out[i])
        else:
            h = h + short_conv_mixer(xn, odd_w_in[i], odd_conv[i], odd_w_out[i])
        h = h + peer(rmsnorm(h, norm_ffn[layer]), peer_w_q[layer], peer_sub_keys[layer],
                     peer_u[layer], peer_v[layer])
    return rmsnorm(h, final_norm)


def setup_inputs(seed=0):
    out = dict(first_inputs(seed))
    for name, value in second_inputs(seed + 1).items():
        if name != "x":
            out[name + "_2"] = value
    return out


def reference(
    x, positions, norm_attn, w_in, b_gate, norm_ckv, w_ukv, q_norm_mla, k_norm_mla, q_norm_dil,
    k_norm_dil, w_o_mla, w_o_dil, w_out, norm_ffn, w_router_group, b_router_group,
    w_router_expert, b_router_expert, w_gate, w_up, w_down, norm_mix_2, norm_ffn_2, even_w_in_2,
    even_w_out_2, odd_w_in_2, odd_conv_2, odd_w_out_2, peer_w_q_2, peer_sub_keys_2, peer_u_2,
    peer_v_2, final_norm_2,
):
    x = first_block(
        x, positions, norm_attn, w_in, b_gate, norm_ckv, w_ukv, q_norm_mla, k_norm_mla,
        q_norm_dil, k_norm_dil, w_o_mla, w_o_dil, w_out, norm_ffn, w_router_group,
        b_router_group, w_router_expert, b_router_expert, w_gate, w_up, w_down,
    )
    return second_block(
        x, norm_mix_2, norm_ffn_2, even_w_in_2, even_w_out_2, odd_w_in_2, odd_conv_2,
        odd_w_out_2, peer_w_q_2, peer_sub_keys_2, peer_u_2, peer_v_2, final_norm_2,
    )


_drawn_inputs = setup_inputs


def setup_inputs(seed=0):
    import zlib

    import numpy as np

    out = dict(_drawn_inputs(seed))
    spreads = {}
    factors = {'b_gate': 8.0,
     'q_norm_mla': 5.386,
     'k_norm_mla': 4.509,
     'q_norm_dil': 8.0,
     'b_router_group': 24.736,
     'b_router_expert': 3.621,
     'norm_ffn_2': 5.43,
     'final_norm_2': 8.004}
    for name, (base, spread) in spreads.items():
        noise = np.random.default_rng([zlib.crc32(name.encode()), seed]).standard_normal(out[name].shape)
        drawn = base * np.exp(spread * noise) if base else spread * noise
        out[name] = jnp.asarray(drawn.astype(out[name].dtype))
    for name, factor in factors.items():
        out[name] = (out[name] * factor).astype(out[name].dtype)
    return out
```

```python
from contextlib import ExitStack

import numpy as np

import concourse.bass as bass
from concourse import mybir

P = 128
F32 = mybir.dt.float32
I32 = mybir.dt.int32
U32 = mybir.dt.uint32
ALU = mybir.AluOpType
ACT = mybir.ActivationFunctionType
X = mybir.AxisListType.X
EPS = 1e-6
NEG = -1e30
T = 256
D = 1024

NSLOT = 6
NG = 14
AR = 28288


class Queues:

    def __init__(self, sems):
        self.sems = sems
        self.count = {e: 0 for e in sems}
        self.items = {e: [] for e in sems}
        self.seen = {e: {} for e in sems}
        self.dma_count = {}

    def waits(self, eng, after):
        need = {}
        stack = list(after)
        while stack:
            a = stack.pop()
            if a is None:
                continue
            if isinstance(a, list):
                stack += a
                continue
            sem, value = a
            if value > self.seen[eng].get(sem.name, 0):
                need[sem.name] = (sem, max(value, need.get(sem.name, (None, 0))[1]))
        for name, (sem, value) in need.items():
            self.seen[eng][name] = value
        return list(need.values())

    def put(self, eng, fn, *after):
        self.count[eng] += 1
        self.items[eng].append((self.waits(eng, after), fn, self.sems[eng], 1))
        return (self.sems[eng], self.count[eng])

    def dma(self, eng, fn, sem, *after):
        self.dma_count[sem.name] = self.dma_count.get(sem.name, 0) + 16
        self.items[eng].append((self.waits(eng, after), fn, sem, 16))
        return (sem, self.dma_count[sem.name])

    def wait(self, eng, *after):
        self.items[eng].append((self.waits(eng, after), None, None, 0))

    def all_done(self):
        return [(self.sems[e], self.count[e]) for e in self.sems if self.count[e]]

    def emit(self, name, eng):
        for waits, fn, sem, n in self.items[name]:
            for s, v in waits:
                eng.wait_ge(s, v)
            if fn is not None:
                fn(eng).then_inc(sem, n)


def build(nc, a, out):
    ctx = ExitStack()
    with ctx:
        def sb(name, shape, dt=F32):
            return ctx.enter_context(nc.sbuf_tensor(name, shape, dt))

        def sem(name):
            return ctx.enter_context(nc.semaphore(name))

        q = Queues({e: sem("s_" + e) for e in ("pe", "dve", "act", "pool")})
        put, dma = q.put, q.dma

        def vec(fn, *after):
            return put("dve", fn, (q.sems["dve"], q.count["dve"]), *after)

        def scal(fn, *after):
            return put("act", fn, (q.sems["act"], q.count["act"]), *after)

        x = sb("x", [P, 2, D])
        xn = sb("xn", [P, 2, D])
        hT = sb("hT", [P, 8, T])
        ring = sb("ring", [P, NSLOT, 2048])
        ident = sb("ident", [P, P])
        gain = sb("gain", [P, 2, D])
        small = sb("small", [P, 2560])
        arena = sb("arena", [P, AR])
        banks = ctx.enter_context(nc.psum_tensor("banks", [P, 8, 512], F32))

        bank_free = [None] * 8
        bank_next = [0]

        def bank():
            b = bank_next[0] % 8
            bank_next[0] += 1
            return b

        slot_free = [None] * NSLOT
        slot_sem = [sem(f"s_slot{i}") for i in range(NSLOT)]
        slot_next = [0]

        def load(src, n):
            s = slot_next[0] % NSLOT
            slot_next[0] += 1
            dst = ring[:, s, 0:n * src.shape[2]].rearrange("p (k c) -> p k c", k=n)
            tok = dma("sp", lambda e: e.dma_start(dst, src), slot_sem[s], slot_free[s])
            return s, dst, tok

        q.items["sp"], q.seen["sp"] = [], {}

        const_sem = [0]

        def fetch(dst, src, *after, eng="act"):
            const_sem[0] += 1
            return dma(eng, lambda e: e.dma_start(dst, src), sem(f"s_c{const_sem[0]}"), *after)

        def row(ap, n):
            return ap.unsqueeze(0).to_broadcast([P, n])

        smallp = [0]

        def sm(*shape):
            n = int(np.prod(shape))
            if smallp[0] + n > 2560:
                raise ValueError("small")
            v = small[:, smallp[0]:smallp[0] + n]
            smallp[0] += n
            if len(shape) == 2:
                v = v.rearrange("p (a b) -> p a b", a=shape[0])
            if len(shape) == 3:
                v = v.rearrange("p (a b c) -> p a b c", a=shape[0], b=shape[1])
            return v

        mhalf = sm(64)
        t_mh = put("pool", lambda e: e.memset(mhalf, -0.5))
        t_id = fetch(ident[:, :], a["c_ident"], eng="sp")

        def rsqrt(dst, ss, n, *after):
            m = dst.shape[1]
            t = vec(lambda e: e.tensor_scalar(dst, ss, 1.0 / n, EPS, ALU.mult, ALU.add), *after)
            return put("pool", lambda e: e.tensor_tensor(dst, dst, mhalf[:, 0:m], ALU.pow), t, t_mh)

        def q_pe():
            return (q.sems["pe"], q.count["pe"])

        evac_turn = [0]

        def copy(eng, dst, src, *after):
            if eng == "act":
                return put("act", lambda e: e.copy(dst, src), *after)
            return put("dve", lambda e: e.tensor_copy(dst, src), *after)

        def evac(dst, src, *after):
            evac_turn[0] ^= 1
            return copy("act" if evac_turn[0] else "dve", dst, src, *after)

        def transposes(pairs, *after, eng=None):
            toks = []
            for dst, srcs in pairs:
                m = srcs[0].shape[1]
                b = bank()

                def go(e, b=b, srcs=srcs, m=m):
                    for i, s in enumerate(srcs):
                        r = e.transpose(banks[0:m, b, i * P:(i + 1) * P], s, ident[:, :])
                    return r
                t = put("pe", go, list(after), t_id, bank_free[b])
                n = len(srcs)
                src = banks[0:m, b, 0:n * P].rearrange("p (k c) -> p k c", k=n)
                t = copy(eng, dst, src, t) if eng else evac(dst, src, t)
                bank_free[b] = t
                toks.append(t)
            return toks

        gain_free = [None, None]
        gain_n = [0]

        def load_gain(src):
            g = gain_n[0] % 2
            gain_n[0] += 1
            return g, fetch(gain[:, g, :], row(src, D), gain_free[g])

        def rmsnorm(g, t_x, t_free, to_T=True):
            gi, t_g = g
            ss = sm(2)
            toks = []
            for c in range(2):
                t = scal(lambda e, c=c: e.activation(xn[:, c, :], x[:, c, :], ACT.Square,
                                                           accum_out=ss[:, c:c + 1]), t_x, t_free)
                t = rsqrt(ss[:, c:c + 1], ss[:, c:c + 1], D, t)
                t = vec(lambda e, c=c: e.scalar_tensor_tensor(
                    xn[:, c, :], x[:, c, :], ss[:, c:c + 1], gain[:, gi, :], ALU.mult, ALU.mult), t, t_g)
                toks.append(t)
            gain_free[gi] = toks[1]
            if not to_T:
                return toks, None
            tt = []
            for c in range(2):
                tt += transposes([(hT[:, k:k + 4, c * P:(c + 1) * P],
                                   [xn[:, c, (k + i) * P:(k + i + 1) * P] for i in range(4)])
                                  for k in (0, 4)], toks[c])
            return toks, tt

        def project(w, c0, n, sink, t_h, lhs=None, kn=8):
            lhs = hT if lhs is None else lhs
            per = max(1, 2048 // n)
            b = [bank(), bank()]
            k = 0
            while k < kn:
                m = min(per, kn - k, 4 if n == 512 else 8)
                s, wt, t_w = load(w[:, k:k + m, c0:c0 + n], m)
                for c in range(2):
                    def go(e, c=c, k=k, m=m, wt=wt):
                        for i in range(m):
                            r = e.matmul(banks[:, b[c], 0:n], lhs[:, k + i, c * P:(c + 1) * P], wt[:, i, :],
                                         start=(k + i == 0), stop=(k + i == kn - 1))
                        return r
                    t = put("pe", go, t_w, t_h, bank_free[b[c]] if k == 0 else None)
                    if k + m == kn:
                        bank_free[b[c]] = sink(c, banks[:, b[c], 0:n], t)
                slot_free[s] = t
                k += m

        def kview(w):
            return w.rearrange("(k p) n -> p k n", p=P)

        t_x = fetch(x[:, :, :], a["x"][0].rearrange("(c p) d -> p c d", p=P), eng="sp")

        def finish(src, t):
            t_o = fetch(out[0].rearrange("(c p) d -> p c d", p=P), src, t, eng="sp")
            q.wait("sp", t_o)

        Pj = arena[:, 0:2 * 7712].rearrange("p (c n) -> p c n", c=2)
        off = 2 * 7712
        qd = arena[:, off:off + 3072].rearrange("p (j t) -> p j t", t=T)
        kd = arena[:, off + 3072:off + 6144].rearrange("p (j t) -> p j t", t=T)
        off += 6144
        Bm = arena[:, off:off + 3 * 128 + 3 * 256]
        off += 1152
        cm = arena[:, off:off + 384]
        off += 384
        E = arena[:, off:off + 2 * 768].rearrange("p (i n) -> p i n", i=2)
        off += 1536
        PT = arena[:, off:off + 2 * 768].rearrange("p (i n) -> p i n", i=2)
        off += 1536
        O = xn[:, 0, :].rearrange("p (c n) -> p c n", c=2)
        OT = xn[:, 1, :].rearrange("p (k t) -> p k t", k=4)
        bg = arena[:, off:off + 2048]
        off += 2048
        assert off <= AR, off
        vecs = sb("vecs", [P, 848])

        g_attn = load_gain(a["norm_attn"][0])
        g_ffn = load_gain(a["norm_ffn"][0])
        t_B = fetch(Bm, a["c_band"])
        t_cm = fetch(cm, a["c_causal"])
        t_bg = fetch(bg, row(a["b_gate"].rearrange("l g d -> (l g d)"), 2048))
        nckv = vecs[:, 0:256]
        t_v = [fetch(nckv, row(a["norm_ckv"][0], 256)),
               fetch(vecs[:, 256:352], row(a["q_norm_mla"][0], 96)),
               fetch(vecs[:, 352:448], row(a["k_norm_mla"][0], 96)),
               fetch(vecs[:, 448:640], row(a["q_norm_dil"].rearrange("l g d -> (l g d)"), 192)),
               fetch(vecs[:, 640:832], row(a["k_norm_dil"].rearrange("l g d -> (l g d)"), 192)),
               fetch(vecs[:, 832:848], a["c_freq"])]
        rb = sm(36)
        rw = sm(8, 36)
        t_v += [fetch(rb[:, 0:4], row(a["b_router_group"][0], 4)),
                fetch(rb[:, 4:36], row(a["b_router_expert"][0], 32)),
                fetch(rw[:, :, 0:4], kview(a["w_router_group"][0])),
                fetch(rw[:, :, 4:36], kview(a["w_router_expert"][0]))]
        pos_i = sb("pos_i", [P, 2], I32)
        t_pos = fetch(pos_i[:, :], a["c_pos"])

        posf = sm(2)
        ang = sm(2, 16)
        kk = sm(2, 16)
        sn = sm(2, 16)
        cs = sm(2, 16)
        MAGIC = 12582912.0
        C1, C2, C3 = 6.28125, 0.0019350051879882812, 3.0199157663448e-7
        t = vec(lambda e: e.tensor_copy(posf, pos_i[:, :]), t_pos)
        for c in range(2):
            t = vec(lambda e, c=c: e.tensor_scalar(ang[:, c, :], vecs[:, 832:848], posf[:, c:c + 1],
                                                          None, ALU.mult), t, t_v[5])
        t = vec(lambda e: e.tensor_scalar(kk, ang, float(1 / (2 * np.pi)), None, ALU.mult), t)
        t = vec(lambda e: e.tensor_scalar(kk, kk, MAGIC, None, ALU.add), t)
        t = vec(lambda e: e.tensor_scalar(kk, kk, MAGIC, None, ALU.subtract), t)
        for cc in (C1, C2, C3):
            t = vec(lambda e, cc=cc: e.scalar_tensor_tensor(ang, kk, -cc, ang, ALU.mult, ALU.add), t)
        t = vec(lambda e: e.tensor_scalar(ang, ang, float(np.float32(3.1415925)), float(np.float32(-3.1415925)), ALU.min, ALU.max), t)
        t1 = scal(lambda e: e.activation(sn, ang, ACT.Sin), t)
        t2 = scal(lambda e: e.activation(cs, ang, ACT.Sin, scale=0.5), t)
        t = vec(lambda e: e.tensor_tensor(cs, cs, cs, ALU.mult), t1, t2)
        t_rope = vec(lambda e: e.tensor_scalar(cs, cs, -2.0, 1.0, ALU.mult, ALU.add), t)

        _, t_h = rmsnorm(g_attn, t_x, None)

        w_in = kview(a["w_in"][0])
        t_P = {}

        def sink_P(c0, n):
            def go(c, ps, t):
                t = evac(Pj[:, c, c0:c0 + n], ps, t)
                t_P[(c0, c)] = t
                return t
            return go

        def pt(lo, hi):
            return [t for (c0, c), t in t_P.items() if lo <= c0 < hi]

        for c0, n in ((0, 512), (512, 512), (1024, 32)):
            project(w_in, c0, n, sink_P(c0, n), t_h)
        for j in range(9):
            project(w_in, 1056 + 512 * j, 512, sink_P(1056 + 512 * j, 512), t_h)

        def gate_sink(c0):
            lo = c0 - 5664

            def go(c, ps, t):
                v = Pj[:, c, c0:c0 + 512]
                t = t_b = vec(lambda e: e.tensor_tensor(v, ps, bg[:, lo:lo + 512], ALU.add), t, t_bg)
                t = scal(lambda e: e.activation(v, v, ACT.Exp, scale=-1.0), t)
                t = vec(lambda e: e.tensor_scalar(v, v, 1.0, None, ALU.add), t)
                t_P[(c0, c)] = vec(lambda e: e.reciprocal(v, v), t)
                return t_b
            return go

        for j in range(4):
            project(w_in, 5664 + 512 * j, 512, gate_sink(5664 + 512 * j), t_h)

        t_proj = q_pe()
        K = xn[:, :, :].rearrange("p c n -> p (c n)")[:, 0:1536].rearrange("p (c h n) -> p c h n", c=2, h=8)
        ckT = hT[:, 0:2, :]
        ssc = sm(2)
        jk = E[:, 0, 0:256]
        for c in range(2):
            v = Pj[:, c, 768:1024]
            t = scal(lambda e, v=v, c=c: e.activation(xn[:, c, 0:256], v, ACT.Square, accum_out=ssc[:, c:c + 1]),
                    pt(512, 1024), t_proj)
        t = rsqrt(ssc, ssc, 256, t)
        for c in range(2):
            v = Pj[:, c, 768:1024]
            t = vec(lambda e, v=v, c=c: e.scalar_tensor_tensor(
                v, v, ssc[:, c:c + 1], nckv, ALU.mult, ALU.mult), t, t_v[0])
        t_ck = []
        for c in range(2):
            t_ck += transposes([(ckT[:, :, c * P:(c + 1) * P],
                                 [Pj[:, c, 768 + i * P:768 + (i + 1) * P] for i in range(2)])], t, t_proj)
        kv = bg.rearrange("p (c n) -> p c n", c=2)
        t_kv = []

        def kv_sink(c0):
            def go(c, ps, t):
                t = evac(kv[:, c, c0:c0 + 512], ps, t, pt(5664, 9999))
                t_kv.append(t)
                return t
            return go

        wu = a["w_ukv"][0].rearrange("(k p) n -> p k n", p=P)
        for c0 in (0, 512):
            project(wu, c0, 512, kv_sink(c0), t_ck, lhs=ckT, kn=2)
        kv4 = bg.rearrange("p (c h n) -> p c h n", c=2, h=8)

        def headnorm(v, g, n, *after):
            h = v.shape[1]
            sq = E[:, 0:2, :].rearrange("p i n -> p (i n)")[:, 0:h * n].rearrange("p (h n) -> p h n", h=h)
            ss = ssq[:, 0:h]
            t = vec(lambda e: e.tensor_tensor(sq, v, v, ALU.mult), *after)
            t = vec(lambda e: e.tensor_reduce(ss, sq, X, ALU.add), t)
            t = rsqrt(ss, ss, n, t)
            t = vec(lambda e: e.tensor_tensor(v, v, ss.unsqueeze(2).to_broadcast([P, h, n]), ALU.mult), t)
            return vec(lambda e: e.tensor_tensor(v, v, g, ALU.mult), t)

        ssq = sm(24)

        def rope(v, c_, s_, half, tmp, *after):
            h = v.shape[1]
            a1, a2 = v[:, :, 0:half], v[:, :, half:2 * half]
            cb = c_.unsqueeze(1).to_broadcast([P, h, half])
            sb_ = s_.unsqueeze(1).to_broadcast([P, h, half])
            u = [tmp[:, i * h * half:(i + 1) * h * half].rearrange("p (h n) -> p h n", h=h) for i in range(4)]
            vec(lambda e: e.tensor_tensor(u[0], a1, cb, ALU.mult), *after)
            vec(lambda e: e.tensor_tensor(u[1], a2, sb_, ALU.mult))
            vec(lambda e: e.tensor_tensor(u[2], a2, cb, ALU.mult))
            t = vec(lambda e: e.tensor_tensor(u[3], a1, sb_, ALU.mult))
            vec(lambda e: e.tensor_tensor(a1, u[0], u[1], ALU.subtract), t)
            return vec(lambda e: e.tensor_tensor(a2, u[2], u[3], ALU.add))

        tmp = E[:, :, :].rearrange("p i n -> p (i n)")
        t_q, t_k = [], []
        for c in range(2):
            qv = Pj[:, c, 0:768].rearrange("p (h n) -> p h n", h=8)
            t = headnorm(qv, vecs[:, 256:352].unsqueeze(1).to_broadcast([P, 8, 96]), 96, pt(0, 1024), t_v[1])
            t_q.append(rope(qv[:, :, 64:96], cs[:, c, :], sn[:, c, :], 16, tmp, t, t_rope))
            t = vec(lambda e, c=c: e.tensor_copy(K[:, c, :, 0:64], kv4[:, c, :, 0:64]), t_kv)
            t = vec(lambda e, c=c: e.tensor_copy(
                K[:, c, :, 64:96], Pj[:, c, 1024:1056].unsqueeze(1).to_broadcast([P, 8, 32])), pt(1024, 1056))
            t = headnorm(K[:, c, :, :], vecs[:, 352:448].unsqueeze(1).to_broadcast([P, 8, 96]), 96, t, t_v[2])
            t_k.append(rope(K[:, c, :, 64:96], cs[:, c, :], sn[:, c, :], 16, tmp, t, t_rope))
        qT = qd[0:96, 0:8, :]
        kT = kd[0:96, 0:8, :]
        t_T = []
        for c in range(2):
            for hh in (0, 4):
                t_T += transposes([(qT[:, hh:hh + 4, c * P:(c + 1) * P],
                                    [Pj[:, c, 96 * h:96 * h + 96] for h in range(hh, hh + 4)])], t_q[c])
                t_T += transposes([(kT[:, hh:hh + 4, c * P:(c + 1) * P],
                                    [K[:, c, h, :] for h in range(hh, hh + 4)])], t_k[c])

        e_free = [[None], [None]]
        pt_free = [[None], [None]]
        ei = [0]
        mx = sm(2, 4)
        den = sm(16)

        def attend(c, parts, scale, vs, ob, oc, dh, dcol, *after):
            i = ei[0] % 2
            ei[0] += 1
            wide = sum(p[2] for p in parts)
            ev = E[:, i, 0:wide]
            col = 0
            used = []
            toks = []
            b, at = None, 512
            groups = []
            for p in parts:
                if at + p[2] > 512:
                    b, at = bank(), 0
                    groups.append((b, []))
                groups[-1][1].append((at, p, col))
                at += p[2]
                col += p[2]
            for b, ps in groups:
                def go(e, b=b, ps=ps):
                    for at, p, _ in ps:
                        r = e.matmul(banks[:, b, at:at + p[2]], p[0], p[1], start=True, stop=True)
                    return r
                t = put("pe", go, list(after), bank_free[b])
                for at, p, col in ps:
                    t2 = vec(lambda e, b=b, at=at, p=p, col=col: e.scalar_tensor_tensor(
                        E[:, i, col:col + p[2]], p[3], p[4], banks[:, b, at:at + p[2]], ALU.mult, ALU.add),
                        t, e_free[i], t_B, t_cm)
                bank_free[b] = t2
            t = vec(lambda e: e.tensor_reduce(mx[:, i, 0:1], ev, X, ALU.max), t2)
            t = vec(lambda e: e.tensor_scalar(mx[:, i, 1:2], mx[:, i, 0:1], -scale, None, ALU.mult), t)
            t = scal(lambda e: e.activation(ev, ev, ACT.Exp, bias=mx[:, i, 1:2], scale=scale,
                                                  accum_out=den[:, dcol:dcol + 1]), t, den_free[0])
            n = wide // P
            tp = []
            for j in range(0, n, 4):
                m = min(4, n - j)
                tp += transposes([(PT[:, i, j * P:(j + m) * P].rearrange("p (k c) -> p k c", k=m),
                                   [E[:, i, (j + r) * P:(j + r + 1) * P] for r in range(m)])], t, pt_free[i])
            e_free[i] = [tp[-1], q_pe()]

            def pv(e):
                for j in range(n):
                    r = e.matmul(banks[:, ob, oc:oc + dh], PT[:, i, j * P:(j + 1) * P], vs[j],
                                 start=(j == 0), stop=(j == n - 1))
                return r
            t = put("pe", pv, tp, bank_free[ob] if oc == 0 else None)
            pt_free[i] = t
            return t

        den_free = [None]
        rden = sm(8)

        def normalise(ob, dst, h, dh, t):
            t = vec(lambda e: e.reciprocal(rden[:, 0:h], den[:, 0:h]), t, act_now())
            den_free[0] = t
            t = vec(lambda e: e.tensor_tensor(
                dst.rearrange("p (h n) -> p h n", h=h),
                banks[:, ob, 0:h * dh].rearrange("p (h n) -> p h n", h=h),
                rden[:, 0:h].unsqueeze(2).to_broadcast([P, h, dh]), ALU.mult), t)
            bank_free[ob] = t
            return t

        def act_now():
            return (q.sems["act"], q.count["act"])

        def causal_part(c, lhsT, rhs_of):
            return (lhsT, rhs_of(0, (c + 1) * P), (c + 1) * P, cm[:, 0:P] if c == 0 else cm[:, P:384], 1.0)

        t_o = []
        for c in range(2):
            ob = bank()
            for h in range(8):
                parts = [causal_part(c, qT[:, h, c * P:(c + 1) * P], lambda lo, hi, h=h: kT[:, h, lo:hi])]
                while bank_next[0] % 8 == ob or (bank_next[0] + 1) % 8 == ob:
                    bank_next[0] += 1
                t = attend(c, parts, 96 ** -0.5, [kv4[:, kc, h, 64:128] for kc in range(c + 1)],
                           ob, 64 * h, 64, h, t_T)
            t_o.append(normalise(ob, O[:, c, :], 8, 64, t))
        t_OT = []
        for c in range(2):
            t_OT += transposes([(OT[:, :, c * P:(c + 1) * P], [O[:, c, k * P:(k + 1) * P] for k in range(4)])], t_o[c])

        t_m = []

        def m0_sink(c0):
            def go(c, ps, t):
                g = Pj[:, c, 5664 + c0:5664 + c0 + 512]
                t = vec(lambda e: e.tensor_tensor(g, g, ps, ALU.mult), t, pt(5664, 9999))
                t_m.append(t)
                return t
            return go

        for c0 in (0, 512):
            project(kview(a["w_o_mla"][0]), c0, 512, m0_sink(c0), t_OT, lhs=OT, kn=4)

        t_d = {}
        for c in range(2):
            for w, go_ in ((0, 448), (1, 640)):
                lo = 1056 + 1536 * w
                ts = []
                for g in range(3):
                    v = Pj[:, c, lo + 512 * g:lo + 512 * g + 512].rearrange("p (h n) -> p h n", h=8)
                    gv = vecs[:, go_ + 64 * g:go_ + 64 * g + 64].unsqueeze(1).to_broadcast([P, 8, 64])
                    ts.append(headnorm(v, gv, 64, pt(1056, 5664), t_v[3], t_v[4], q_pe(), act_now()))
                t_d[(w, c)] = ts
        t_T = []
        t_qfree = q_pe()
        for c in range(2):
            for w, dst in ((0, qd), (1, kd)):
                lo = 1056 + 1536 * w
                for g in range(3):
                    t_T += transposes([(dst[:, 4 * g:4 * g + 4, c * P:(c + 1) * P],
                                        [Pj[:, c, lo + 512 * g + P * i:lo + 512 * g + P * (i + 1)] for i in range(4)])],
                                      t_d[(w, c)], t_qfree)
        t_o = []
        for c in range(2):
            ob = bank()
            for h in range(8):
                p0 = 64 * (h % 2)
                slope = 2.0 ** (-8.0 * (h + 1.0) / 8)
                kw = (c + 1) * P
                bo = 0 if c == 0 else 384
                parts = [(qd[p0:p0 + 64, 4 * g + h // 2, c * P:(c + 1) * P],
                          kd[p0:p0 + 64, 4 * g + h // 2, 0:kw], kw,
                          Bm[:, bo + g * kw:bo + (g + 1) * kw], -8.0 * slope) for g in range(3)]
                while any((bank_next[0] + i) % 8 == ob for i in range(4)):
                    bank_next[0] += 1
                vs = [Pj[:, kc, 4128 + 512 * g + 64 * h:4128 + 512 * g + 64 * h + 64]
                      for g in range(3) for kc in range(c + 1)]
                t = attend(c, parts, 0.125, vs, ob, 64 * h, 64, h, t_T)
            t_o.append(normalise(ob, O[:, c, :], 8, 64, [t, t_OT, q_pe()]))
        t_OT = []
        t_f = q_pe()
        for c in range(2):
            t_OT += transposes([(OT[:, :, c * P:(c + 1) * P], [O[:, c, k * P:(k + 1) * P] for k in range(4)])],
                               t_o[c], t_f)
        t_m2 = []

        def m1_sink(c0):
            def go(c, ps, t):
                g = Pj[:, c, 6688 + c0:6688 + c0 + 512]
                m = Pj[:, c, 5664 + c0:5664 + c0 + 512]
                t = t_b = vec(lambda e: e.tensor_tensor(g, g, ps, ALU.mult), t, pt(5664, 9999))
                t_m2.append(vec(lambda e: e.tensor_tensor(m, m, g, ALU.add), t, t_m))
                return t_b
            return go

        for c0 in (0, 512):
            project(kview(a["w_o_dil"][0]), c0, 512, m1_sink(c0), t_OT, lhs=OT, kn=4)
        t_hT = []
        t_f = q_pe()
        for c in range(2):
            t_hT += transposes([(hT[:, k:k + 4, c * P:(c + 1) * P],
                                 [Pj[:, c, 5664 + (k + i) * P:5664 + (k + i + 1) * P] for i in range(4)])
                                for k in (0, 4)], t_m2, t_f)

        def residual_sink(toks, c0):
            def go(c, ps, t):
                v = x[:, c, c0:c0 + 512]
                t = vec(lambda e: e.tensor_tensor(v, v, ps, ALU.add), t)
                toks.append(t)
                return t
            return go

        t_r = []
        for c0 in (0, 512):
            project(kview(a["w_out"][0]), c0, 512, residual_sink(t_r, c0), t_hT)

        _, t_h = rmsnorm(g_ffn, t_r, q_pe())
        t_fence = q.all_done()
        comb = sm(2, 32)
        lg = sm(2, 36)
        iota8 = sm(8)
        t_io = put("pool", lambda e: e.iota(iota8, [[1, 8]], base=0, channel_multiplier=0,
                                            allow_small_or_imprecise_dtypes=True))
        br = bank()

        def router(e):
            for c in range(2):
                for k in range(8):
                    r = e.matmul(banks[:, br, 64 * c:64 * c + 36], hT[:, k, c * P:(c + 1) * P], rw[:, k, :],
                                 start=(k == 0), stop=(k == 7))
            return r
        t = put("pe", router, t_h, t_v, bank_free[br])
        for c in range(2):
            t = vec(lambda e, c=c: e.tensor_tensor(lg[:, c, :], banks[:, br, 64 * c:64 * c + 36], rb, ALU.add),
                    t, t_v)
        bank_free[br] = t
        idx = sb("idx", [P, 16], U32)
        w8, g8, v8, w1, gone, one1, one2 = sm(8), sm(8), sm(8), sm(8), sm(4), sm(8), sm(8)
        t_c = []
        for c in range(2):
            l = lg[:, c, :]
            t = vec(lambda e: e.memset(g8, NEG), t)
            t = vec(lambda e, l=l: e.tensor_copy(g8[:, 0:4], l[:, 0:4]), t)
            t = vec(lambda e: e.max(v8, g8), t)
            t = vec(lambda e: e.max_index(idx[:, 0:8], v8, g8), t)
            t = vec(lambda e: e.tensor_scalar(w1[:, 0:1], v8[:, 0:1], -1.0, None, ALU.mult), t)
            ta = scal(lambda e: e.activation(w8[:, 0:4], g8[:, 0:4], ACT.Exp, bias=w1[:, 0:1],
                                                   accum_out=w1[:, 1:2]), t)
            t = vec(lambda e: e.tensor_copy(w1[:, 2:3], idx[:, 0:1]), t)
            t = vec(lambda e: e.tensor_scalar(gone, iota8[:, 0:4], w1[:, 2:3], None, ALU.is_equal), t, t_io)
            sel = comb[:, c, :].rearrange("p (g e) -> p g e", g=4)
            t = vec(lambda e, l=l, sel=sel: e.tensor_tensor(
                sel, l[:, 4:36].rearrange("p (g e) -> p g e", g=4),
                gone.unsqueeze(2).to_broadcast([P, 4, 8]), ALU.mult), t)
            t = vec(lambda e, sel=sel: e.tensor_reduce(
                g8, sel.rearrange("p g e -> p e g"), X, ALU.add), t, ta)
            t = vec(lambda e: e.max(v8, g8), t)
            t = vec(lambda e: e.max_index(idx[:, 0:8], v8, g8), t)
            t = vec(lambda e: e.tensor_copy(w1[:, 2:4], idx[:, 0:2]), t)
            t = vec(lambda e: e.tensor_scalar(w1[:, 0:1], v8[:, 0:1], -1.0, None, ALU.mult), t)
            ta = scal(lambda e: e.activation(w8[:, 0:2], v8[:, 0:2], ACT.Exp, bias=w1[:, 0:1],
                                                   accum_out=w1[:, 4:5]), t)
            t = vec(lambda e: e.tensor_scalar(w1[:, 4:5], w1[:, 4:5], w1[:, 1:2], None, ALU.mult), ta)
            t = vec(lambda e: e.reciprocal(w1[:, 4:5], w1[:, 4:5]), t)
            t = vec(lambda e: e.tensor_scalar(w8[:, 0:2], w8[:, 0:2], w1[:, 4:5], None, ALU.mult), t)
            t = vec(lambda e: e.tensor_scalar(one1, iota8, w1[:, 2:3], w8[:, 0:1], ALU.is_equal, ALU.mult), t)
            t = vec(lambda e: e.tensor_scalar(one2, iota8, w1[:, 3:4], w8[:, 1:2], ALU.is_equal, ALU.mult), t)
            t = vec(lambda e: e.tensor_tensor(one1, one1, one2, ALU.add), t)
            t = vec(lambda e, sel=sel: e.tensor_tensor(
                sel, gone.unsqueeze(2).to_broadcast([P, 4, 8]),
                one1.unsqueeze(1).to_broadcast([P, 4, 8]), ALU.mult), t)
            t_c.append(t)

        he = arena[:, 0:2 * 512].rearrange("p (i n) -> p i n", i=2)
        he_free = [t_fence, t_fence]

        def up(e_):
            gs, us = [], []
            for w, lst in ((a["w_gate"], gs), (a["w_up"], us)):
                s, wt, t_w = load(kview(w[0][e_]), 8)
                b = bank()

                def go(e, wt=wt, b=b):
                    for f in range(2):
                        for k in range(8):
                            r = e.matmul(banks[:, b, f * T:(f + 1) * T], wt[:, k, f * P:(f + 1) * P], hT[:, k, :],
                                         start=(k == 0), stop=(k == 7))
                    return r
                t = put("pe", go, t_w, t_h, bank_free[b])
                slot_free[s] = t
                lst += [b, t]
            i = e_ % 2
            t = put("act", lambda e: e.activation(he[:, i, :], banks[:, gs[0], :], ACT.Silu), gs[1], he_free[i])
            bank_free[gs[0]] = t
            t = put("dve", lambda e: e.tensor_tensor(he[:, i, :], he[:, i, :], banks[:, us[0], :], ALU.mult),
                    t, us[1])
            bank_free[us[0]] = t
            return t

        t_acc = [t_r]

        def down(e_, t_he):
            i = e_ % 2
            s, wt, t_w = load(a["w_down"][0][e_].rearrange("(k p) n -> p k n", p=P), 2)
            for c in range(2):
                for hf in range(2):
                    b = bank()

                    def go(e, c=c, hf=hf, b=b):
                        for f in range(2):
                            r = e.matmul(banks[:, b, :], he[:, i, f * T + c * P:f * T + (c + 1) * P],
                                         wt[:, f, hf * 512:(hf + 1) * 512], start=(f == 0), stop=(f == 1))
                        return r
                    t = put("pe", go, t_w, t_he, bank_free[b])
                    v = x[:, c, hf * 512:(hf + 1) * 512]
                    bank_free[b] = put("dve", lambda e, c=c, b=b, v=v: e.scalar_tensor_tensor(
                        v, banks[:, b, :], comb[:, c, e_:e_ + 1], v, ALU.mult, ALU.add), t, t_c, t_acc)
            slot_free[s] = t
            he_free[i] = t
            t_acc[0] = bank_free[b]

        pend = up(0)
        for e_ in range(32):
            nxt = up(e_ + 1) if e_ < 31 else None
            down(e_, pend)
            pend = nxt
        t_r = t_acc[0]

        g_mix0 = load_gain(a["norm_mix_2"][0])
        P2 = arena[:, 0:7168].rearrange("p (c n) -> p c n", c=2)
        q2 = arena[:, 7168:7168 + 4096].rearrange("p (j t) -> p j t", t=T)
        dec = arena[:, 11264:11264 + 1536].rearrange("p (h n) -> p h n", h=4)
        tab = arena[:, 12800:13056].rearrange("p (s c n) -> p s c n", s=2, c=2)
        RT = arena[:, 13056:13056 + 768].rearrange("p (i n) -> p i n", i=2)
        tmp2 = arena[:, 14000:14000 + 2048]
        cat = arena[:, 16384:16384 + 2048].rearrange("p (c n) -> p c n", c=2)
        t_fence = q.all_done()
        t_dec = fetch(dec, a["c_decay"], t_fence)
        t_tab = fetch(tab, a["c_rope2"], t_fence)
        _, t_h = rmsnorm(g_mix0, t_r, q_pe())
        t_P.clear()
        w_e = kview(a["even_w_in_2"][0])

        def sink_P2(c0):
            def go(c, ps, t):
                v = P2[:, c, c0:c0 + 512]
                if c0 == 3072:
                    t = scal(lambda e: e.activation(v, ps, ACT.Silu), t, t_fence)
                else:
                    t = evac(v, ps, t, t_fence)
                t_P[(c0, c)] = t
                return t
            return go
        for j in range(7):
            project(w_e, 512 * j, 512, sink_P2(512 * j), t_h)
        t_kinds = {}
        for c in range(2):
            for lo, c0s in ((0, (0, 512)), (1536, (1536, 2048))):
                v = P2[:, c, lo:lo + 1024].rearrange("p (h n) -> p h n", h=8)
                t_kinds[(lo, c)] = rope(v, tab[:, 0, c, :], tab[:, 1, c, :], 64, tmp2,
                                        [t_P[(x_, c)] for x_ in c0s], t_tab)
        t_T = {}
        for kind, lo in enumerate((0, 512, 1536, 2048)):
            t_T[kind] = []
            for c in range(2):
                t_T[kind] += transposes([(q2[:, 4 * kind:4 * kind + 4, c * P:(c + 1) * P],
                                          [P2[:, c, lo + i * P:lo + (i + 1) * P] for i in range(4)])],
                                        t_kinds[(0 if lo < 1024 else 1536, c)])
        t_cat = []
        for c in range(2):
            ob = bank()
            for h in range(4):
                parts = [causal_part(c, q2[:, h, c * P:(c + 1) * P], lambda lo, hi, h=h: q2[:, 4 + h, lo:hi])]
                while bank_next[0] % 8 == ob or (bank_next[0] + 1) % 8 == ob:
                    bank_next[0] += 1
                t = attend(c, parts, 128 ** -0.5, [P2[:, kc, 1024 + P * h:1024 + P * (h + 1)] for kc in range(c + 1)],
                           ob, P * h, P, h, t_T[0], t_T[1], t_P[(1024, 0)], t_P[(1024, 1)])
            t_cat.append(normalise(ob, cat[:, c, 0:512], 4, 128, t))
        rt_free = [None, None]
        ob0, ob1 = bank(), bank()
        for h in range(4):
            i = h % 2
            while bank_next[0] % 8 in (ob0, ob1):
                bank_next[0] += 1
            b = bank()

            def go(e, h=h, b=b):
                e.matmul(banks[:, b, 0:256], q2[:, 12 + h, 0:P], q2[:, 8 + h, :], start=True, stop=True)
                return e.matmul(banks[:, b, 256:384], q2[:, 12 + h, P:T], q2[:, 8 + h, P:T], start=True, stop=True)
            t = put("pe", go, t_T[2], t_T[3], bank_free[b])
            t = vec(lambda e, h=h, b=b, i=i: e.tensor_tensor(RT[:, i, :], banks[:, b, 0:384], dec[:, h, :],
                                                                    ALU.mult), t, t_dec, rt_free[i])
            bank_free[b] = t

            def go(e, h=h, i=i):
                v0 = P2[:, 0, 2560 + P * h:2560 + P * (h + 1)]
                v1 = P2[:, 1, 2560 + P * h:2560 + P * (h + 1)]
                cs_ = slice(P * h, P * (h + 1))
                e.matmul(banks[:, ob0, cs_], RT[:, i, 0:P], v0, start=True, stop=True)
                e.matmul(banks[:, ob1, cs_], RT[:, i, P:T], v0, start=True, stop=False)
                return e.matmul(banks[:, ob1, cs_], RT[:, i, T:384], v1, start=False, stop=True)
            t = put("pe", go, t, t_P[(2560, 0)], t_P[(2560, 1)],
                    [bank_free[ob0], bank_free[ob1]] if h == 0 else None)
            rt_free[i] = t
        for c, ob in ((0, ob0), (1, ob1)):
            cv = cat[:, c, 512:1024]
            cv3 = cv.rearrange("p (h n) -> p h n", h=4)
            sq = tmp2[:, 0:512].rearrange("p (h n) -> p h n", h=4)
            ss = ssq[:, 0:4]
            t = vec(lambda e, cv=cv, ob=ob: e.tensor_copy(cv, banks[:, ob, :]), t)
            bank_free[ob] = t
            t = vec(lambda e, cv3=cv3: e.tensor_tensor(sq, cv3, cv3, ALU.mult), t)
            t = vec(lambda e: e.tensor_reduce(ss, sq, X, ALU.add), t)
            t = rsqrt(ss, ss, 128, t)
            t = vec(lambda e, cv3=cv3: e.tensor_tensor(
                cv3, cv3, ss.unsqueeze(2).to_broadcast([P, 4, P]), ALU.mult), t)
            t = vec(lambda e, cv=cv, c=c: e.tensor_tensor(cv, cv, P2[:, c, 3072:3584], ALU.mult),
                    t, t_P[(3072, c)])
            t_cat.append(t)
        t_f = q_pe()
        t_hT = []
        for c in range(2):
            t_hT += transposes([(hT[:, k:k + 4, c * P:(c + 1) * P],
                                 [cat[:, c, (k + i) * P:(k + i + 1) * P] for i in range(4)])
                                for k in (0, 4)], t_cat, t_f)
        t_r2 = []
        for c0 in (0, 512):
            project(kview(a["even_w_out_2"][0]), c0, 512, residual_sink(t_r2, c0), t_hT)
        t_r = t_r2

        iota16 = sm(16)
        t_i16 = put("pool", lambda e: e.iota(iota16, [[1, 16]], base=0, channel_multiplier=0,
                                             allow_small_or_imprecise_dtypes=True))
        g_sems = [sem(f"s_g{i}") for i in range(NG)]
        rows_free = [None] * NG
        rows_n = [0]
        base = 12288 + NG * D
        assert base + 1280 <= AR
        iu = arena[:, base:base + 256].bitcast(U32)
        pu = arena[:, base + 256:base + 512].bitcast(U32)
        eix = arena[:, base + 512:base + 768].bitcast(U32).rearrange("p (c n) -> p c n", c=2)
        diag = arena[:, base + 768:base + 1280].rearrange("p (i n) -> p i n", i=4)
        vals = sm(16, 16)
        ti = sm(16, 16)
        tops = sm(2, 128)
        hid = sm(2, 128)
        af = sm(128)
        e12 = sm(2, 128)
        gz = sm(16)

        def peer(layer, g, t_r):
            t_fence = q.all_done()
            qp = arena[:, 0:4096].rearrange("p (j t) -> p j t", t=T)
            sc = arena[:, 4096:8192].rearrange("p (c j n) -> p c j n", c=2, j=16)
            cand = arena[:, 8192:10240].rearrange("p (h n) -> p h n", h=8)
            eq = arena[:, 10240:12288].rearrange("p (h k j) -> p h k j", h=8, k=16)
            rows = arena[:, 12288:12288 + NG * D].rearrange("p (i d) -> p i d", i=NG)
            for i in range(NG):
                rows_free[i] = t_fence
            toks_xn, t_h = rmsnorm(g, t_r, q_pe())
            t_q = []
            w = kview(a["peer_w_q_2"][layer])
            for jj in range(8):
                s, wt, t_w = load(w[:, :, 256 * jj:256 * (jj + 1)], 8)
                b = bank()

                def go(e, wt=wt, b=b):
                    for f in range(2):
                        for k in range(8):
                            r = e.matmul(banks[:, b, f * T:(f + 1) * T], wt[:, k, f * P:(f + 1) * P], hT[:, k, :],
                                         start=(k == 0), stop=(k == 7))
                    return r
                t = put("pe", go, t_w, t_h, bank_free[b])
                slot_free[s] = t
                t = evac(qp[:, 2 * jj:2 * jj + 2, :].rearrange("p j t -> p (j t)"), banks[:, b, :], t, t_fence)
                bank_free[b] = t
                t_q.append(t)
            s, kt, t_w = load(a["c_keys"][layer], 16)
            t_s = {}
            for c in range(2):
                for j4 in range(4):
                    b = bank()

                    def go(e, c=c, j4=j4, b=b):
                        for i in range(4):
                            j = 4 * j4 + i
                            r = e.matmul(banks[:, b, i * P:(i + 1) * P], qp[:, j, c * P:(c + 1) * P], kt[:, j, :],
                                         start=True, stop=True)
                        return r
                    t = put("pe", go, t_w, t_q, bank_free[b])
                    t_s[(c, j4)] = bank_free[b] = evac(
                        sc[:, c, 4 * j4:4 * j4 + 4, :].rearrange("p j n -> p (j n)"), banks[:, b, :], t, t_fence)
            slot_free[s] = (q.sems["pe"], q.count["pe"])

            def top16(v, vout, iout, *after):
                t = vec(lambda e: e.max(vout[:, 0:8], v), *after)
                t = vec(lambda e: e.max_index(iout[:, 0:8], vout[:, 0:8], v), t)
                t = vec(lambda e: e.match_replace(v, vout[:, 0:8], v, -3e38), t)
                t = vec(lambda e: e.max(vout[:, 8:16], v), t)
                return vec(lambda e: e.max_index(iout[:, 8:16], vout[:, 8:16], v), t)

            def select(c):
                for j in range(16):
                    t = top16(sc[:, c, j, :], vals[:, j, :], iu[:, 16 * j:16 * j + 16], t_s[(c, j // 4)])
                t = vec(lambda e: e.tensor_copy(ti.rearrange("p a b -> p (a b)"), iu), t)
                v4 = vals.rearrange("p (h s) n -> p s h n", s=2)
                i4 = ti.rearrange("p (h s) n -> p s h n", s=2)
                for h in range(8):
                    t = vec(lambda e, h=h: e.tensor_tensor(
                        cand[:, h, :].rearrange("p (i j) -> p i j", i=16),
                        vals[:, 2 * h, :].unsqueeze(2).to_broadcast([P, 16, 16]),
                        vals[:, 2 * h + 1, :].unsqueeze(1).to_broadcast([P, 16, 16]), ALU.add), t)
                ts = tops[:, c, :]
                for h in range(8):
                    t = top16(cand[:, h, :], ts[:, 16 * h:16 * h + 16], pu[:, 16 * h:16 * h + 16], t)
                t = vec(lambda e: e.tensor_scalar(pu[:, 128:256], pu[:, 0:128], 4, None,
                                                         ALU.logical_shift_right), t)
                t = vec(lambda e: e.tensor_scalar(pu[:, 0:128], pu[:, 0:128], 15, None,
                                                         ALU.bitwise_and), t)
                for s_, lo in ((0, 128), (1, 0)):
                    t = vec(lambda e, lo=lo: e.tensor_copy(af, pu[:, lo:lo + 128]), t)
                    for h in range(8):
                        vec(lambda e, h=h: e.tensor_tensor(
                            eq[:, h], iota16.unsqueeze(1).to_broadcast([P, 16, 16]),
                            af[:, 16 * h:16 * h + 16].unsqueeze(2).to_broadcast([P, 16, 16]), ALU.is_equal),
                            t if h == 0 else None, t_i16)
                    t = dve_now()
                    for h in range(8):
                        vec(lambda e, h=h, s_=s_: e.tensor_tensor(
                            eq[:, h], eq[:, h], ti[:, 2 * h + s_, :].unsqueeze(1).to_broadcast([P, 16, 16]),
                            ALU.mult), t)
                    t = dve_now()
                    t = vec(lambda e, s_=s_: e.tensor_reduce(
                        e12[:, s_, :], eq.rearrange("p h k j -> p (h k) j"), X, ALU.add), t)
                t = vec(lambda e: e.scalar_tensor_tensor(e12[:, 0, :], e12[:, 0, :], 128.0, e12[:, 1, :],
                                                                ALU.mult, ALU.add), t)
                t_e = vec(lambda e: e.tensor_scalar(eix[:, c, :], e12[:, 0, :], float(128 * 128 * layer), None,
                                                    ALU.add), t)
                ts3 = ts.rearrange("p (h k) -> p h k", h=8)
                t = vec(lambda e: e.tensor_tensor(
                    e12[:, 1, :].rearrange("p (h k) -> p h k", h=8), ts3,
                    ts3[:, :, 0:1].to_broadcast([P, 8, 16]), ALU.subtract), t_e)
                t = scal(lambda e: e.activation(ts, e12[:, 1, :], ACT.Exp), t)
                t = vec(lambda e: e.tensor_reduce(gz[:, 0:8], ts3, X, ALU.add), t)
                t = vec(lambda e: e.reciprocal(gz[:, 8:16], gz[:, 0:8]), t)
                t = vec(lambda e: e.tensor_tensor(
                    ts3, ts3, gz[:, 8:16].unsqueeze(2).to_broadcast([P, 8, 16]), ALU.mult), t)
                return t_e, t

            def dve_now():
                return (q.sems["dve"], q.count["dve"])

            def gather(table, c, j, t_e):
                i = rows_n[0] % NG
                rows_n[0] += 1
                t = dma("pool", lambda e: e.indirect_dma_start(
                    rows[:, i, :], None, table.rearrange("l e d -> (l e) d"),
                    bass.IndirectOffsetOnAxis(ap=eix[:, c, j:j + 1], axis=0)), g_sems[i], rows_free[i], t_e)
                return i, t

            def u_step(c, j, t_e):
                i, t = gather(a["peer_u_2"], c, j, t_e)
                rows_free[i] = put("dve", lambda e: e.tensor_tensor_reduce(
                    rows[:, i, :], rows[:, i, :], xn[:, c, :], 1.0, 0.0, ALU.mult, ALU.add,
                    hid[:, c, j:j + 1]), t, toks_xn)

            dfree = [None] * 4
            dn = [0]

            def v_step(c, j, t_e, t_w, acc):
                i, t = gather(a["peer_v_2"], c, j, t_e)
                if j % 3 == 2 and c == 1:
                    rows_free[i] = acc_tok[0] = put("dve", lambda e: e.scalar_tensor_tensor(
                        x[:, c, :], rows[:, i, :], hid[:, c, j:j + 1], x[:, c, :], ALU.mult, ALU.add),
                        t, t_w, t_r, acc_tok[0])
                    return
                d = dn[0] % 4
                dn[0] += 1
                td = put("act", lambda e: e.activation(diag[:, d, :], ident[:, :], ACT.Copy,
                                                       scale=hid[:, c, j:j + 1]), t_w, t_id, dfree[d])

                def go(e):
                    for hf in range(2):
                        r = e.matmul(banks[:, acc[hf], :], diag[:, d, :], rows[:, i, hf * 512:(hf + 1) * 512],
                                     start=(j == 0), stop=(j == 127))
                    return r
                dfree[d] = rows_free[i] = put("pe", go, t, td, [bank_free[acc[0]], bank_free[acc[1]]] if j == 0 else None)

            def weigh(c, t_g):
                t = scal(lambda e: e.activation(hid[:, c, :], hid[:, c, :], ACT.Gelu), dve_now())
                return vec(lambda e: e.tensor_tensor(hid[:, c, :], hid[:, c, :], tops[:, c, :], ALU.mult),
                           t, t_g)

            acc_tok = [None]
            t_e0, t_g0 = select(0)
            for j in range(64):
                u_step(0, j, t_e0)
            t_e1, t_g1 = select(1)
            for j in range(64, 128):
                u_step(0, j, t_e0)
            t_w0 = weigh(0, t_g0)
            acc0 = [bank(), bank()]
            acc1 = [bank(), bank()]
            for j in range(128):
                v_step(0, j, t_e0, t_w0, acc0)
                u_step(1, j, t_e1)
            t_w1 = weigh(1, t_g1)
            for j in range(128):
                v_step(1, j, t_e1, t_w1, acc1)
            ts = []
            for c, acc in ((0, acc0), (1, acc1)):
                for hf in range(2):
                    v = x[:, c, hf * 512:(hf + 1) * 512]
                    t = vec(lambda e, v=v, b=acc[hf]: e.tensor_tensor(v, v, banks[:, b, :], ALU.add),
                            q_pe(), acc_tok[0], t_r)
                    bank_free[acc[hf]] = t
                    ts.append(t)
            return ts

        g = load_gain(a["norm_ffn_2"][0])
        g_mix1 = load_gain(a["norm_mix_2"][1])
        t_r = peer(0, g, t_r)

        t_fence = q.all_done()
        _, t_h = rmsnorm(g_mix1, t_r, q_pe())
        cw = sm(24)
        t_cw = fetch(cw, a["c_conv"])
        bgT = arena[:, 0:2048].rearrange("p (k t) -> p k t", k=8)
        hxT = arena[:, 2048:4096].rearrange("p (k t) -> p k t", k=8)
        uT = arena[:, 4096:4096 + 8 * 258].rearrange("p (k t) -> p k t", k=8)
        yT = arena[:, 6400:6400 + 2048].rearrange("p (k t) -> p k t", k=8)
        cgT = arena[:, 8448:8448 + 2048].rearrange("p (k t) -> p k t", k=8)
        w = kview(a["odd_w_in_2"][0])
        t_z = put("pool", lambda e: e.memset(uT[:, :, 0:2], 0.0), t_fence)
        t_b = {}
        for jj in range(12):
            s, wt, t_w = load(w[:, :, 256 * jj:256 * (jj + 1)], 8)
            b = bank()

            def go(e, wt=wt, b=b):
                for f in range(2):
                    for k in range(8):
                        r = e.matmul(banks[:, b, f * T:(f + 1) * T], wt[:, k, f * P:(f + 1) * P], hT[:, k, :],
                                     start=(k == 0), stop=(k == 7))
                return r
            t = put("pe", go, t_w, t_h, bank_free[b])
            slot_free[s] = t
            kd_, k0 = jj // 4, 2 * (jj % 4)
            dst = (bgT, cgT, hxT)[kd_]
            t = evac(dst[:, k0:k0 + 2, :].rearrange("p j t -> p (j t)"), banks[:, b, :], t, t_fence)
            bank_free[b] = t
            t_b[jj] = t
        t_y = []
        for k in range(8):
            t = vec(lambda e, k=k: e.tensor_tensor(uT[:, k, 2:258], cgT[:, k, :], hxT[:, k, :], ALU.mult),
                    t_b[4 + k // 2], t_b[8 + k // 2], t_z)
            t = vec(lambda e, k=k: e.tensor_scalar(yT[:, k, :], uT[:, k, 0:256], cw[:, k:k + 1], None,
                                                          ALU.mult), t, t_cw)
            for i in (1, 2):
                t = vec(lambda e, k=k, i=i: e.scalar_tensor_tensor(
                    yT[:, k, :], uT[:, k, i:i + 256], cw[:, 8 * i + k:8 * i + k + 1], yT[:, k, :],
                    ALU.mult, ALU.add), t)
            t = vec(lambda e, k=k: e.tensor_tensor(yT[:, k, :], yT[:, k, :], bgT[:, k, :], ALU.mult), t,
                    t_b[k // 2])
            t_y.append(t)
        t_r2 = []
        for c0 in (0, 512):
            project(kview(a["odd_w_out_2"][0]), c0, 512, residual_sink(t_r2, c0), t_y, lhs=yT)
        t_r = t_r2
        g = load_gain(a["norm_ffn_2"][1])
        g_fin = load_gain(a["final_norm_2"])
        t_r = peer(1, g, t_r)
        toks, _ = rmsnorm(g_fin, t_r, q.all_done(), to_T=False)
        return wrap(nc, ctx, q, finish, xn, toks)


def wrap(nc, ctx, q, finish, src, t):
    finish(src[:, :, :], t)
    block = ctx.enter_context(nc.Block())

    @block.sync
    def _(e):
        q.emit("sp", e)

    @block.tensor
    def _(e):
        q.emit("pe", e)

    @block.vector
    def _(e):
        q.emit("dve", e)

    @block.scalar
    def _(e):
        q.emit("act", e)

    @block.gpsimd
    def _(e):
        q.emit("pool", e)


def constants():
    c = {}
    c["c_ident"] = np.eye(P, dtype=np.float32)
    qi = np.arange(T)[:, None]
    ki = np.arange(T)[None, :]
    d = qi - ki
    band = []
    for dil in (1, 4, 16):
        ok = (d >= 0) & (d % dil == 0) & (d <= 128 * dil)
        band.append(np.where(ok, d, 1e30).astype(np.float32))
    c["c_band"] = np.concatenate([b[0:P, 0:P] for b in band] + [b[P:T] for b in band], axis=1)
    cm = np.where(d >= 0, 0.0, NEG).astype(np.float32)
    c["c_causal"] = np.concatenate([cm[0:P, 0:P], cm[P:T]], axis=1)
    f = (np.float32(10000.0) ** (-np.arange(16, dtype=np.float32) / np.float32(16))).astype(np.float32)
    c["c_freq"] = np.repeat(f[None, :], P, axis=0)
    inv = (np.float32(10000.0) ** (-np.arange(64, dtype=np.float32) / np.float32(64))).astype(np.float32)
    ang = (np.arange(T, dtype=np.float32)[:, None] * inv[None, :]).astype(np.float64)
    tab = np.stack([np.cos(ang), np.sin(ang)]).astype(np.float32)
    c["c_rope2"] = np.ascontiguousarray(tab.reshape(2, 2, P, 64).transpose(2, 0, 1, 3))
    dec = []
    for h in range(4):
        lg = np.log(1.0 - 2.0 ** (-5.0 - h))
        m = np.where(d.T <= 0, np.exp(lg * np.abs(d.T)), 0.0) * 0 + np.where(
            (ki - qi) >= 0, np.exp(lg * np.maximum(ki - qi, 0)), 0.0)
        m = (m * 128 ** -0.5).astype(np.float32)
        dec.append(np.concatenate([m[0:P, :], m[P:T, P:T]], axis=1))
    c["c_decay"] = np.ascontiguousarray(np.stack(dec, axis=1))
    return c


_OUTS = [((1, 256, 1024), "float32")]


def kernel(**inputs):
    import concourse.bacc as _bacc
    from concourse.bass_utils import run_bass_kernel_spmd as _run

    nc = _bacc.Bacc("TRN2", target_bir_lowering=False, num_devices=1)
    data = {k: np.ascontiguousarray(v) for k, v in inputs.items() if k != "peer_sub_keys_2"}
    data.update(constants())
    keys = np.asarray(inputs["peer_sub_keys_2"])
    data["c_keys"] = np.ascontiguousarray(keys.transpose(0, 4, 1, 2, 3).reshape(2, P, 16, P))
    data["c_conv"] = np.ascontiguousarray(data.pop("odd_conv_2")[0].reshape(3, 8, P).transpose(2, 0, 1).reshape(P, 24))
    data["c_pos"] = np.ascontiguousarray(data.pop("positions").reshape(2, P).T)
    arrays, args = {}, {}
    for name, v in data.items():
        arrays[f"in_{name}_dram"] = v
        args[name] = nc.dram_tensor(f"in_{name}_dram", v.shape, mybir.dt.from_np(v.dtype),
                                    kind="ExternalInput").ap()
    outs = [nc.dram_tensor(f"out_{i}_dram", shape, mybir.dt.from_np(np.dtype(dt)), kind="ExternalOutput").ap()
            for i, (shape, dt) in enumerate(_OUTS)]
    build(nc, args, outs[0])
    r = _run(nc, [arrays], core_ids=[0])
    return r.results[0]["out_0_dram"]
```

```python
from contextlib import ExitStack

import numpy as np

import concourse.bass as bass
from concourse import mybir

P = 128
F32 = mybir.dt.float32
I32 = mybir.dt.int32
U32 = mybir.dt.uint32
ALU = mybir.AluOpType
ACT = mybir.ActivationFunctionType
X = mybir.AxisListType.X
EPS = 1e-6
NEG = -1e30
T = 256
D = 1024

NSLOT = 6
NG = 20
AR = 29056


class Queues:

    def __init__(self, sems):
        self.sems = sems
        self.count = {e: 0 for e in sems}
        self.items = {e: [] for e in sems}
        self.seen = {e: {} for e in sems}
        self.dma_count = {}

    def waits(self, eng, after):
        need = {}
        stack = list(after)
        while stack:
            a = stack.pop()
            if a is None:
                continue
            if isinstance(a, list):
                stack += a
                continue
            sem, value = a
            if value > self.seen[eng].get(sem.name, 0):
                need[sem.name] = (sem, max(value, need.get(sem.name, (None, 0))[1]))
        for name, (sem, value) in need.items():
            self.seen[eng][name] = value
        return list(need.values())

    def put(self, eng, fn, *after):
        self.count[eng] += 1
        self.items[eng].append((self.waits(eng, after), fn, self.sems[eng], 1))
        return (self.sems[eng], self.count[eng])

    def dma(self, eng, fn, sem, *after):
        self.dma_count[sem.name] = self.dma_count.get(sem.name, 0) + 16
        self.items[eng].append((self.waits(eng, after), fn, sem, 16))
        return (sem, self.dma_count[sem.name])

    def wait(self, eng, *after):
        self.items[eng].append((self.waits(eng, after), None, None, 0))

    def step(self, eng, fn, *after):
        self.items[eng].append((self.waits(eng, after), fn, None, 0))

    def all_done(self):
        return [(self.sems[e], self.count[e]) for e in self.sems if self.count[e]]

    def emit(self, name, eng):
        for waits, fn, sem, n in self.items[name]:
            for s, v in waits:
                eng.wait_ge(s, v)
            if sem is not None:
                fn(eng).then_inc(sem, n)
            elif fn is not None:
                fn(eng)


def build(nc, a, out):
    ctx = ExitStack()
    with ctx:
        def sb(name, shape, dt=F32):
            return ctx.enter_context(nc.sbuf_tensor(name, shape, dt))

        def sem(name):
            return ctx.enter_context(nc.semaphore(name))

        q = Queues({e: sem("s_" + e) for e in ("pe", "dve", "act", "pool")})
        put, dma = q.put, q.dma

        def vec(fn, *after):
            return put("dve", fn, (q.sems["dve"], q.count["dve"]), *after)

        def scal(fn, *after):
            return put("act", fn, (q.sems["act"], q.count["act"]), *after)

        x = sb("x", [P, 2, D])
        xn = sb("xn", [P, 2, D])
        hT = sb("hT", [P, 8, T])
        ring = sb("ring", [P, NSLOT, 2048])
        ident = sb("ident", [P, P])
        gain = sb("gain", [P, 2, D])
        small = sb("small", [P, 2560])
        arena = sb("arena", [P, AR])
        banks = ctx.enter_context(nc.psum_tensor("banks", [P, 8, 512], F32))

        bank_free = [None] * 8
        bank_next = [0]

        held = set()

        def bank(hold=False):
            while bank_next[0] % 8 in held:
                bank_next[0] += 1
            b = bank_next[0] % 8
            bank_next[0] += 1
            if hold:
                held.add(b)
            return b

        def dve_now():
            return (q.sems["dve"], q.count["dve"])

        def act_now():
            return (q.sems["act"], q.count["act"])

        slot_free = [None] * NSLOT
        slot_sem = [sem(f"s_slot{i}") for i in range(NSLOT)]
        slot_next = [0]

        def load(src, n):
            s = slot_next[0] % NSLOT
            slot_next[0] += 1
            dst = ring[:, s, 0:n * src.shape[2]].rearrange("p (k c) -> p k c", k=n)
            tok = dma("sp", lambda e: e.dma_start(dst, src), slot_sem[s], slot_free[s])
            return s, dst, tok

        q.items["sp"], q.seen["sp"] = [], {}

        const_sem = [0]

        def fetch(dst, src, *after, eng="act"):
            const_sem[0] += 1
            return dma(eng, lambda e: e.dma_start(dst, src), sem(f"s_c{const_sem[0]}"), *after)

        def row(ap, n):
            return ap.unsqueeze(0).to_broadcast([P, n])

        smallp = [0]

        def sm(*shape):
            n = int(np.prod(shape))
            if smallp[0] + n > 2560:
                raise ValueError("small")
            v = small[:, smallp[0]:smallp[0] + n]
            smallp[0] += n
            if len(shape) == 2:
                v = v.rearrange("p (a b) -> p a b", a=shape[0])
            if len(shape) == 3:
                v = v.rearrange("p (a b c) -> p a b c", a=shape[0], b=shape[1])
            return v

        mhalf = sm(64)
        t_mh = put("pool", lambda e: e.memset(mhalf, -0.5))
        t_id = fetch(ident[:, :], a["c_ident"], eng="sp")

        def rsqrt(dst, ss, n, *after):
            m = dst.shape[1]
            t = vec(lambda e: e.tensor_scalar(dst, ss, 1.0 / n, EPS, ALU.mult, ALU.add), *after)
            return put("pool", lambda e: e.tensor_tensor(dst, dst, mhalf[:, 0:m], ALU.pow), t, t_mh)

        def q_pe():
            return (q.sems["pe"], q.count["pe"])

        evac_turn = [0]

        def copy(eng, dst, src, *after):
            if eng == "act":
                return put("act", lambda e: e.copy(dst, src), *after)
            return put("dve", lambda e: e.tensor_copy(dst, src), *after)

        def evac(dst, src, *after):
            evac_turn[0] ^= 1
            return copy("act" if evac_turn[0] else "dve", dst, src, *after)

        def transposes(pairs, *after, eng=None):
            toks = []
            for dst, srcs in pairs:
                m = srcs[0].shape[1]
                b = bank()

                def go(e, b=b, srcs=srcs, m=m):
                    for i, s in enumerate(srcs):
                        r = e.transpose(banks[0:m, b, i * P:(i + 1) * P], s, ident[:, :])
                    return r
                t = put("pe", go, list(after), t_id, bank_free[b])
                n = len(srcs)
                src = banks[0:m, b, 0:n * P].rearrange("p (k c) -> p k c", k=n)
                t = copy(eng, dst, src, t) if eng else evac(dst, src, t)
                bank_free[b] = t
                toks.append(t)
            return toks

        gain_free = [None, None]
        gain_n = [0]

        def load_gain(src):
            g = gain_n[0] % 2
            gain_n[0] += 1
            return g, fetch(gain[:, g, :], row(src, D), gain_free[g])

        def rmsnorm(g, t_x, t_free, to_T=True):
            gi, t_g = g
            ss = sm(2)
            toks = []
            for c in range(2):
                t = scal(lambda e, c=c: e.activation(xn[:, c, :], x[:, c, :], ACT.Square,
                                                           accum_out=ss[:, c:c + 1]), t_x, t_free)
                t = rsqrt(ss[:, c:c + 1], ss[:, c:c + 1], D, t)
                t = vec(lambda e, c=c: e.scalar_tensor_tensor(
                    xn[:, c, :], x[:, c, :], ss[:, c:c + 1], gain[:, gi, :], ALU.mult, ALU.mult), t, t_g)
                toks.append(t)
            gain_free[gi] = toks[1]
            if not to_T:
                return toks, None
            tt = []
            for c in range(2):
                tt += transposes([(hT[:, k:k + 4, c * P:(c + 1) * P],
                                   [xn[:, c, (k + i) * P:(k + i + 1) * P] for i in range(4)])
                                  for k in (0, 4)], toks[c])
            return toks, tt

        def project_steps(w, c0, n, sink, t_h, lhs=None, kn=8):
            lhs = hT if lhs is None else lhs
            per = max(1, 2048 // n)
            b = [bank(hold=True), bank(hold=True)]
            k = 0
            while k < kn:
                m = min(per, kn - k, 4 if n == 512 else 8)
                s, wt, t_w = load(w[:, k:k + m, c0:c0 + n], m)
                for c in range(2):
                    def go(e, c=c, k=k, m=m, wt=wt):
                        for i in range(m):
                            r = e.matmul(banks[:, b[c], 0:n], lhs[:, k + i, c * P:(c + 1) * P], wt[:, i, :],
                                         start=(k + i == 0), stop=(k + i == kn - 1))
                        return r
                    t = put("pe", go, t_w, t_h, bank_free[b[c]] if k == 0 else None)
                    if k + m == kn:
                        bank_free[b[c]] = sink(c, banks[:, b[c], 0:n], t)
                        held.discard(b[c])
                slot_free[s] = t
                k += m
                yield

        def project(*args, **kw):
            for _ in project_steps(*args, **kw):
                pass

        filler = []

        def fill(n=1):
            for _ in range(n):
                while filler:
                    if next(filler[0], 0) != 0:
                        break
                    filler.pop(0)
                else:
                    return

        def kview(w):
            return w.rearrange("(k p) n -> p k n", p=P)

        t_x = fetch(x[:, :, :], a["x"][0].rearrange("(c p) d -> p c d", p=P), eng="sp")

        def finish(src, t):
            t_o = fetch(out[0].rearrange("(c p) d -> p c d", p=P), src, t, eng="sp")
            q.wait("sp", t_o)

        Pj = arena[:, 0:2 * 7712].rearrange("p (c n) -> p c n", c=2)
        off = 2 * 7712
        qd = arena[:, off:off + 3072].rearrange("p (j t) -> p j t", t=T)
        kd = arena[:, off + 3072:off + 6144].rearrange("p (j t) -> p j t", t=T)
        off += 6144
        Bm = arena[:, off:off + 3 * 128 + 3 * 256]
        off += 1152
        cm = arena[:, off:off + 384]
        off += 384
        E = arena[:, off:off + 3 * 768].rearrange("p (i n) -> p i n", i=3)
        off += 2304
        PT = arena[:, off:off + 2 * 768].rearrange("p (i n) -> p i n", i=2)
        off += 1536
        O = xn[:, 0, :].rearrange("p (c n) -> p c n", c=2)
        OT = xn[:, 1, :].rearrange("p (k t) -> p k t", k=4)
        kv_all = arena[:, off:off + 2048]
        off += 2048
        assert off <= AR, off
        vecs = sb("vecs", [P, 848])

        g_attn = load_gain(a["norm_attn"][0])
        t_B = fetch(Bm, a["c_band"], t_x, eng="pool")
        t_cm = fetch(cm, a["c_causal"], t_x, eng="pool")
        nckv = vecs[:, 0:256]
        t_v = [fetch(nckv, row(a["norm_ckv"][0], 256), t_x, eng="pool"),
               fetch(vecs[:, 256:352], row(a["q_norm_mla"][0], 96), t_x, eng="pool"),
               fetch(vecs[:, 352:448], row(a["k_norm_mla"][0], 96), t_x, eng="pool"),
               fetch(vecs[:, 448:640], row(a["q_norm_dil"].rearrange("l g d -> (l g d)"), 192)),
               fetch(vecs[:, 640:832], row(a["k_norm_dil"].rearrange("l g d -> (l g d)"), 192)),
               fetch(vecs[:, 832:848], a["c_freq"], t_x, eng="pool")]
        rb = sm(36)
        rw = sm(8, 36)
        t_v += [fetch(rb[:, 0:4], row(a["b_router_group"][0], 4), t_x, eng="pool"),
                fetch(rb[:, 4:36], row(a["b_router_expert"][0], 32), t_x, eng="pool"),
                fetch(rw[:, :, 0:4], kview(a["w_router_group"][0]), t_x, eng="pool"),
                fetch(rw[:, :, 4:36], kview(a["w_router_expert"][0]), t_x, eng="pool")]
        pos_i = sb("pos_i", [P, 2], I32)
        t_pos = fetch(pos_i[:, :], a["c_pos"], t_x, eng="pool")

        _, t_h = rmsnorm(g_attn, t_x, None)
        g_ffn = load_gain(a["norm_ffn"][0])

        posf = sm(2)
        ang = sm(2, 16)
        kk = sm(2, 16)
        sn = sm(2, 16)
        cs = sm(2, 16)
        MAGIC = 12582912.0
        C1, C2, C3 = 6.28125, 0.0019350051879882812, 3.0199157663448e-7
        t = vec(lambda e: e.tensor_copy(posf, pos_i[:, :]), t_pos)
        for c in range(2):
            t = vec(lambda e, c=c: e.tensor_scalar(ang[:, c, :], vecs[:, 832:848], posf[:, c:c + 1],
                                                          None, ALU.mult), t, t_v[5])
        t = vec(lambda e: e.tensor_scalar(kk, ang, float(1 / (2 * np.pi)), None, ALU.mult), t)
        t = vec(lambda e: e.tensor_scalar(kk, kk, MAGIC, None, ALU.add), t)
        t = vec(lambda e: e.tensor_scalar(kk, kk, MAGIC, None, ALU.subtract), t)
        for cc in (C1, C2, C3):
            t = vec(lambda e, cc=cc: e.scalar_tensor_tensor(ang, kk, -cc, ang, ALU.mult, ALU.add), t)
        t = vec(lambda e: e.tensor_scalar(ang, ang, float(np.float32(3.1415925)), float(np.float32(-3.1415925)), ALU.min, ALU.max), t)
        t1 = scal(lambda e: e.activation(sn, ang, ACT.Sin), t)
        t2 = scal(lambda e: e.activation(cs, ang, ACT.Sin, scale=0.5), t)
        t = vec(lambda e: e.tensor_tensor(cs, cs, cs, ALU.mult), t1, t2)
        t_rope = vec(lambda e: e.tensor_scalar(cs, cs, -2.0, 1.0, ALU.mult, ALU.add), t)

        w_in = kview(a["w_in"][0])
        t_P = {}

        def sink_P(c0, n):
            def go(c, ps, t):
                t = evac(Pj[:, c, c0:c0 + n], ps, t)
                t_P[(c0, c)] = t
                return t
            return go

        def pt(lo, hi):
            return [t for (c0, c), t in t_P.items() if lo <= c0 < hi]

        for c0, n in ((512, 512), (1024, 32), (0, 512)):
            project(w_in, c0, n, sink_P(c0, n), t_h)

        def sink_act(c0):
            def go(c, ps, t):
                t_P[(c0, c)] = t = copy("act", Pj[:, c, c0:c0 + 512], ps, t)
                return t
            return go

        b_gate = a["b_gate"].rearrange("l g d -> (l g d)")

        def gate_steps(c0):
            lo = c0 - 5664
            s, bt, t_bias = load(b_gate[lo:lo + 512].unsqueeze(0).unsqueeze(0).to_broadcast([P, 1, 512]), 1)

            def go(c, ps, t):
                v = Pj[:, c, c0:c0 + 512]
                t = put("dve", lambda e: e.tensor_tensor(v, ps, bt[:, 0, :], ALU.add), t, t_bias)
                t_P[(c0, c)] = slot_free[s] = t
                return t
            yield from project_steps(w_in, c0, 512, go, t_h)

        filler.extend(project_steps(w_in, 1056 + 512 * j, 512, sink_act(1056 + 512 * j), t_h)
                      for j in (0, 3, 6, 1, 4, 7, 2, 5, 8))
        filler.extend(gate_steps(5664 + 512 * j) for j in range(4))

        def need(lo, hi):
            want = [(c0, c) for c0 in range(1056, 7712, 512) if lo <= c0 < hi for c in range(2)]
            while any(w_ not in t_P for w_ in want):
                fill()
            return [t_P[w_] for w_ in want]

        scratch = gain[:, 0, :]
        s_free = [gain_free[0]]
        ssq = sm(2, 24)
        ss_n = [0]

        def headnorm(v, g, n, *after):
            h = v.shape[1]
            sq = scratch[:, 0:h * n].rearrange("p (h n) -> p h n", h=h)
            ss = ssq[:, ss_n[0] % 2, 0:h]
            ss_n[0] += 1
            t = scal(lambda e: e.activation(sq, v, ACT.Square), s_free[0], *after)
            s_free[0] = t = vec(lambda e: e.tensor_reduce(ss, sq, X, ALU.add), t)
            t = rsqrt(ss, ss, n, t)
            t = vec(lambda e: e.tensor_tensor(v, v, ss.unsqueeze(2).to_broadcast([P, h, n]), ALU.mult), t)
            return vec(lambda e: e.tensor_tensor(v, v, g, ALU.mult), t)

        def rope(v, c_, s_, half, tmp, *after):
            h = v.shape[1]
            a1, a2 = v[:, :, 0:half], v[:, :, half:2 * half]
            cb = c_.unsqueeze(1).to_broadcast([P, h, half])
            sb_ = s_.unsqueeze(1).to_broadcast([P, h, half])
            u = [tmp[:, i * h * half:(i + 1) * h * half].rearrange("p (h n) -> p h n", h=h) for i in range(4)]
            t = [dve_now(), *after]
            put("dve", lambda e: e.tensor_tensor(u[0], a1, cb, ALU.mult), t)
            put("dve", lambda e: e.tensor_tensor(u[1], a2, sb_, ALU.mult), t)
            put("dve", lambda e: e.tensor_tensor(u[2], a2, cb, ALU.mult), t)
            t = put("dve", lambda e: e.tensor_tensor(u[3], a1, sb_, ALU.mult), t)
            put("dve", lambda e: e.tensor_tensor(a1, u[0], u[1], ALU.subtract), t)
            return put("dve", lambda e: e.tensor_tensor(a2, u[2], u[3], ALU.add), t)

        xflat = xn[:, :, :].rearrange("p c n -> p (c n)")
        K = xflat[:, 0:1536].rearrange("p (c h n) -> p c h n", c=2, h=8)
        ckT = xflat[:, 1536:2048].rearrange("p (k t) -> p k t", k=2)
        t_mla = [t_P[(c0, c)] for c0 in (0, 512, 1024) for c in range(2)]
        t_ckv = [t_P[(512, c)] for c in range(2)]
        ssc = sm(2)
        t_x0 = q_pe()
        for c in range(2):
            v = Pj[:, c, 768:1024]
            t = scal(lambda e, v=v, c=c: e.activation(xn[:, c, 0:256], v, ACT.Square,
                                                      accum_out=ssc[:, c:c + 1]), t_ckv, t_x0)
        t = rsqrt(ssc, ssc, 256, t)
        for c in range(2):
            v = Pj[:, c, 768:1024]
            t = vec(lambda e, v=v, c=c: e.scalar_tensor_tensor(
                v, v, ssc[:, c:c + 1], nckv, ALU.mult, ALU.mult), t, t_v[0])
        fill(1)
        t_ck = []
        for c in range(2):
            t_ck += transposes([(ckT[:, :, c * P:(c + 1) * P],
                                 [Pj[:, c, 768 + i * P:768 + (i + 1) * P] for i in range(2)])], t, eng="act")
        t_q, t_k = [], []
        for c in range(2):
            qv = Pj[:, c, 0:768].rearrange("p (h n) -> p h n", h=8)
            t = headnorm(qv, vecs[:, 256:352].unsqueeze(1).to_broadcast([P, 8, 96]), 96, t_mla, t_v[1])
            t_q.append(rope(qv[:, :, 64:96], cs[:, c, :], sn[:, c, :], 16, scratch, t, t_rope))
            s_free[0] = dve_now()
        fill(1)
        kv = kv_all.rearrange("p (c n) -> p c n", c=2)
        t_kv = []

        def kv_sink(c0):
            def go(c, ps, t):
                t = copy("act", kv[:, c, c0:c0 + 512], ps, t)
                t_kv.append(t)
                return t
            return go

        wu = a["w_ukv"][0].rearrange("(k p) n -> p k n", p=P)
        for c0 in (0, 512):
            project(wu, c0, 512, kv_sink(c0), t_ck, lhs=ckT, kn=2)
        kv4 = kv_all.rearrange("p (c h n) -> p c h n", c=2, h=8)
        for c in range(2):
            t = vec(lambda e, c=c: e.tensor_copy(K[:, c, :, 0:64], kv4[:, c, :, 0:64]), t_kv)
            t = vec(lambda e, c=c: e.tensor_copy(
                K[:, c, :, 64:96], Pj[:, c, 1024:1056].unsqueeze(1).to_broadcast([P, 8, 32])), t_mla)
            t = headnorm(K[:, c, :, :], vecs[:, 352:448].unsqueeze(1).to_broadcast([P, 8, 96]), 96, t, t_v[2])
            t_k.append(rope(K[:, c, :, 64:96], cs[:, c, :], sn[:, c, :], 16, scratch, t, t_rope))
            s_free[0] = dve_now()
        qT = qd[0:96, 0:8, :]
        kT = kd[0:96, 0:8, :]
        fill(2)
        t_T = []
        for c in range(2):
            for hh in (0, 4):
                t_T += transposes([(qT[:, hh:hh + 4, c * P:(c + 1) * P],
                                    [Pj[:, c, 96 * h:96 * h + 96] for h in range(hh, hh + 4)])], t_q[c], eng="act")
        fill(1)
        for c in range(2):
            for hh in (0, 4):
                t_T += transposes([(kT[:, hh:hh + 4, c * P:(c + 1) * P],
                                    [K[:, c, h, :] for h in range(hh, hh + 4)])], t_k[c], eng="act")
            fill(1)

        e_free = [None] * 3
        pt_free = [None] * 2
        mx = sm(3, 2)
        den = sm(16)
        den_free = [None, None]
        rden = sm(8)

        def attend(jobs, fills):
            state = {}

            def scores(n):
                c, parts, scale, vs, ob, oc, dh, dcol, after = jobs[n]
                i = n % 3
                groups, at, col = [], 512, 0
                for p in parts:
                    if at + p[2] > 512:
                        groups.append((bank(), []))
                        at = 0
                    groups[-1][1].append((at, p, col))
                    at += p[2]
                    col += p[2]
                for b, ps in groups:
                    def go(e, b=b, ps=ps):
                        for at, p, _ in ps:
                            r = e.matmul(banks[:, b, at:at + p[2]], p[0], p[1], start=True, stop=True)
                        return r
                    t = put("pe", go, after, bank_free[b])
                    for at, p, col in ps:
                        t2 = put("dve", lambda e, b=b, at=at, p=p, col=col: e.scalar_tensor_tensor(
                            E[:, i, col:col + p[2]], p[3], p[4], banks[:, b, at:at + p[2]], ALU.mult, ALU.add),
                            t, e_free[i], t_B, t_cm)
                    bank_free[b] = t2
                wide = sum(p[2] for p in parts)
                ev = E[:, i, 0:wide]
                t = put("dve", lambda e: e.tensor_reduce(mx[:, i, 0:1], ev, X, ALU.max), t2)
                t = put("dve", lambda e: e.tensor_scalar(mx[:, i, 1:2], mx[:, i, 0:1], -scale, None, ALU.mult), t)
                t = put("act", lambda e: e.activation(ev, ev, ACT.Exp, bias=mx[:, i, 1:2], scale=scale,
                                                      accum_out=den[:, dcol:dcol + 1]), t, den_free[c])
                state[n] = t, wide // P

            def turn(n):
                t, m = state[n]
                i, o = n % 3, n % 2
                tp = []
                for j in range(0, m, 4):
                    w_ = min(4, m - j)
                    tp += transposes([(PT[:, o, j * P:(j + w_) * P].rearrange("p (k c) -> p k c", k=w_),
                                       [E[:, i, (j + r) * P:(j + r + 1) * P] for r in range(w_)])], t, pt_free[o],
                                     eng="act")
                e_free[i] = q_pe()
                state[n] = tp, m, t

            def values(n):
                c, parts, scale, vs, ob, oc, dh, dcol, after = jobs[n]
                tp, m, t_exp = state.pop(n)
                o = n % 2

                def pv(e):
                    for j in range(m):
                        r = e.matmul(banks[:, ob, oc:oc + dh], PT[:, o, j * P:(j + 1) * P], vs[j],
                                     start=(j == 0), stop=(j == m - 1))
                    return r
                pt_free[o] = t = put("pe", pv, tp, bank_free[ob] if oc == 0 else None)
                done[n] = [t, t_exp]

            done = {}
            for n in range(len(jobs) + 2):
                if n < len(jobs):
                    scores(n)
                fill(fills(n))
                if 1 <= n <= len(jobs):
                    turn(n - 1)
                if n >= 2:
                    values(n - 2)
                    c, ob = jobs[n - 2][0], jobs[n - 2][4]
                    if n == len(jobs) + 1 or jobs[n - 1][0] != c:
                        yield c, ob, done[n - 2]

        def normalise(c, ob, dst, h, dh, t):
            dv = den[:, 8 * c:8 * c + h]
            den_free[c] = vec(lambda e: e.reciprocal(rden[:, 0:h], dv), t)
            t = vec(lambda e: e.tensor_tensor(
                dst.rearrange("p (h n) -> p h n", h=h),
                banks[:, ob, 0:h * dh].rearrange("p (h n) -> p h n", h=h),
                rden[:, 0:h].unsqueeze(2).to_broadcast([P, h, dh]), ALU.mult), t)
            bank_free[ob] = t
            held.discard(ob)
            return t

        def causal_part(c, lhsT, rhs_of):
            return (lhsT, rhs_of(0, (c + 1) * P), (c + 1) * P, cm[:, 0:P] if c == 0 else cm[:, P:384], 1.0)

        jobs = []
        for c in range(2):
            ob = bank(hold=True)
            for h in range(8):
                parts = [causal_part(c, qT[:, h, c * P:(c + 1) * P], lambda lo, hi, h=h: kT[:, h, lo:hi])]
                jobs.append((c, parts, 96 ** -0.5, [kv4[:, kc, h, 64:128] for kc in range(c + 1)],
                             ob, 64 * h, 64, 8 * c + h, t_T))
        t_o = []
        for c, ob, t in attend(jobs, lambda n: 1 if n < 10 else 0):
            t_o.append(normalise(c, ob, O[:, c, :], 8, 64, t))

        t_d = {}
        t_qfree = q_pe()
        t_OT = []
        for g in range(3):
            for w, go_ in ((0, 448), (1, 640)):
                need(1056 + 1536 * w + 512 * g, 1056 + 1536 * w + 512 * g + 1)
        for g in range(3):
            for c in range(2):
                for w, go_ in ((0, 448), (1, 640)):
                    lo = 1056 + 1536 * w + 512 * g
                    v = Pj[:, c, lo:lo + 512].rearrange("p (h n) -> p h n", h=8)
                    gv = vecs[:, go_ + 64 * g:go_ + 64 * g + 64].unsqueeze(1).to_broadcast([P, 8, 64])
                    t_d[(w, c, g)] = headnorm(v, gv, 64, need(lo, lo + 1), t_v[3], t_v[4])
        for c in range(2):
            t_OT += transposes([(OT[:, :, c * P:(c + 1) * P], [O[:, c, k * P:(k + 1) * P] for k in range(4)])],
                               t_o[c], eng="act")
        t_T = []
        for g in range(3):
            for c in range(2):
                for w, dst in ((0, qd), (1, kd)):
                    lo = 1056 + 1536 * w + 512 * g
                    t_T += transposes([(dst[:, 4 * g:4 * g + 4, c * P:(c + 1) * P],
                                        [Pj[:, c, lo + P * i:lo + P * (i + 1)] for i in range(4)])],
                                      t_d[(w, c, g)], t_qfree, eng="act")
                fill(1)

        t_m = []
        t_sig = {}

        def sigmoid():
            t_g = need(5664, 7712)
            for c in range(2):
                v = Pj[:, c, 5664:7712]
                t_sig[c] = scal(lambda e, v=v: e.activation(v, v, ACT.Sigmoid), t_g)

        def m0_steps(c0):
            if not t_sig:
                sigmoid()

            def go(c, ps, t):
                g = Pj[:, c, 5664 + c0:5664 + c0 + 512]
                t = vec(lambda e: e.tensor_tensor(g, g, ps, ALU.mult), t, t_sig[c])
                t_m.append(t)
                return t
            yield from project_steps(kview(a["w_o_mla"][0]), c0, 512, go, t_OT, lhs=OT, kn=4)

        t_v8 = need(4128, 5664)
        need(5664, 7712)
        filler.extend(m0_steps(c0) for c0 in (0, 512))
        jobs = []
        for c in range(2):
            ob = bank(hold=True)
            for h in range(8):
                p0 = 64 * (h % 2)
                slope = 2.0 ** (-8.0 * (h + 1.0) / 8)
                kw = (c + 1) * P
                bo = 0 if c == 0 else 384
                parts = [(qd[p0:p0 + 64, 4 * g + h // 2, c * P:(c + 1) * P],
                          kd[p0:p0 + 64, 4 * g + h // 2, 0:kw], kw,
                          Bm[:, bo + g * kw:bo + (g + 1) * kw], -8.0 * slope) for g in range(3)]
                vs = [Pj[:, kc, 4128 + 512 * g + 64 * h:4128 + 512 * g + 64 * h + 64]
                      for g in range(3) for kc in range(c + 1)]
                jobs.append((c, parts, 0.125, vs, ob, 64 * h, 64, 8 * c + h, [t_T, t_v8]))
        t_o = []
        for c, ob, t in attend(jobs, lambda n: 1 if n in (3, 5, 7, 9) else 0):
            t_o.append(normalise(c, ob, O[:, c, :], 8, 64, [t, t_OT]))
        fill(4)
        t_f = q_pe()
        t_OT = []
        for c in range(2):
            t_OT += transposes([(OT[:, :, c * P:(c + 1) * P], [O[:, c, k * P:(k + 1) * P] for k in range(4)])],
                               t_o[c], t_f)
        t_m2 = []

        def m1_sink(c0):
            def go(c, ps, t):
                g = Pj[:, c, 6688 + c0:6688 + c0 + 512]
                m = Pj[:, c, 5664 + c0:5664 + c0 + 512]
                t = t_b = vec(lambda e: e.tensor_tensor(g, g, ps, ALU.mult), t, t_sig[c])
                t_m2.append(vec(lambda e: e.tensor_tensor(m, m, g, ALU.add), t, t_m))
                return t_b
            return go

        for c0 in (0, 512):
            project(kview(a["w_o_dil"][0]), c0, 512, m1_sink(c0), t_OT, lhs=OT, kn=4)
        t_hT = []
        t_f = q_pe()
        for c in range(2):
            t_hT += transposes([(hT[:, k:k + 4, c * P:(c + 1) * P],
                                 [Pj[:, c, 5664 + (k + i) * P:5664 + (k + i + 1) * P] for i in range(4)])
                                for k in (0, 4)], t_m2, t_f)

        def residual_sink(toks, c0):
            def go(c, ps, t):
                v = x[:, c, c0:c0 + 512]
                t = vec(lambda e: e.tensor_tensor(v, v, ps, ALU.add), t)
                toks.append(t)
                return t
            return go

        t_r = []
        for c0 in (0, 512):
            project(kview(a["w_out"][0]), c0, 512, residual_sink(t_r, c0), t_hT)
        gain_free[0] = q.all_done()

        t_xn, t_h = rmsnorm(g_ffn, t_r, q_pe())
        t_fence = q.all_done()
        NT = 35
        NTW = 36
        NONE = 4095.0
        at = [0]

        def take(n):
            v = arena[:, at[0]:at[0] + n]
            at[0] += n
            assert at[0] <= AR
            return v
        lg = take(72).rearrange("p (c n) -> p c n", c=2)
        oh = take(128).rearrange("p (c k n) -> p c k n", c=2, k=2)
        Ms = take(64).rearrange("p (c n) -> p c n", c=2)
        g8, v8, w8, w1 = take(8), take(8), take(8), take(8)
        idx = take(16).bitcast(U32)
        gone = take(4)
        ek, wk, rk, ok, fk = take(4), take(4), take(4), take(4), take(4)
        rks = take(96)
        over, oi, oo, eqo = take(32), take(32), take(32), take(32)
        jk = take(32)
        overT = take(128)
        eo = take(3)
        iota32, ids = take(32), take(4)
        idu, slot_idx = take(4).bitcast(U32), take(4).bitcast(U32)
        eo_u = take(3).bitcast(U32)
        fill_u = take(NTW).bitcast(U32)
        tab_r = take(NTW).bitcast(U32)
        tab_g = take(NTW).bitcast(U32)
        tri = take(P)
        tri32 = take(32)
        ones = take(P)
        xg = take(4 * D).rearrange("p (i d) -> p i d", i=4)
        gT = take(3 * D).rearrange("p (i k t) -> p i k t", i=3, k=8)
        he = take(512).rearrange("p (i n) -> p i n", i=2)
        heT = take(512).rearrange("p (i f t) -> p i f t", i=2, f=2)
        ys = take(3 * D).rearrange("p (i d) -> p i d", i=3)
        yb = take(4 * D).rearrange("p (c k d) -> p c k d", c=2, k=2)

        h_rows = nc.dram_tensor("h_rows", [T, D], F32).ap()
        y_rows = nc.dram_tensor("y_rows", [2 * T, D], F32).ap()
        slots = nc.dram_tensor("slots", [P * NTW, 1], U32).ap()

        t_tri = fetch(tri, a["c_tri"], t_fence)
        t_tri32 = fetch(tri32[0:32, :], a["c_tri"][0:32, 0:32], t_fence)
        t_hr = fetch(h_rows.rearrange("(c p) d -> p c d", p=P), xn[:, :, :], t_xn, eng="sp")
        t_one = put("pool", lambda e: e.memset(ones, 1.0), t_fence)
        t_x0 = put("pool", lambda e: e.memset(fill_u, int(NONE)), t_fence)
        t_s0 = fetch(slots.rearrange("(p t) o -> p (t o)", p=P), fill_u, t_x0)
        put("pool", lambda e: e.iota(iota32, [[1, 32]], base=0, channel_multiplier=0,
                                     allow_small_or_imprecise_dtypes=True), t_fence)
        t_io = put("pool", lambda e: e.iota(ids.rearrange("p (c k) -> p c k", c=2), [[2 * P, 2], [1, 2]], base=0,
                                     channel_multiplier=2, allow_small_or_imprecise_dtypes=True), t_fence)
        t_xg = put("pool", lambda e: e.memset(xg, 0.0), t_fence)
        t_ids = vec(lambda e: e.tensor_copy(idu, ids), t_io, t_fence)

        br = bank()

        def router(e):
            for c in range(2):
                for k in range(8):
                    r = e.matmul(banks[:, br, 64 * c:64 * c + 36], hT[:, k, c * P:(c + 1) * P], rw[:, k, :],
                                 start=(k == 0), stop=(k == 7))
            return r
        t = put("pe", router, t_h, t_v, bank_free[br])
        for c in range(2):
            t = vec(lambda e, c=c: e.tensor_tensor(lg[:, c, :], banks[:, br, 64 * c:64 * c + 36], rb, ALU.add),
                    t, t_v)
        bank_free[br] = t
        for c in range(2):
            l = lg[:, c, :]
            t = vec(lambda e: e.memset(g8, NEG), t)
            t = vec(lambda e, l=l: e.tensor_copy(g8[:, 0:4], l[:, 0:4]), t)
            t = vec(lambda e: e.max(v8, g8), t)
            t = vec(lambda e: e.max_index(idx[:, 0:8], v8, g8), t)
            t = vec(lambda e: e.tensor_scalar(w1[:, 0:1], v8[:, 0:1], -1.0, None, ALU.mult), t)
            ta = scal(lambda e: e.activation(w8[:, 0:4], g8[:, 0:4], ACT.Exp, bias=w1[:, 0:1],
                                             accum_out=w1[:, 1:2]), t)
            t = vec(lambda e: e.tensor_copy(w1[:, 2:3], idx[:, 0:1]), t)
            t = vec(lambda e: e.tensor_scalar(gone, iota32[:, 0:4], w1[:, 2:3], None, ALU.is_equal), t, t_io)
            sel = Ms[:, c, :].rearrange("p (g e) -> p g e", g=4)
            t = vec(lambda e, l=l, sel=sel: e.tensor_tensor(
                sel, l[:, 4:36].rearrange("p (g e) -> p g e", g=4),
                gone.unsqueeze(2).to_broadcast([P, 4, 8]), ALU.mult), t)
            t = vec(lambda e, sel=sel: e.tensor_reduce(g8, sel.rearrange("p g e -> p e g"), X, ALU.add), t, ta)
            t = vec(lambda e: e.max(v8, g8), t)
            t = vec(lambda e: e.max_index(idx[:, 0:8], v8, g8), t)
            t = vec(lambda e: e.tensor_copy(w1[:, 4:6], idx[:, 0:2]), t)
            t = vec(lambda e, c=c: e.scalar_tensor_tensor(
                ek[:, 2 * c:2 * c + 2], w1[:, 2:3].to_broadcast([P, 2]), 8.0, w1[:, 4:6], ALU.mult, ALU.add), t)
            t = vec(lambda e: e.tensor_scalar(w1[:, 0:1], v8[:, 0:1], -1.0, None, ALU.mult), t)
            ta = scal(lambda e: e.activation(w8[:, 0:2], v8[:, 0:2], ACT.Exp, bias=w1[:, 0:1],
                                             accum_out=w1[:, 6:7]), t)
            for k in range(2):
                t = vec(lambda e, c=c, k=k: e.tensor_scalar(
                    oh[:, c, k, :], iota32, ek[:, 2 * c + k:2 * c + k + 1], None, ALU.is_equal), t)
            t_M = t = vec(lambda e, c=c: e.tensor_tensor(Ms[:, c, :], oh[:, c, 0, :], oh[:, c, 1, :], ALU.add), t)
            t = vec(lambda e: e.tensor_scalar(w1[:, 6:7], w1[:, 6:7], w1[:, 1:2], None, ALU.mult), ta)
            t = vec(lambda e: e.reciprocal(w1[:, 6:7], w1[:, 6:7]), t)
            t = t_wk = vec(lambda e, c=c: e.tensor_scalar(wk[:, 2 * c:2 * c + 2], w8[:, 0:2], w1[:, 6:7], None,
                                                          ALU.mult), t)

        bk = bank()

        def ranks(e):
            e.matmul(banks[:, bk, 0:32], tri, Ms[:, 0, :], start=True, stop=True)
            e.matmul(banks[:, bk, 32:64], tri, Ms[:, 1, :], start=True, stop=False)
            e.matmul(banks[:, bk, 32:64], ones, Ms[:, 0, :], start=False, stop=True)
            e.matmul(banks[:, bk, 64:96], ones, Ms[:, 0, :], start=True, stop=False)
            return e.matmul(banks[:, bk, 64:96], ones, Ms[:, 1, :], start=False, stop=True)
        t1 = put("pe", ranks, t_M, t_tri, t_one, bank_free[bk])
        bk2 = bank()

        def counts(e):
            e.matmul(banks[0:32, bk2, 0:P], Ms[:, 0, :], ones, start=True, stop=False)
            return e.matmul(banks[0:32, bk2, 0:P], Ms[:, 1, :], ones, start=False, stop=True)
        t2 = put("pe", counts, bank_free[bk2])
        t = vec(lambda e: e.tensor_scalar(overT[0:32, :], banks[0:32, bk2, 0:P], float(P), None, ALU.is_gt), t2)
        bank_free[bk2] = t
        bk3 = bank()
        t3 = put("pe", lambda e: e.matmul(banks[:, bk3, 0:32], overT[0:32, :], tri32[0:32, :], start=True, stop=True),
                 t, t_tri32, bank_free[bk3])
        t = vec(lambda e: e.tensor_copy(rks, banks[:, bk, 0:96]), t1)
        bank_free[bk] = t
        for c in range(2):
            for k in range(2):
                t = vec(lambda e, c=c, k=k: e.tensor_tensor_reduce(
                    jk, oh[:, c, k, :], rks[:, 32 * c:32 * c + 32], 1.0, 0.0, ALU.mult, ALU.add,
                    rk[:, 2 * c + k:2 * c + k + 1]), t)
        t = vec(lambda e: e.tensor_scalar(over, rks[:, 64:96], float(P), None, ALU.is_gt), t)
        t = vec(lambda e: e.tensor_copy(oo, banks[:, bk3, 0:32]), t3)
        bank_free[bk3] = t
        for c in range(2):
            for k in range(2):
                t = vec(lambda e, c=c, k=k: e.tensor_tensor_reduce(
                    jk, oh[:, c, k, :], oo, 1.0, 0.0, ALU.mult, ALU.add, ok[:, 2 * c + k:2 * c + k + 1]), t)
        t = vec(lambda e: e.tensor_scalar(fk, rk, float(P), None, ALU.is_ge), t)
        t = vec(lambda e: e.scalar_tensor_tensor(rk, fk, -float(P), rk, ALU.mult, ALU.add), t)
        t = vec(lambda e: e.tensor_tensor(ok, ok, ek, ALU.subtract), t)
        t = vec(lambda e: e.scalar_tensor_tensor(ok, ok, 32.0, fk, ALU.add, ALU.mult), t)
        t = vec(lambda e: e.tensor_tensor(ok, ok, ek, ALU.add), t)
        t_slot = vec(lambda e: e.scalar_tensor_tensor(slot_idx, rk, float(NTW), ok, ALU.mult, ALU.add), t)
        sc_sem = sem("s_slots")
        for j in range(4):
            t_sc = dma("pool", lambda e, j=j: e.indirect_dma_start(
                slots, bass.IndirectOffsetOnAxis(ap=slot_idx[:, j:j + 1], axis=0), idu[:, j:j + 1], None),
                sc_sem, t_slot, t_s0, t_ids)
        t_tab = fetch(tab_r, slots.rearrange("(p t) o -> p (t o)", p=P), t_sc)
        t_tabg = vec(lambda e: e.tensor_scalar(tab_g, tab_r, 1, None, ALU.logical_shift_right), t_tab)
        t = vec(lambda e: e.tensor_tensor(oi, over, iota32, ALU.mult))
        for o in range(3):
            t = vec(lambda e, o=o: e.tensor_scalar(eqo, oo, float(o), None, ALU.is_equal), t)
            t = vec(lambda e, o=o: e.tensor_tensor_reduce(jk, eqo, oi, 1.0, 0.0, ALU.mult, ALU.add, eo[:, o:o + 1]), t)
        t_eo = vec(lambda e: e.tensor_copy(eo_u, eo), t)
        second = {}

        def read_expert(o):
            def go(e):
                second[o] = e.value_load(eo_u[0:1, o:o + 1], min_val=0, max_val=31)
            q.step("sp", go, t_eo)

        xg_sems = [sem(f"s_xg{i}") for i in range(4)]
        ys_sems = [sem(f"s_ys{i}") for i in range(3)]
        xg_free = [t_xg] * 4
        ys_free = [t_fence] * 3
        gT_free, he_free, heT_free = [t_fence] * 3, [t_fence] * 2, [t_fence] * 2
        xg_tok = {}

        def rows_in(n):
            i = n % 4
            xg_tok[n] = dma("pool", lambda e: e.indirect_dma_start(
                xg[:, i, :], None, h_rows, bass.IndirectOffsetOnAxis(ap=tab_g[:, n:n + 1], axis=0),
                bounds_check=T - 1, oob_is_err=False), xg_sems[i], xg_free[i], t_tabg, t_hr, t_xg)

        def expert(w, n):
            if n < 32:
                return w[0][n]
            return w[0][bass.ds(second[n - 32], 1)].rearrange("a r c -> (a r) c")

        def load_pair(n, kk):
            s = slot_next[0] % NSLOT
            slot_next[0] += 1
            dst = ring[:, s, :].rearrange("p (k g c) -> p k g c", k=4, g=2)
            for g_, w in enumerate((a["w_gate"], a["w_up"])):
                t = dma("sp", lambda e, g_=g_, w=w: e.dma_start(
                    dst[:, :, g_, :], expert(w, n).rearrange("(k p) n -> p k n", p=P)[:, kk:kk + 4, :]),
                    slot_sem[s], slot_free[s])
            return s, dst.rearrange("p k g c -> p k (g c)"), t

        def turn_rows(n):
            if n + 3 < NT:
                rows_in(n + 3)
            i = n % 4
            t = transposes([(gT[:, n % 3, k:k + 4, :],
                             [xg[:, i, (k + r_) * P:(k + r_ + 1) * P] for r_ in range(4)])
                            for k in (0, 4)], xg_tok[n], gT_free[n % 3])
            xg_free[i] = q_pe()
            return t

        def up(n, tt):
            if n >= 32:
                read_expert(n - 32)
            j = n % 2
            b = bank(hold=True)
            for kk in (0, 4):
                s, wt, t_w = load_pair(n, kk)

                def go(e, kk=kk, wt=wt):
                    for k in range(4):
                        r = e.matmul(banks[:, b, :], gT[:, n % 3, kk + k, :], wt[:, k, :],
                                     start=(kk + k == 0), stop=(kk + k == 7))
                    return r
                t = put("pe", go, t_w, tt, bank_free[b])
                slot_free[s] = t
            gT_free[n % 3] = t
            hv = he[:, j, :]
            t = put("act", lambda e: e.activation(hv, banks[:, b, 0:256], ACT.Silu), t, he_free[j])
            t = put("dve", lambda e: e.tensor_tensor(hv, hv, banks[:, b, 256:512], ALU.mult), t)
            bank_free[b] = t
            held.discard(b)
            return t

        def turn_he(n, t_he):
            j = n % 2
            tt = transposes([(heT[:, j, :, :], [he[:, j, f * P:(f + 1) * P] for f in range(2)])], t_he, heT_free[j],
                            eng="act")
            he_free[j] = q_pe()
            return tt

        def down(n, tt):
            j = n % 2
            i = n % 3
            s = slot_next[0] % NSLOT
            slot_next[0] += 1
            wt = ring[:, s, :].rearrange("p (k c) -> p k c", k=2)
            t_w = dma("sp", lambda e: e.dma_start(
                wt, expert(a["w_down"], n).rearrange("(k p) n -> p k n", p=P)), slot_sem[s], slot_free[s])
            tc = []
            for hf in range(2):
                b = bank()

                def go(e, hf=hf, b=b):
                    for f in range(2):
                        r = e.matmul(banks[:, b, :], heT[:, j, f, :], wt[:, f, hf * 512:(hf + 1) * 512],
                                     start=(f == 0), stop=(f == 1))
                    return r
                t = put("pe", go, t_w, tt, bank_free[b])
                bank_free[b] = t2 = evac(ys[:, i, hf * 512:(hf + 1) * 512], banks[:, b, :], t, ys_free[i])
                tc.append(t2)
            slot_free[s] = heT_free[j] = t
            ys_free[i] = dma("pool", lambda e: e.indirect_dma_start(
                y_rows, bass.IndirectOffsetOnAxis(ap=tab_r[:, n:n + 1], axis=0), ys[:, i, :], None,
                bounds_check=2 * T - 1, oob_is_err=False), ys_sems[i], tc)

        for n in range(3):
            rows_in(n)
        tts = {0: turn_rows(0), 1: turn_rows(1)}
        pend = up(0, tts[0])
        for n in range(NT):
            if n + 2 < NT:
                tts[n + 2] = turn_rows(n + 2)
            th = turn_he(n, pend)
            if n + 1 < NT:
                pend = up(n + 1, tts[n + 1])
            down(n, th)
        t_yb = fetch(yb, y_rows.rearrange("(c p k) d -> p c k d", p=P, k=2), ys_free)
        t_r = []
        for c in range(2):
            for k in range(2):
                t = vec(lambda e, c=c, k=k: e.scalar_tensor_tensor(
                    x[:, c, :], yb[:, c, k, :], wk[:, 2 * c + k:2 * c + k + 1], x[:, c, :], ALU.mult, ALU.add),
                    t_yb, t_wk)
            t_r.append(t)

        g_mix0 = load_gain(a["norm_mix_2"][0])
        P2 = arena[:, 0:7168].rearrange("p (c n) -> p c n", c=2)
        q2 = arena[:, 7168:7168 + 4096].rearrange("p (j t) -> p j t", t=T)
        dec = arena[:, 11264:11264 + 1536].rearrange("p (h n) -> p h n", h=4)
        tab = arena[:, 12800:13056].rearrange("p (s c n) -> p s c n", s=2, c=2)
        RT = arena[:, 13056:13056 + 768].rearrange("p (i n) -> p i n", i=2)
        tmp2 = arena[:, 14000:14000 + 2048]
        cat = arena[:, 16384:16384 + 2048].rearrange("p (c n) -> p c n", c=2)
        t_fence = q.all_done()
        t_dec = fetch(dec, a["c_decay"], t_fence)
        t_tab = fetch(tab, a["c_rope2"], t_fence)
        _, t_h = rmsnorm(g_mix0, t_r, q_pe())
        t_P.clear()
        w_e = kview(a["even_w_in_2"][0])

        def sink_P2(c0):
            def go(c, ps, t):
                v = P2[:, c, c0:c0 + 512]
                if c0 == 3072:
                    t = scal(lambda e: e.activation(v, ps, ACT.Silu), t, t_fence)
                else:
                    t = evac(v, ps, t, t_fence)
                t_P[(c0, c)] = t
                return t
            return go
        for j in (0, 1):
            project(w_e, 512 * j, 512, sink_P2(512 * j), t_h)
        filler.extend(project_steps(w_e, 512 * j, 512, sink_P2(512 * j), t_h) for j in (2, 3, 4, 5, 6))

        def need2(c0, c):
            while (c0, c) not in t_P:
                fill()
            return t_P[(c0, c)]

        t_kinds = {}

        def rope_pair(lo):
            for c in range(2):
                v = P2[:, c, lo:lo + 1024].rearrange("p (h n) -> p h n", h=8)
                t_kinds[(lo, c)] = rope(v, tab[:, 0, c, :], tab[:, 1, c, :], 64, tmp2,
                                        need2(lo, c), need2(lo + 512, c), t_tab)

        t_T = {}

        def turn_kinds(kinds):
            for kind in kinds:
                lo = (0, 512, 1536, 2048)[kind]
                t_T[kind] = []
                for c in range(2):
                    t_T[kind] += transposes([(q2[:, 4 * kind:4 * kind + 4, c * P:(c + 1) * P],
                                              [P2[:, c, lo + i * P:lo + (i + 1) * P] for i in range(4)])],
                                            t_kinds[(0 if lo < 1024 else 1536, c)])

        rope_pair(0)
        fill(2)
        turn_kinds((0, 1))
        jobs = []
        for c in range(2):
            ob = bank(hold=True)
            for h in range(4):
                parts = [causal_part(c, q2[:, h, c * P:(c + 1) * P], lambda lo, hi, h=h: q2[:, 4 + h, lo:hi])]
                jobs.append((c, parts, 128 ** -0.5, [P2[:, kc, 1024 + P * h:1024 + P * (h + 1)] for kc in range(c + 1)],
                             ob, P * h, P, 8 * c + h, [t_T[0], t_T[1], need2(1024, 0), need2(1024, 1)]))
        t_cat = []
        for c, ob, t in attend(jobs, lambda n: 1):
            t_cat.append(normalise(c, ob, cat[:, c, 0:512], 4, 128, t))
            if c == 0:
                rope_pair(1536)
        turn_kinds((2, 3))
        while filler:
            fill()
        rt_free = [None, None]
        ob0, ob1 = bank(hold=True), bank(hold=True)
        for h in range(4):
            i = h % 2
            b = bank()

            def go(e, h=h, b=b):
                e.matmul(banks[:, b, 0:256], q2[:, 12 + h, 0:P], q2[:, 8 + h, :], start=True, stop=True)
                return e.matmul(banks[:, b, 256:384], q2[:, 12 + h, P:T], q2[:, 8 + h, P:T], start=True, stop=True)
            t = put("pe", go, t_T[2], t_T[3], bank_free[b])
            t = vec(lambda e, h=h, b=b, i=i: e.tensor_tensor(RT[:, i, :], banks[:, b, 0:384], dec[:, h, :],
                                                                    ALU.mult), t, t_dec, rt_free[i])
            bank_free[b] = t

            def go(e, h=h, i=i):
                v0 = P2[:, 0, 2560 + P * h:2560 + P * (h + 1)]
                v1 = P2[:, 1, 2560 + P * h:2560 + P * (h + 1)]
                cs_ = slice(P * h, P * (h + 1))
                e.matmul(banks[:, ob0, cs_], RT[:, i, 0:P], v0, start=True, stop=True)
                e.matmul(banks[:, ob1, cs_], RT[:, i, P:T], v0, start=True, stop=False)
                return e.matmul(banks[:, ob1, cs_], RT[:, i, T:384], v1, start=False, stop=True)
            t = put("pe", go, t, t_P[(2560, 0)], t_P[(2560, 1)],
                    [bank_free[ob0], bank_free[ob1]] if h == 0 else None)
            rt_free[i] = t
        for c, ob in ((0, ob0), (1, ob1)):
            cv = cat[:, c, 512:1024]
            cv3 = cv.rearrange("p (h n) -> p h n", h=4)
            sq = tmp2[:, 0:512].rearrange("p (h n) -> p h n", h=4)
            ss = ssq[:, 0, 0:4]
            t = vec(lambda e, cv=cv, ob=ob: e.tensor_copy(cv, banks[:, ob, :]), t)
            bank_free[ob] = t
            held.discard(ob)
            t = vec(lambda e, cv3=cv3: e.tensor_tensor(sq, cv3, cv3, ALU.mult), t)
            t = vec(lambda e: e.tensor_reduce(ss, sq, X, ALU.add), t)
            t = rsqrt(ss, ss, 128, t)
            t = vec(lambda e, cv3=cv3: e.tensor_tensor(
                cv3, cv3, ss.unsqueeze(2).to_broadcast([P, 4, P]), ALU.mult), t)
            t = vec(lambda e, cv=cv, c=c: e.tensor_tensor(cv, cv, P2[:, c, 3072:3584], ALU.mult),
                    t, t_P[(3072, c)])
            t_cat.append(t)
        t_f = q_pe()
        t_hT = []
        for c in range(2):
            t_hT += transposes([(hT[:, k:k + 4, c * P:(c + 1) * P],
                                 [cat[:, c, (k + i) * P:(k + i + 1) * P] for i in range(4)])
                                for k in (0, 4)], t_cat, t_f)
        t_r2 = []
        for c0 in (0, 512):
            project(kview(a["even_w_out_2"][0]), c0, 512, residual_sink(t_r2, c0), t_hT)
        t_r = t_r2

        iota16 = sm(16)
        t_i16 = put("pool", lambda e: e.iota(iota16, [[1, 16]], base=0, channel_multiplier=0,
                                             allow_small_or_imprecise_dtypes=True))
        g_sems = [sem(f"s_g{i}") for i in range(NG)]
        rows_free = [None] * NG
        rows_n = [0]
        tops = sm(2, 128)
        hid = sm(2, 128)
        top3 = tops.rearrange("p c (h k) -> p c h k", h=8)
        hid3 = hid.rearrange("p c (h k) -> p c h k", h=8)
        gz = sm(4)

        def peer(layer, g, t_r):
            t_fence = q.all_done()
            at = [0]

            def take(n):
                v = arena[:, at[0]:at[0] + n]
                at[0] += n
                assert at[0] <= AR
                return v
            rows = take(NG * D).rearrange("p (i d) -> p i d", i=NG)
            qp = [take(512) for _ in range(2)]
            sc = [take(512).rearrange("p (j n) -> p j n", j=4) for _ in range(2)]
            cand = take(512).rearrange("p (c n) -> p c n", c=2)
            eq = take(512)
            diag = take(512).rearrange("p (i n) -> p i n", i=4)
            vals = take(64).rearrange("p (j n) -> p j n", j=4)
            ti = take(64)
            iu = take(64).bitcast(U32)
            pu = take(96).bitcast(U32)
            eix = take(256).bitcast(U32).rearrange("p (c n) -> p c n", c=2)
            af = take(32)
            e12 = take(64).rearrange("p (s n) -> p s n", s=2)
            table_u = a["peer_u_2"].rearrange("l e d -> (l e) d")
            table_v = a["peer_v_2"].rearrange("l e d -> (l e) d")
            for i in range(NG):
                rows_free[i] = t_fence
            toks_xn, t_h = rmsnorm(g, t_r, q_pe())
            w = kview(a["peer_w_q_2"][layer])
            kt = take(2048).rearrange("p (j n) -> p j n", j=16)
            t_kt = fetch(kt, a["c_keys"][layer], t_fence)
            qp_free, sc_free = [t_fence, t_fence], [t_fence, t_fence]
            t_sc = {}
            acc = [[bank(hold=True), bank(hold=True)], [bank(hold=True), bank(hold=True)]]

            def score(h):
                s, wt, t_w = load(w[:, :, 256 * h:256 * (h + 1)], 8)
                b = bank()

                def go(e):
                    for f in range(2):
                        for k in range(8):
                            r = e.matmul(banks[:, b, f * T:(f + 1) * T], wt[:, k, f * P:(f + 1) * P], hT[:, k, :],
                                         start=(k == 0), stop=(k == 7))
                    return r
                t = put("pe", go, t_w, t_h, bank_free[b])
                slot_free[s] = t
                qv = qp[h % 2]
                bank_free[b] = t = put("act", lambda e: e.copy(qv, banks[:, b, :]), t, qp_free[h % 2])
                b2 = bank()

                def go2(e):
                    for c in range(2):
                        for f in range(2):
                            r = e.matmul(banks[:, b2, (2 * c + f) * P:(2 * c + f + 1) * P],
                                         qv[:, f * T + c * P:f * T + (c + 1) * P], kt[:, 2 * h + f, :],
                                         start=True, stop=True)
                    return r
                t = put("pe", go2, t, t_kt, bank_free[b2])
                qp_free[h % 2] = t
                bank_free[b2] = t_sc[h] = put("act", lambda e: e.copy(
                    sc[h % 2].rearrange("p j n -> p (j n)"), banks[:, b2, :]), t, sc_free[h % 2])

            t_sel = {}

            def select(h):
                t_cell = [t_sc[h]]

                def step(fn, *after):
                    t_cell[0] = put("dve", fn, t_cell[0], (q.sems["dve"], q.count["dve"]), *after)
                    return t_cell[0]

                def top16(v, vout, iout):
                    step(lambda e: e.max(vout[:, 0:8], v))
                    yield
                    step(lambda e: e.max_index(iout[:, 0:8], vout[:, 0:8], v))
                    yield
                    step(lambda e: e.match_replace(v, vout[:, 0:8], v, -3e38))
                    yield
                    step(lambda e: e.max(vout[:, 8:16], v))
                    yield
                    step(lambda e: e.max_index(iout[:, 8:16], vout[:, 8:16], v))
                    yield

                for j in range(4):
                    yield from top16(sc[h % 2][:, j, :], vals[:, j, :], iu[:, 16 * j:16 * j + 16])
                sc_free[h % 2] = t_cell[0]
                step(lambda e: e.tensor_copy(ti, iu))
                yield
                for c in range(2):
                    step(lambda e, c=c: e.tensor_tensor(
                        cand[:, c, :].rearrange("p (i j) -> p i j", i=16),
                        vals[:, 2 * c, :].unsqueeze(2).to_broadcast([P, 16, 16]),
                        vals[:, 2 * c + 1, :].unsqueeze(1).to_broadcast([P, 16, 16]), ALU.add))
                    yield
                for c in range(2):
                    yield from top16(cand[:, c, :], top3[:, c, h, :], pu[:, 16 * c:16 * c + 16])
                e3 = e12[:, 0, :].rearrange("p (c k) -> p c k", c=2)
                tv = top3[:, :, h, :]
                t_x = step(lambda e: e.tensor_tensor(e3, tv, tv[:, :, 0:1].to_broadcast([P, 2, 16]), ALU.subtract))
                t_x = put("act", lambda e: e.activation(tv, e3, ACT.Exp), t_x)
                yield
                step(lambda e: e.tensor_scalar(pu[:, 32:64], pu[:, 0:32], 4, None, ALU.logical_shift_right))
                yield
                step(lambda e: e.tensor_scalar(pu[:, 64:96], pu[:, 0:32], 15, None, ALU.bitwise_and))
                yield
                for s_, lo in ((0, 32), (1, 64)):
                    step(lambda e, lo=lo: e.tensor_copy(af, pu[:, lo:lo + 32]))
                    yield
                    step(lambda e: e.tensor_tensor(
                        eq.rearrange("p (m j) -> p m j", j=16), iota16.unsqueeze(1).to_broadcast([P, 32, 16]),
                        af.unsqueeze(2).to_broadcast([P, 32, 16]), ALU.is_equal), t_i16)
                    yield
                    step(lambda e, s_=s_: e.tensor_tensor(
                        eq.rearrange("p (c k j) -> p c k j", c=2, k=16), eq.rearrange("p (c k j) -> p c k j", c=2, k=16),
                        ti.rearrange("p (c s j) -> p s c j", c=2, s=2)[:, s_].unsqueeze(2).to_broadcast([P, 2, 16, 16]),
                        ALU.mult))
                    yield
                    step(lambda e, s_=s_: e.tensor_reduce(
                        e12[:, s_, :], eq.rearrange("p (m j) -> p m j", j=16), X, ALU.add), t_x)
                    yield
                step(lambda e: e.scalar_tensor_tensor(e12[:, 0, :], e12[:, 0, :], 128.0, e12[:, 1, :],
                                                      ALU.mult, ALU.add))
                yield
                t_e = step(lambda e: e.tensor_scalar(
                    eix[:, :, 16 * h:16 * h + 16], e12[:, 0, :].rearrange("p (c k) -> p c k", c=2),
                    float(128 * 128 * layer), None, ALU.add))
                yield
                step(lambda e: e.tensor_reduce(gz[:, 0:2], tv, X, ALU.add))
                yield
                step(lambda e: e.reciprocal(gz[:, 2:4], gz[:, 0:2]))
                yield
                t_g = step(lambda e: e.tensor_tensor(tv, tv, gz[:, 2:4].unsqueeze(2).to_broadcast([P, 2, 16]), ALU.mult))
                t_sel[h] = (t_e, t_g)

            def gather(table, h, c, k):
                i = rows_n[0] % NG
                rows_n[0] += 1
                t = dma("pool", lambda e: e.indirect_dma_start(
                    rows[:, i, :], None, table,
                    bass.IndirectOffsetOnAxis(ap=eix[:, c, 16 * h + k:16 * h + k + 1], axis=0)),
                    g_sems[i], rows_free[i], t_sel[h][0])
                return i, t

            def u_step(h, c, k):
                i, t = gather(table_u, h, c, k)
                rows_free[i] = put("dve", lambda e: e.tensor_tensor_reduce(
                    rows[:, i, :], rows[:, i, :], xn[:, c, :], 1.0, 0.0, ALU.mult, ALU.add,
                    hid3[:, c, h, k:k + 1]), t, toks_xn)
                return rows_free[i]

            d_free = [None] * 4
            d_n = [0]
            acc_tok = [t_r, t_r]
            on_pe = {}

            def v_step(h, c, k, t_w):
                i, t = gather(table_v, h, c, k)
                if h == 7 and k % 3 == 2:
                    rows_free[i] = acc_tok[c] = put("dve", lambda e: e.scalar_tensor_tensor(
                        x[:, c, :], rows[:, i, :], hid3[:, c, h, k:k + 1], x[:, c, :], ALU.mult, ALU.add),
                        t, t_w, acc_tok[c])
                    return
                d = d_n[0] % 4
                d_n[0] += 1
                td = put("act", lambda e: e.activation(diag[:, d, :], ident[:, :], ACT.Copy,
                                                       scale=hid3[:, c, h, k:k + 1]), t_w, t_id, d_free[d])
                first, last = c not in on_pe, (h == 7 and k == 15)

                def go(e):
                    for hf in range(2):
                        r = e.matmul(banks[:, acc[c][hf], :], diag[:, d, :], rows[:, i, hf * 512:(hf + 1) * 512],
                                     start=first, stop=last)
                    return r
                d_free[d] = rows_free[i] = on_pe[c] = put(
                    "pe", go, t, td, [bank_free[acc[c][0]], bank_free[acc[c][1]]] if first else None)

            score(0)
            for _ in select(0):
                pass
            score(1)
            t_w = None
            for h in range(9):
                if h + 2 < 8:
                    score(h + 2)
                nxt = select(h + 1) if h + 1 < 8 else iter(())
                for k in range(16):
                    for c in range(2):
                        if h < 8:
                            t_u = u_step(h, c, k)
                        if h > 0:
                            v_step(h - 1, c, k, t_w)
                        for _ in range(2):
                            next(nxt, None)
                for _ in nxt:
                    pass
                if h < 8:
                    hv = hid3[:, :, h, :]
                    t = put("act", lambda e, hv=hv: e.activation(hv, hv, ACT.Gelu), t_u)
                    t_w = put("dve", lambda e, hv=hv, h=h: e.tensor_tensor(hv, hv, top3[:, :, h, :], ALU.mult),
                              t, t_sel[h][1])
            ts = []
            for c in range(2):
                for hf in range(2):
                    v = x[:, c, hf * 512:(hf + 1) * 512]
                    t = vec(lambda e, v=v, b=acc[c][hf]: e.tensor_tensor(v, v, banks[:, b, :], ALU.add),
                            on_pe[c], acc_tok[c])
                    bank_free[acc[c][hf]] = t
                    held.discard(acc[c][hf])
                    ts.append(t)
            return ts

        g = load_gain(a["norm_ffn_2"][0])
        g_mix1 = load_gain(a["norm_mix_2"][1])
        t_r = peer(0, g, t_r)

        t_fence = q.all_done()
        _, t_h = rmsnorm(g_mix1, t_r, q_pe())
        cw = sm(24)
        t_cw = fetch(cw, a["c_conv"])
        bgT = arena[:, 0:2048].rearrange("p (k t) -> p k t", k=8)
        hxT = arena[:, 2048:4096].rearrange("p (k t) -> p k t", k=8)
        uT = arena[:, 4096:4096 + 8 * 258].rearrange("p (k t) -> p k t", k=8)
        yT = arena[:, 6400:6400 + 2048].rearrange("p (k t) -> p k t", k=8)
        cgT = arena[:, 8448:8448 + 2048].rearrange("p (k t) -> p k t", k=8)
        w = kview(a["odd_w_in_2"][0])
        t_z = put("pool", lambda e: e.memset(uT[:, :, 0:2], 0.0), t_fence)
        t_b = {}
        for jj in range(12):
            s, wt, t_w = load(w[:, :, 256 * jj:256 * (jj + 1)], 8)
            b = bank()

            def go(e, wt=wt, b=b):
                for f in range(2):
                    for k in range(8):
                        r = e.matmul(banks[:, b, f * T:(f + 1) * T], wt[:, k, f * P:(f + 1) * P], hT[:, k, :],
                                     start=(k == 0), stop=(k == 7))
                return r
            t = put("pe", go, t_w, t_h, bank_free[b])
            slot_free[s] = t
            kd_, k0 = jj // 4, 2 * (jj % 4)
            dst = (bgT, cgT, hxT)[kd_]
            t = evac(dst[:, k0:k0 + 2, :].rearrange("p j t -> p (j t)"), banks[:, b, :], t, t_fence)
            bank_free[b] = t
            t_b[jj] = t
        t_y = []
        for k in range(8):
            t = vec(lambda e, k=k: e.tensor_tensor(uT[:, k, 2:258], cgT[:, k, :], hxT[:, k, :], ALU.mult),
                    t_b[4 + k // 2], t_b[8 + k // 2], t_z)
            t = vec(lambda e, k=k: e.tensor_scalar(yT[:, k, :], uT[:, k, 0:256], cw[:, k:k + 1], None,
                                                          ALU.mult), t, t_cw)
            for i in (1, 2):
                t = vec(lambda e, k=k, i=i: e.scalar_tensor_tensor(
                    yT[:, k, :], uT[:, k, i:i + 256], cw[:, 8 * i + k:8 * i + k + 1], yT[:, k, :],
                    ALU.mult, ALU.add), t)
            t = vec(lambda e, k=k: e.tensor_tensor(yT[:, k, :], yT[:, k, :], bgT[:, k, :], ALU.mult), t,
                    t_b[k // 2])
            t_y.append(t)
        t_r2 = []
        for c0 in (0, 512):
            project(kview(a["odd_w_out_2"][0]), c0, 512, residual_sink(t_r2, c0), t_y, lhs=yT)
        t_r = t_r2
        g = load_gain(a["norm_ffn_2"][1])
        g_fin = load_gain(a["final_norm_2"])
        t_r = peer(1, g, t_r)
        toks, _ = rmsnorm(g_fin, t_r, q.all_done(), to_T=False)
        return wrap(nc, ctx, q, finish, xn, toks)


def wrap(nc, ctx, q, finish, src, t):
    finish(src[:, :, :], t)
    block = ctx.enter_context(nc.Block())

    @block.sync
    def _(e):
        q.emit("sp", e)

    @block.tensor
    def _(e):
        q.emit("pe", e)

    @block.vector
    def _(e):
        q.emit("dve", e)

    @block.scalar
    def _(e):
        q.emit("act", e)

    @block.gpsimd
    def _(e):
        q.emit("pool", e)


def constants():
    c = {}
    c["c_ident"] = np.eye(P, dtype=np.float32)
    qi = np.arange(T)[:, None]
    ki = np.arange(T)[None, :]
    d = qi - ki
    band = []
    for dil in (1, 4, 16):
        ok = (d >= 0) & (d % dil == 0) & (d <= 128 * dil)
        band.append(np.where(ok, d, 1e30).astype(np.float32))
    c["c_band"] = np.concatenate([b[0:P, 0:P] for b in band] + [b[P:T] for b in band], axis=1)
    cm = np.where(d >= 0, 0.0, NEG).astype(np.float32)
    c["c_causal"] = np.concatenate([cm[0:P, 0:P], cm[P:T]], axis=1)
    f = (np.float32(10000.0) ** (-np.arange(16, dtype=np.float32) / np.float32(16))).astype(np.float32)
    c["c_freq"] = np.repeat(f[None, :], P, axis=0)
    inv = (np.float32(10000.0) ** (-np.arange(64, dtype=np.float32) / np.float32(64))).astype(np.float32)
    ang = (np.arange(T, dtype=np.float32)[:, None] * inv[None, :]).astype(np.float64)
    tab = np.stack([np.cos(ang), np.sin(ang)]).astype(np.float32)
    c["c_tri"] = np.triu(np.ones((P, P), np.float32), 1)
    c["c_rope2"] = np.ascontiguousarray(tab.reshape(2, 2, P, 64).transpose(2, 0, 1, 3))
    dec = []
    for h in range(4):
        lg = np.log(1.0 - 2.0 ** (-5.0 - h))
        m = np.where(d.T <= 0, np.exp(lg * np.abs(d.T)), 0.0) * 0 + np.where(
            (ki - qi) >= 0, np.exp(lg * np.maximum(ki - qi, 0)), 0.0)
        m = (m * 128 ** -0.5).astype(np.float32)
        dec.append(np.concatenate([m[0:P, :], m[P:T, P:T]], axis=1))
    c["c_decay"] = np.ascontiguousarray(np.stack(dec, axis=1))
    return c


_OUTS = [((1, 256, 1024), "float32")]


def kernel(**inputs):
    import concourse.bacc as _bacc
    from concourse.bass_utils import run_bass_kernel_spmd as _run

    nc = _bacc.Bacc("TRN2", target_bir_lowering=False, num_devices=1)
    data = {k: np.ascontiguousarray(v) for k, v in inputs.items() if k != "peer_sub_keys_2"}
    data.update(constants())
    keys = np.asarray(inputs["peer_sub_keys_2"])
    data["c_keys"] = np.ascontiguousarray(keys.transpose(0, 4, 1, 2, 3).reshape(2, P, 16, P))
    data["c_conv"] = np.ascontiguousarray(data.pop("odd_conv_2")[0].reshape(3, 8, P).transpose(2, 0, 1).reshape(P, 24))
    data["c_pos"] = np.ascontiguousarray(data.pop("positions").reshape(2, P).T)
    arrays, args = {}, {}
    for name, v in data.items():
        arrays[f"in_{name}_dram"] = v
        args[name] = nc.dram_tensor(f"in_{name}_dram", v.shape, mybir.dt.from_np(v.dtype),
                                    kind="ExternalInput").ap()
    outs = [nc.dram_tensor(f"out_{i}_dram", shape, mybir.dt.from_np(np.dtype(dt)), kind="ExternalOutput").ap()
            for i, (shape, dt) in enumerate(_OUTS)]
    build(nc, args, outs[0])
    r = _run(nc, [arrays], core_ids=[0])
    return r.results[0]["out_0_dram"]
```

```python
from contextlib import ExitStack

import numpy as np

import concourse.bass as bass
from concourse import mybir

P = 128
F32 = mybir.dt.float32
I32 = mybir.dt.int32
U32 = mybir.dt.uint32
ALU = mybir.AluOpType
ACT = mybir.ActivationFunctionType
X = mybir.AxisListType.X
EPS = 1e-6
NEG = -1e30
T = 256
D = 1024

NSLOT = 6
NG = 20
AR = 29056


class Queues:

    def __init__(self, sems):
        self.sems = sems
        self.count = {e: 0 for e in sems}
        self.items = {e: [] for e in sems}
        self.seen = {e: {} for e in sems}
        self.dma_count = {}

    def waits(self, eng, after):
        need = {}
        stack = list(after)
        while stack:
            a = stack.pop()
            if a is None:
                continue
            if isinstance(a, list):
                stack += a
                continue
            sem, value = a
            if value > self.seen[eng].get(sem.name, 0):
                need[sem.name] = (sem, max(value, need.get(sem.name, (None, 0))[1]))
        for name, (sem, value) in need.items():
            self.seen[eng][name] = value
        return list(need.values())

    def put(self, eng, fn, *after):
        self.count[eng] += 1
        self.items[eng].append((self.waits(eng, after), fn, self.sems[eng], 1))
        return (self.sems[eng], self.count[eng])

    def dma(self, eng, fn, sem, *after):
        self.dma_count[sem.name] = self.dma_count.get(sem.name, 0) + 16
        self.items[eng].append((self.waits(eng, after), fn, sem, 16))
        return (sem, self.dma_count[sem.name])

    def wait(self, eng, *after):
        self.items[eng].append((self.waits(eng, after), None, None, 0))

    def step(self, eng, fn, *after):
        self.items[eng].append((self.waits(eng, after), fn, None, 0))

    def begin_if(self, number, *after):
        self.before = dict(self.count), dict(self.dma_count), {e: dict(s) for e, s in self.seen.items()}
        self.inside = {e: len(self.items[e]) for e in self.items}
        for e in self.items:
            self.items[e].append(("if", self.waits(e, after), number))
            self.before[2][e] = dict(self.seen[e])

    def end_if(self, inner):
        count, dma_count, seen = self.before
        for e in self.items:
            adds = {}
            for it in self.items[e][self.inside[e] + 1:]:
                if it[2] is not None and it[2].name not in inner:
                    s, n = adds.get(it[2].name, (it[2], 0))
                    adds[it[2].name] = (s, n + it[3])
            own = self.sems[e].name if e in self.sems else None
            self.items[e].append(("else", [(s, count[e] if name == own else dma_count.get(name, 0), n)
                                           for name, (s, n) in adds.items()]))
            self.seen[e] = seen[e]

    def all_done(self):
        return [(self.sems[e], self.count[e]) for e in self.sems if self.count[e]]

    def emit(self, name, eng):
        items = self.items[name]
        n = 0
        while n < len(items):
            if items[n][0] != "if":
                self.issue(eng, items[n])
                n += 1
                continue
            _, waits, number = items[n]
            for s, v in waits:
                eng.wait_ge(s, v)
            some = eng.value_load(number, min_val=0, max_val=3)
            n += 1
            with eng.If(some > 0):
                while items[n][0] != "else":
                    self.issue(eng, items[n])
                    n += 1
            with eng.Else():
                for s, before, add in items[n][1]:
                    if before:
                        eng.wait_ge(s, before)
                    eng.sem_inc(s, add)
            n += 1

    def issue(self, eng, item):
        waits, fn, sem, n = item
        for s, v in waits:
            eng.wait_ge(s, v)
        if sem is not None:
            fn(eng).then_inc(sem, n)
        elif fn is not None:
            fn(eng)


def build(nc, a, out):
    ctx = ExitStack()
    with ctx:
        def sb(name, shape, dt=F32):
            return ctx.enter_context(nc.sbuf_tensor(name, shape, dt))

        def sem(name):
            return ctx.enter_context(nc.semaphore(name))

        q = Queues({e: sem("s_" + e) for e in ("pe", "dve", "act", "pool")})
        put, dma = q.put, q.dma

        def vec(fn, *after):
            return put("dve", fn, (q.sems["dve"], q.count["dve"]), *after)

        def scal(fn, *after):
            return put("act", fn, (q.sems["act"], q.count["act"]), *after)

        x = sb("x", [P, 2, D])
        xn = sb("xn", [P, 2, D])
        hT = sb("hT", [P, 8, T])
        ring = sb("ring", [P, NSLOT, 2048])
        ident = sb("ident", [P, P])
        gain = sb("gain", [P, 2, D])
        small = sb("small", [P, 2560])
        arena = sb("arena", [P, AR])
        banks = ctx.enter_context(nc.psum_tensor("banks", [P, 8, 512], F32))

        bank_free = [None] * 8
        bank_next = [0]

        held = set()

        def bank(hold=False):
            while bank_next[0] % 8 in held:
                bank_next[0] += 1
            b = bank_next[0] % 8
            bank_next[0] += 1
            if hold:
                held.add(b)
            return b

        def dve_now():
            return (q.sems["dve"], q.count["dve"])

        def act_now():
            return (q.sems["act"], q.count["act"])

        slot_free = [None] * NSLOT
        slot_sem = [sem(f"s_slot{i}") for i in range(NSLOT)]
        slot_next = [0]

        load_wait = [[]]

        def load(src, n):
            if load_wait[0]:
                left, after = load_wait[0][0]
                if left == 0:
                    q.wait("sp", after)
                    load_wait[0].pop(0)
                else:
                    load_wait[0][0] = (left - 1, after)
            s = slot_next[0] % NSLOT
            slot_next[0] += 1
            dst = ring[:, s, 0:n * src.shape[2]].rearrange("p (k c) -> p k c", k=n)
            tok = dma("sp", lambda e: e.dma_start(dst, src), slot_sem[s], slot_free[s])
            return s, dst, tok

        q.items["sp"], q.seen["sp"] = [], {}

        const_sem = [0]

        def fetch(dst, src, *after, eng="act"):
            const_sem[0] += 1
            return dma(eng, lambda e: e.dma_start(dst, src), sem(f"s_c{const_sem[0]}"), *after)

        def row(ap, n):
            return ap.unsqueeze(0).to_broadcast([P, n])

        smallp = [0]

        def sm(*shape):
            n = int(np.prod(shape))
            if smallp[0] + n > 2560:
                raise ValueError("small")
            v = small[:, smallp[0]:smallp[0] + n]
            smallp[0] += n
            if len(shape) == 2:
                v = v.rearrange("p (a b) -> p a b", a=shape[0])
            if len(shape) == 3:
                v = v.rearrange("p (a b c) -> p a b c", a=shape[0], b=shape[1])
            return v

        mhalf = sm(64)
        t_mh = put("pool", lambda e: e.memset(mhalf, -0.5))
        t_id = fetch(ident[:, :], a["c_ident"], eng="sp")

        def rsqrt(dst, ss, n, *after):
            m = dst.shape[1]
            t = vec(lambda e: e.tensor_scalar(dst, ss, 1.0 / n, EPS, ALU.mult, ALU.add), *after)
            return put("pool", lambda e: e.tensor_tensor(dst, dst, mhalf[:, 0:m], ALU.pow), t, t_mh)

        def q_pe():
            return (q.sems["pe"], q.count["pe"])

        evac_turn = [0]

        def copy(eng, dst, src, *after):
            if eng == "act":
                return put("act", lambda e: e.copy(dst, src), *after)
            return put("dve", lambda e: e.tensor_copy(dst, src), *after)

        def evac(dst, src, *after):
            evac_turn[0] ^= 1
            return copy("act" if evac_turn[0] else "dve", dst, src, *after)

        def transposes(pairs, *after, eng=None):
            toks = []
            for dst, srcs in pairs:
                m = srcs[0].shape[1]
                b = bank()

                def go(e, b=b, srcs=srcs, m=m):
                    for i, s in enumerate(srcs):
                        r = e.transpose(banks[0:m, b, i * P:(i + 1) * P], s, ident[:, :])
                    return r
                t = put("pe", go, list(after), t_id, bank_free[b])
                n = len(srcs)
                src = banks[0:m, b, 0:n * P].rearrange("p (k c) -> p k c", k=n)
                t = copy(eng, dst, src, t) if eng else evac(dst, src, t)
                bank_free[b] = t
                toks.append(t)
            return toks

        gain_free = [None, None]
        gain_n = [0]

        def load_gain(src):
            g = gain_n[0] % 2
            gain_n[0] += 1
            return g, fetch(gain[:, g, :], row(src, D), gain_free[g])

        def norm_chunk(c, g, ss, t_x, t_free):
            gi, t_g = g
            t = scal(lambda e: e.activation(xn[:, c, :], x[:, c, :], ACT.Square, accum_out=ss[:, c:c + 1]),
                     t_x, t_free)
            t = rsqrt(ss[:, c:c + 1], ss[:, c:c + 1], D, t)
            gain_free[gi] = t = vec(lambda e: e.scalar_tensor_tensor(
                xn[:, c, :], x[:, c, :], ss[:, c:c + 1], gain[:, gi, :], ALU.mult, ALU.mult), t, t_g)
            return t

        def turn_chunk(c, t):
            return transposes([(hT[:, k:k + 4, c * P:(c + 1) * P],
                                [xn[:, c, (k + i) * P:(k + i + 1) * P] for i in range(4)])
                               for k in (0, 4)], t)

        def rmsnorm(g, t_x, t_free, to_T=True):
            ss = sm(2)
            toks = [norm_chunk(c, g, ss, t_x[c], t_free) for c in range(2)]
            return toks, [turn_chunk(c, toks[c]) for c in range(2)] if to_T else None

        def residual_norm(w, lhs, t_lhs, g, mid=None):
            slots_ = []
            for c0 in (0, 512):
                for k in (0, 4):
                    slots_.append((c0, k, *load(w[:, k:k + 4, c0:c0 + 512], 4)))
            ss = sm(2)
            t_free = q_pe()
            t_x, t_n, t_t = [[], []], [None, None], [None, None]

            def product(c, c0):
                b = bank()
                for c0_, k, s, wt, t_w in slots_:
                    if c0_ != c0:
                        continue

                    def go(e, k=k, wt=wt):
                        for i in range(4):
                            r = e.matmul(banks[:, b, :], lhs[:, k + i, c * P:(c + 1) * P], wt[:, i, :],
                                         start=(k + i == 0), stop=(k + i == 7))
                        return r
                    t = slot_free[s] = put("pe", go, t_w, t_lhs[c], bank_free[b] if k == 0 else None)

                def add():
                    v = x[:, c, c0:c0 + 512]
                    bank_free[b] = t_ = vec(lambda e: e.tensor_tensor(v, v, banks[:, b, :], ALU.add), t)
                    t_x[c].append(t_)
                    held.discard(b)
                held.add(b)
                return add
            product(0, 0)()
            product(0, 512)()
            t_n[0] = norm_chunk(0, g, ss, t_x[0], t_free)
            product(1, 0)()
            t_t[0] = turn_chunk(0, t_n[0])
            if mid:
                mid[0](t_t[0])
            add = product(1, 512)
            if mid:
                mid[1](t_x[0], t_n[0])
            add()
            t_n[1] = norm_chunk(1, g, ss, t_x[1], t_free)
            t_t[1] = turn_chunk(1, t_n[1])
            return t_x, t_n, t_t

        def project_steps(w, c0, n, sink, t_h, lhs=None, kn=8):
            lhs = hT if lhs is None else lhs
            per = max(1, 2048 // n)
            b = [bank(hold=True), bank(hold=True)]
            k = 0
            while k < kn:
                m = min(per, kn - k, 4 if n == 512 else 8)
                s, wt, t_w = load(w[:, k:k + m, c0:c0 + n], m)
                for c in range(2):
                    def go(e, c=c, k=k, m=m, wt=wt):
                        for i in range(m):
                            r = e.matmul(banks[:, b[c], 0:n], lhs[:, k + i, c * P:(c + 1) * P], wt[:, i, :],
                                         start=(k + i == 0), stop=(k + i == kn - 1))
                        return r
                    t = put("pe", go, t_w, t_h, bank_free[b[c]] if k == 0 else None)
                    if k + m == kn:
                        bank_free[b[c]] = sink(c, banks[:, b[c], 0:n], t)
                        held.discard(b[c])
                slot_free[s] = t
                k += m
                yield

        def project(*args, **kw):
            for _ in project_steps(*args, **kw):
                pass

        filler = []

        def fill(n=1):
            for _ in range(n):
                while filler:
                    if next(filler[0], 0) != 0:
                        break
                    filler.pop(0)
                else:
                    return

        def kview(w):
            return w.rearrange("(k p) n -> p k n", p=P)

        t_x = fetch(x[:, :, :], a["x"][0].rearrange("(c p) d -> p c d", p=P), eng="sp")

        def finish(src, t):
            t_o = fetch(out[0].rearrange("(c p) d -> p c d", p=P), src, t, eng="sp")
            q.wait("sp", t_o)

        Pj = arena[:, 0:2 * 7712].rearrange("p (c n) -> p c n", c=2)
        off = 2 * 7712
        qd = arena[:, off:off + 3072].rearrange("p (j t) -> p j t", t=T)
        kd = arena[:, off + 3072:off + 6144].rearrange("p (j t) -> p j t", t=T)
        off += 6144
        Bm = arena[:, off:off + 3 * 128 + 3 * 256]
        off += 1152
        cm = arena[:, off:off + 384]
        off += 384
        E = arena[:, off:off + 3 * 768].rearrange("p (i n) -> p i n", i=3)
        off += 2304
        PT = arena[:, off:off + 2 * 768].rearrange("p (i n) -> p i n", i=2)
        off += 1536
        O = xn[:, 0, :].rearrange("p (c n) -> p c n", c=2)
        OT = xn[:, 1, :].rearrange("p (k t) -> p k t", k=4)
        kv_all = arena[:, off:off + 2048]
        off += 2048
        assert off <= AR, off
        vecs = sb("vecs", [P, 848])

        g_attn = load_gain(a["norm_attn"][0])
        _, t_h = rmsnorm(g_attn, [t_x, t_x], None)
        t_B = fetch(Bm, a["c_band"], t_x, eng="pool")
        t_cm = fetch(cm, a["c_causal"], t_x, eng="pool")
        nckv = vecs[:, 0:256]
        t_v = [fetch(nckv, row(a["norm_ckv"][0], 256), t_x, eng="pool"),
               fetch(vecs[:, 256:352], row(a["q_norm_mla"][0], 96), t_x, eng="pool"),
               fetch(vecs[:, 352:448], row(a["k_norm_mla"][0], 96), t_x, eng="pool"),
               fetch(vecs[:, 448:640], row(a["q_norm_dil"].rearrange("l g d -> (l g d)"), 192)),
               fetch(vecs[:, 640:832], row(a["k_norm_dil"].rearrange("l g d -> (l g d)"), 192)),
               fetch(vecs[:, 832:848], a["c_freq"], t_x, eng="pool")]
        rb = sm(36)
        rw = sm(8, 36)
        t_v += [fetch(rb[:, 0:4], row(a["b_router_group"][0], 4), t_x, eng="pool"),
                fetch(rb[:, 4:36], row(a["b_router_expert"][0], 32), t_x, eng="pool"),
                fetch(rw[:, :, 0:4], kview(a["w_router_group"][0]), t_x, eng="pool"),
                fetch(rw[:, :, 4:36], kview(a["w_router_expert"][0]), t_x, eng="pool")]
        pos_i = sb("pos_i", [P, 2], I32)
        t_pos = fetch(pos_i[:, :], a["c_pos"], t_x, eng="pool")

        g_ffn = load_gain(a["norm_ffn"][0])

        NONE = 4095.0
        iota32, ids, iota128, ones, tri, tri32 = sm(36), sm(4), sm(P), sm(P), sm(P), sm(32)
        t_tri = fetch(tri, a["c_tri"], t_x, eng="pool")
        t_tri32 = fetch(tri32[0:32, :], a["c_tri"][0:32, 0:32], t_x, eng="pool")
        t_one = put("pool", lambda e: e.memset(ones, 1.0))
        put("pool", lambda e: e.iota(iota32, [[1, 36]], base=0, channel_multiplier=0,
                                     allow_small_or_imprecise_dtypes=True))
        put("pool", lambda e: e.iota(iota128, [[1, P]], base=0, channel_multiplier=0,
                                     allow_small_or_imprecise_dtypes=True))
        t = t_io = put("pool", lambda e: e.iota(ids.rearrange("p (c k) -> p c k", c=2), [[2 * P, 2], [1, 2]], base=0,
                                                channel_multiplier=2, allow_small_or_imprecise_dtypes=True))
        t_ids = put("pool", lambda e: e.tensor_scalar(ids, ids, -NONE, None, ALU.add), t)

        posf = sm(2)
        ang = sm(2, 16)
        kk = sm(2, 16)
        sn = sm(2, 16)
        cs = sm(2, 16)
        MAGIC = 12582912.0
        C1, C2, C3 = 6.28125, 0.0019350051879882812, 3.0199157663448e-7
        t = vec(lambda e: e.tensor_copy(posf, pos_i[:, :]), t_pos)
        for c in range(2):
            t = vec(lambda e, c=c: e.tensor_scalar(ang[:, c, :], vecs[:, 832:848], posf[:, c:c + 1],
                                                          None, ALU.mult), t, t_v[5])
        t = vec(lambda e: e.tensor_scalar(kk, ang, float(1 / (2 * np.pi)), None, ALU.mult), t)
        t = vec(lambda e: e.tensor_scalar(kk, kk, MAGIC, None, ALU.add), t)
        t = vec(lambda e: e.tensor_scalar(kk, kk, MAGIC, None, ALU.subtract), t)
        for cc in (C1, C2, C3):
            t = vec(lambda e, cc=cc: e.scalar_tensor_tensor(ang, kk, -cc, ang, ALU.mult, ALU.add), t)
        t = vec(lambda e: e.tensor_scalar(ang, ang, float(np.float32(3.1415925)), float(np.float32(-3.1415925)), ALU.min, ALU.max), t)
        t1 = scal(lambda e: e.activation(sn, ang, ACT.Sin), t)
        t2 = scal(lambda e: e.activation(cs, ang, ACT.Sin, scale=0.5), t)
        t = vec(lambda e: e.tensor_tensor(cs, cs, cs, ALU.mult), t1, t2)
        t_rope = vec(lambda e: e.tensor_scalar(cs, cs, -2.0, 1.0, ALU.mult, ALU.add), t)

        w_in = kview(a["w_in"][0])
        t_P = {}

        def sink_P(c0, n):
            def go(c, ps, t):
                t = evac(Pj[:, c, c0:c0 + n], ps, t)
                t_P[(c0, c)] = t
                return t
            return go

        def pt(lo, hi):
            return [t for (c0, c), t in t_P.items() if lo <= c0 < hi]

        for c0, n in ((512, 512), (1024, 32), (0, 512)):
            project(w_in, c0, n, sink_P(c0, n), t_h)

        def sink_act(c0):
            def go(c, ps, t):
                t_P[(c0, c)] = t = copy("act", Pj[:, c, c0:c0 + 512], ps, t)
                return t
            return go

        b_gate = a["b_gate"].rearrange("l g d -> (l g d)")

        def gate_steps(c0):
            lo = c0 - 5664
            s, bt, t_bias = load(b_gate[lo:lo + 512].unsqueeze(0).unsqueeze(0).to_broadcast([P, 1, 512]), 1)

            def go(c, ps, t):
                v = Pj[:, c, c0:c0 + 512]
                t = put("dve", lambda e: e.tensor_tensor(v, ps, bt[:, 0, :], ALU.add), t, t_bias)
                t_P[(c0, c)] = slot_free[s] = t
                return t
            yield from project_steps(w_in, c0, 512, go, t_h)

        filler.extend(project_steps(w_in, 1056 + 512 * j, 512, sink_act(1056 + 512 * j), t_h)
                      for j in (0, 3, 6, 1, 4, 7, 2, 5, 8))
        filler.extend(gate_steps(5664 + 512 * j) for j in range(4))

        def need(lo, hi):
            want = [(c0, c) for c0 in range(1056, 7712, 512) if lo <= c0 < hi for c in range(2)]
            while any(w_ not in t_P for w_ in want):
                fill()
            return [t_P[w_] for w_ in want]

        scratch = gain[:, 0, :]
        s_free = [gain_free[0]]
        ssq = sm(2, 24)
        ss_n = [0]

        def headnorm(v, g, n, *after):
            h = v.shape[1]
            sq = scratch[:, 0:h * n].rearrange("p (h n) -> p h n", h=h)
            ss = ssq[:, ss_n[0] % 2, 0:h]
            ss_n[0] += 1
            t = scal(lambda e: e.activation(sq, v, ACT.Square), s_free[0], *after)
            s_free[0] = t = vec(lambda e: e.tensor_reduce(ss, sq, X, ALU.add), t)
            t = rsqrt(ss, ss, n, t)
            t = vec(lambda e: e.tensor_tensor(v, v, ss.unsqueeze(2).to_broadcast([P, h, n]), ALU.mult), t)
            return vec(lambda e: e.tensor_tensor(v, v, g, ALU.mult), t)

        def rope(v, c_, s_, half, tmp, *after):
            h = v.shape[1]
            a1, a2 = v[:, :, 0:half], v[:, :, half:2 * half]
            cb = c_.unsqueeze(1).to_broadcast([P, h, half])
            sb_ = s_.unsqueeze(1).to_broadcast([P, h, half])
            u = [tmp[:, i * h * half:(i + 1) * h * half].rearrange("p (h n) -> p h n", h=h) for i in range(4)]
            t = [dve_now(), *after]
            put("dve", lambda e: e.tensor_tensor(u[0], a1, cb, ALU.mult), t)
            put("dve", lambda e: e.tensor_tensor(u[1], a2, sb_, ALU.mult), t)
            put("dve", lambda e: e.tensor_tensor(u[2], a2, cb, ALU.mult), t)
            t = put("dve", lambda e: e.tensor_tensor(u[3], a1, sb_, ALU.mult), t)
            put("dve", lambda e: e.tensor_tensor(a1, u[0], u[1], ALU.subtract), t)
            return put("dve", lambda e: e.tensor_tensor(a2, u[2], u[3], ALU.add), t)

        xflat = xn[:, :, :].rearrange("p c n -> p (c n)")
        K = xflat[:, 0:1536].rearrange("p (c h n) -> p c h n", c=2, h=8)
        ckT = xflat[:, 1536:2048].rearrange("p (k t) -> p k t", k=2)
        t_mla = [t_P[(c0, c)] for c0 in (0, 512, 1024) for c in range(2)]
        t_ckv = [t_P[(512, c)] for c in range(2)]
        ssc = sm(2)
        t_x0 = q_pe()
        for c in range(2):
            v = Pj[:, c, 768:1024]
            t = scal(lambda e, v=v, c=c: e.activation(xn[:, c, 0:256], v, ACT.Square,
                                                      accum_out=ssc[:, c:c + 1]), t_ckv, t_x0)
        t = rsqrt(ssc, ssc, 256, t)
        for c in range(2):
            v = Pj[:, c, 768:1024]
            t = vec(lambda e, v=v, c=c: e.scalar_tensor_tensor(
                v, v, ssc[:, c:c + 1], nckv, ALU.mult, ALU.mult), t, t_v[0])
        fill(1)
        t_ck = []
        for c in range(2):
            t_ck += transposes([(ckT[:, :, c * P:(c + 1) * P],
                                 [Pj[:, c, 768 + i * P:768 + (i + 1) * P] for i in range(2)])], t, eng="act")
        t_q, t_k = [], []
        for c in range(2):
            qv = Pj[:, c, 0:768].rearrange("p (h n) -> p h n", h=8)
            t = headnorm(qv, vecs[:, 256:352].unsqueeze(1).to_broadcast([P, 8, 96]), 96, t_mla, t_v[1])
            t_q.append(rope(qv[:, :, 64:96], cs[:, c, :], sn[:, c, :], 16, scratch, t, t_rope))
            s_free[0] = dve_now()
        fill(1)
        kv = kv_all.rearrange("p (c n) -> p c n", c=2)
        t_kv = []

        def kv_sink(c0):
            def go(c, ps, t):
                t = copy("act", kv[:, c, c0:c0 + 512], ps, t)
                t_kv.append(t)
                return t
            return go

        wu = a["w_ukv"][0].rearrange("(k p) n -> p k n", p=P)
        for c0 in (0, 512):
            project(wu, c0, 512, kv_sink(c0), t_ck, lhs=ckT, kn=2)
        kv4 = kv_all.rearrange("p (c h n) -> p c h n", c=2, h=8)
        for c in range(2):
            t = vec(lambda e, c=c: e.tensor_copy(K[:, c, :, 0:64], kv4[:, c, :, 0:64]), t_kv)
            t = vec(lambda e, c=c: e.tensor_copy(
                K[:, c, :, 64:96], Pj[:, c, 1024:1056].unsqueeze(1).to_broadcast([P, 8, 32])), t_mla)
            t = headnorm(K[:, c, :, :], vecs[:, 352:448].unsqueeze(1).to_broadcast([P, 8, 96]), 96, t, t_v[2])
            t_k.append(rope(K[:, c, :, 64:96], cs[:, c, :], sn[:, c, :], 16, scratch, t, t_rope))
            s_free[0] = dve_now()
        qT = qd[0:96, 0:8, :]
        kT = kd[0:96, 0:8, :]
        fill(2)
        t_T = []
        for c in range(2):
            for hh in (0, 4):
                t_T += transposes([(qT[:, hh:hh + 4, c * P:(c + 1) * P],
                                    [Pj[:, c, 96 * h:96 * h + 96] for h in range(hh, hh + 4)])], t_q[c], eng="act")
        fill(1)
        for c in range(2):
            for hh in (0, 4):
                t_T += transposes([(kT[:, hh:hh + 4, c * P:(c + 1) * P],
                                    [K[:, c, h, :] for h in range(hh, hh + 4)])], t_k[c], eng="act")
            fill(1)

        e_free = [None] * 3
        pt_free = [None] * 2
        mx = sm(3, 2)
        den = sm(16)
        den_free = [None, None]
        rden = sm(8)

        def attend(jobs, fills):
            state = {}

            def scores(n):
                c, parts, scale, vs, ob, oc, dh, dcol, after = jobs[n]
                i = n % 3
                groups, at, col = [], 512, 0
                for p in parts:
                    if at + p[2] > 512:
                        groups.append((bank(), []))
                        at = 0
                    groups[-1][1].append((at, p, col))
                    at += p[2]
                    col += p[2]
                for b, ps in groups:
                    def go(e, b=b, ps=ps):
                        for at, p, _ in ps:
                            r = e.matmul(banks[:, b, at:at + p[2]], p[0], p[1], start=True, stop=True)
                        return r
                    t = put("pe", go, after, bank_free[b])
                    for at, p, col in ps:
                        t2 = put("dve", lambda e, b=b, at=at, p=p, col=col: e.scalar_tensor_tensor(
                            E[:, i, col:col + p[2]], p[3], p[4], banks[:, b, at:at + p[2]], ALU.mult, ALU.add),
                            t, e_free[i], t_B, t_cm)
                    bank_free[b] = t2
                wide = sum(p[2] for p in parts)
                ev = E[:, i, 0:wide]
                t = put("dve", lambda e: e.tensor_reduce(mx[:, i, 0:1], ev, X, ALU.max), t2)
                t = put("dve", lambda e: e.tensor_scalar(mx[:, i, 1:2], mx[:, i, 0:1], -scale, None, ALU.mult), t)
                t = put("act", lambda e: e.activation(ev, ev, ACT.Exp, bias=mx[:, i, 1:2], scale=scale,
                                                      accum_out=den[:, dcol:dcol + 1]), t, den_free[c])
                state[n] = t, wide // P

            def turn(n):
                t, m = state[n]
                i, o = n % 3, n % 2
                tp = []
                for j in range(0, m, 4):
                    w_ = min(4, m - j)
                    tp += transposes([(PT[:, o, j * P:(j + w_) * P].rearrange("p (k c) -> p k c", k=w_),
                                       [E[:, i, (j + r) * P:(j + r + 1) * P] for r in range(w_)])], t, pt_free[o],
                                     eng="act")
                e_free[i] = q_pe()
                state[n] = tp, m, t

            def values(n):
                c, parts, scale, vs, ob, oc, dh, dcol, after = jobs[n]
                tp, m, t_exp = state.pop(n)
                o = n % 2

                def pv(e):
                    for j in range(m):
                        r = e.matmul(banks[:, ob, oc:oc + dh], PT[:, o, j * P:(j + 1) * P], vs[j],
                                     start=(j == 0), stop=(j == m - 1))
                    return r
                pt_free[o] = t = put("pe", pv, tp, bank_free[ob] if oc == 0 else None)
                done[n] = [t, t_exp]

            done = {}
            for n in range(len(jobs) + 2):
                if n < len(jobs):
                    scores(n)
                fill(fills(n))
                if 1 <= n <= len(jobs):
                    turn(n - 1)
                if n >= 2:
                    values(n - 2)
                    c, ob = jobs[n - 2][0], jobs[n - 2][4]
                    if n == len(jobs) + 1 or jobs[n - 1][0] != c:
                        yield c, ob, done[n - 2]

        def normalise(c, ob, dst, h, dh, t):
            dv = den[:, 8 * c:8 * c + h]
            den_free[c] = vec(lambda e: e.reciprocal(rden[:, 0:h], dv), t)
            t = vec(lambda e: e.tensor_tensor(
                dst.rearrange("p (h n) -> p h n", h=h),
                banks[:, ob, 0:h * dh].rearrange("p (h n) -> p h n", h=h),
                rden[:, 0:h].unsqueeze(2).to_broadcast([P, h, dh]), ALU.mult), t)
            bank_free[ob] = t
            held.discard(ob)
            return t

        def causal_part(c, lhsT, rhs_of):
            return (lhsT, rhs_of(0, (c + 1) * P), (c + 1) * P, cm[:, 0:P] if c == 0 else cm[:, P:384], 1.0)

        jobs = []
        for c in range(2):
            ob = bank(hold=True)
            for h in range(8):
                parts = [causal_part(c, qT[:, h, c * P:(c + 1) * P], lambda lo, hi, h=h: kT[:, h, lo:hi])]
                jobs.append((c, parts, 96 ** -0.5, [kv4[:, kc, h, 64:128] for kc in range(c + 1)],
                             ob, 64 * h, 64, 8 * c + h, t_T))
        t_o = []
        for c, ob, t in attend(jobs, lambda n: 1 if n < 10 or n in (11, 13, 15) else 0):
            t_o.append(normalise(c, ob, O[:, c, :], 8, 64, t))

        t_d = {}
        t_qfree = q_pe()
        t_OT = []
        for g in range(3):
            for w, go_ in ((0, 448), (1, 640)):
                need(1056 + 1536 * w + 512 * g, 1056 + 1536 * w + 512 * g + 1)
        ssd = sm(96)
        t_rs = []
        todo = []
        s_half = [s_free[0], s_free[0]]
        for g in range(3):
            for c in range(2):
                for w, go_ in ((0, 448), (1, 640)):
                    lo = 1056 + 1536 * w + 512 * g
                    v = Pj[:, c, lo:lo + 512].rearrange("p (h n) -> p h n", h=8)
                    i = len(todo)
                    sq = scratch[:, 512 * (i % 2):512 * (i % 2) + 512].rearrange("p (h n) -> p h n", h=8)
                    t = scal(lambda e, v=v, sq=sq: e.activation(sq, v, ACT.Square), s_half[i % 2], need(lo, lo + 1))
                    s_half[i % 2] = t = put("dve", lambda e, sq=sq, i=i: e.tensor_reduce(
                        ssd[:, 8 * i:8 * i + 8], sq, X, ALU.add), t)
                    todo.append((v, go_, w, c, g))
            t_rs.append(rsqrt(ssd[:, 32 * g:32 * g + 32], ssd[:, 32 * g:32 * g + 32], 64, t))
        for i, (v, go_, w, c, g) in enumerate(todo):
            t = t_rs[g]
            r = ssd[:, 8 * i:8 * i + 8].unsqueeze(2).to_broadcast([P, 8, 64])
            gv = vecs[:, go_ + 64 * g:go_ + 64 * g + 64].unsqueeze(1).to_broadcast([P, 8, 64])
            t = vec(lambda e, v=v, r=r: e.tensor_tensor(v, v, r, ALU.mult), t)
            t = t_d[(w, c, g)] = vec(lambda e, v=v, gv=gv: e.tensor_tensor(v, v, gv, ALU.mult), t, t_v[3], t_v[4])
        for c in range(2):
            t_OT += transposes([(OT[:, :, c * P:(c + 1) * P], [O[:, c, k * P:(k + 1) * P] for k in range(4)])],
                               t_o[c], eng="act")
        fill(4)
        t_T = []
        for g in range(3):
            for c in range(2):
                for w, dst in ((0, qd), (1, kd)):
                    lo = 1056 + 1536 * w + 512 * g
                    t_T += transposes([(dst[:, 4 * g:4 * g + 4, c * P:(c + 1) * P],
                                        [Pj[:, c, lo + P * i:lo + P * (i + 1)] for i in range(4)])],
                                      t_d[(w, c, g)], t_qfree, eng="act")
                fill(1)

        t_m = []
        t_sig = {}

        def sigmoid():
            t_g = need(5664, 7712)
            for c in range(2):
                v = Pj[:, c, 5664:7712]
                t_sig[c] = scal(lambda e, v=v: e.activation(v, v, ACT.Sigmoid), t_g)

        def m0_steps(c0):
            if not t_sig:
                sigmoid()

            def go(c, ps, t):
                g = Pj[:, c, 5664 + c0:5664 + c0 + 512]
                t = vec(lambda e: e.tensor_tensor(g, g, ps, ALU.mult), t, t_sig[c])
                t_m.append(t)
                return t
            yield from project_steps(kview(a["w_o_mla"][0]), c0, 512, go, t_OT, lhs=OT, kn=4)

        t_v8 = need(4128, 5664)
        need(5664, 7712)
        filler.extend(m0_steps(c0) for c0 in (0, 512))
        jobs = []
        for c in range(2):
            ob = bank(hold=True)
            for h in range(8):
                p0 = 64 * (h % 2)
                slope = 2.0 ** (-8.0 * (h + 1.0) / 8)
                kw = (c + 1) * P
                bo = 0 if c == 0 else 384
                parts = [(qd[p0:p0 + 64, 4 * g + h // 2, c * P:(c + 1) * P],
                          kd[p0:p0 + 64, 4 * g + h // 2, 0:kw], kw,
                          Bm[:, bo + g * kw:bo + (g + 1) * kw], -8.0 * slope) for g in range(3)]
                vs = [Pj[:, kc, 4128 + 512 * g + 64 * h:4128 + 512 * g + 64 * h + 64]
                      for g in range(3) for kc in range(c + 1)]
                jobs.append((c, parts, 0.125, vs, ob, 64 * h, 64, 8 * c + h, [t_T, t_v8]))
        t_o = []
        for c, ob, t in attend(jobs, lambda n: 1 if n in (3, 5, 7, 9) else 0):
            t_o.append(normalise(c, ob, O[:, c, :], 8, 64, [t, t_OT]))
        fill(4)
        t_f = q_pe()
        t_OT = []
        for c in range(2):
            t_OT += transposes([(OT[:, :, c * P:(c + 1) * P], [O[:, c, k * P:(k + 1) * P] for k in range(4)])],
                               t_o[c], t_f)
        t_m2 = []

        def m1_sink(c0):
            def go(c, ps, t):
                g = Pj[:, c, 6688 + c0:6688 + c0 + 512]
                m = Pj[:, c, 5664 + c0:5664 + c0 + 512]
                t = t_b = vec(lambda e: e.tensor_tensor(g, g, ps, ALU.mult), t, t_sig[c])
                t_m2.append(vec(lambda e: e.tensor_tensor(m, m, g, ALU.add), t, t_m))
                return t_b
            return go

        for c0 in (0, 512):
            project(kview(a["w_o_dil"][0]), c0, 512, m1_sink(c0), t_OT, lhs=OT, kn=4)
        t_hT = []
        t_f = q_pe()
        for c in range(2):
            t_hT += transposes([(hT[:, k:k + 4, c * P:(c + 1) * P],
                                 [Pj[:, c, 5664 + (k + i) * P:5664 + (k + i + 1) * P] for i in range(4)])
                                for k in (0, 4)], t_m2, t_f)

        t_fence = q.all_done()
        NT = 35
        NTW = 36
        at = [0]

        def take(n):
            v = arena[:, at[0]:at[0] + n]
            at[0] += n
            assert at[0] <= AR
            return v
        lg = take(72).rearrange("p (c n) -> p c n", c=2)
        oh = take(128).rearrange("p (c k n) -> p c k n", c=2, k=2)
        Ms = take(64).rearrange("p (c n) -> p c n", c=2)
        g8s, s8s, v8s, w8s, w1s = [[take(8) for _ in range(2)] for _ in range(5)]
        u8s = [take(8) for _ in range(2)]
        idx = take(16).bitcast(U32)
        gone = take(4)
        rowhot, tilehot = take(4 * P), take(4 * 36)
        ek, wk, rk, ok, fk = take(4), take(4), take(4), take(4), take(4)
        rks = take(96)
        over, oi, oo, eqo = take(32), take(32), take(32), take(32)
        jk = take(32)
        overT = take(128)
        eo = take(4)
        eo_u = take(4).bitcast(U32)
        tab_r = take(NTW).bitcast(U32)
        tab_g = take(NTW).bitcast(U32)
        xg = take(4 * D).rearrange("p (i d) -> p i d", i=4)
        gT = take(3 * D).rearrange("p (i k t) -> p i k t", i=3, k=8)
        he = take(512).rearrange("p (i n) -> p i n", i=2)
        heT = take(512).rearrange("p (i f t) -> p i f t", i=2, f=2)
        ys = take(3 * D).rearrange("p (i d) -> p i d", i=3)
        yb = take(4 * D).rearrange("p (c k d) -> p c k d", c=2, k=2)

        h_rows = nc.dram_tensor("h_rows", [T, D], F32).ap()
        y_rows = nc.dram_tensor("y_rows", [2 * T, D], F32).ap()

        t_xg = put("pool", lambda e: e.memset(xg, 0.0), t_fence)

        i32 = iota32[:, 0:32]
        t_neg = [put("dve", lambda e, c=c: e.memset(g8s[c], NEG), t_fence) for c in range(2)]
        t_lg = {}

        def router(c, t):
            br = bank(hold=True)

            def go(e):
                for k in range(8):
                    r = e.matmul(banks[:, br, 0:36], hT[:, k, c * P:(c + 1) * P], rw[:, k, :],
                                 start=(k == 0), stop=(k == 7))
                return r
            t_lg[c] = br, put("pe", go, t, t_v, bank_free[br])

        def choose(c):
            br, t = t_lg[c]
            t = bank_free[br] = vec(lambda e: e.tensor_tensor(lg[:, c, :], banks[:, br, 0:36], rb, ALU.add), t, t_v)
            held.discard(br)
            l, g8, s8, v8, u8, w1, w8 = lg[:, c, :], g8s[c], s8s[c], v8s[c], u8s[c], w1s[c], w8s[c]
            t = vec(lambda e, l=l, g8=g8: e.tensor_copy(g8[:, 0:4], l[:, 0:4]), t, t_neg)
            t = vec(lambda e, v8=v8, g8=g8: e.max(v8, g8), t)
            t = vec(lambda e, v8=v8, g8=g8: e.max_index(idx[:, 0:8], v8, g8), t)
            t = vec(lambda e, w1=w1: e.tensor_copy(w1[:, 2:3], idx[:, 0:1]), t)
            t = vec(lambda e, w1=w1: e.tensor_scalar(gone, i32[:, 0:4], w1[:, 2:3], None, ALU.is_equal), t, t_io)
            sel = Ms[:, c, :].rearrange("p (g e) -> p g e", g=4)
            t = vec(lambda e, l=l, sel=sel: e.tensor_tensor(
                sel, l[:, 4:36].rearrange("p (g e) -> p g e", g=4),
                gone.unsqueeze(2).to_broadcast([P, 4, 8]), ALU.mult), t)
            t = vec(lambda e, sel=sel, s8=s8: e.tensor_reduce(s8, sel.rearrange("p g e -> p e g"), X, ALU.add), t)
            t = vec(lambda e, u8=u8, s8=s8: e.max(u8, s8), t)
            t = vec(lambda e, u8=u8, s8=s8: e.max_index(idx[:, 8:16], u8, s8), t)
            t = vec(lambda e, w1=w1: e.tensor_copy(w1[:, 4:6], idx[:, 8:10]), t)
            t = vec(lambda e, c=c, w1=w1: e.scalar_tensor_tensor(
                ek[:, 2 * c:2 * c + 2], w1[:, 2:3].to_broadcast([P, 2]), 8.0, w1[:, 4:6], ALU.mult, ALU.add), t)
            for k in range(2):
                t = vec(lambda e, c=c, k=k: e.tensor_scalar(
                    oh[:, c, k, :], i32, ek[:, 2 * c + k:2 * c + k + 1], None, ALU.is_equal), t)
            t_Ms[c] = vec(lambda e, c=c: e.tensor_tensor(Ms[:, c, :], oh[:, c, 0, :], oh[:, c, 1, :], ALU.add), t)

        t_Ms = {}
        t_h0 = []
        t_x, t_xn, t_h = residual_norm(kview(a["w_out"][0]), hT, [t_hT, t_hT], g_ffn,
                                       (t_h0.append, lambda t_x0, t_n0: router(0, t_h0[0])))
        router(1, t_h[1])
        choose(0)
        t_hr = fetch(h_rows.rearrange("(c p) d -> p c d", p=P), xn[:, :, :], t_xn, eng="sp")
        choose(1)
        t_r = t_x
        gain_free[0] = q.all_done()
        t_M = [t_Ms[0], t_Ms[1]]
        t = dve_now()

        bk = bank()

        def ranks(e):
            e.matmul(banks[:, bk, 0:32], tri, Ms[:, 0, :], start=True, stop=True)
            e.matmul(banks[:, bk, 32:64], tri, Ms[:, 1, :], start=True, stop=False)
            e.matmul(banks[:, bk, 32:64], ones, Ms[:, 0, :], start=False, stop=True)
            e.matmul(banks[:, bk, 64:96], ones, Ms[:, 0, :], start=True, stop=False)
            return e.matmul(banks[:, bk, 64:96], ones, Ms[:, 1, :], start=False, stop=True)
        t1 = put("pe", ranks, t_M, t_tri, t_one, bank_free[bk])
        bk2 = bank()

        def counts(e):
            e.matmul(banks[0:32, bk2, 0:P], Ms[:, 0, :], ones, start=True, stop=False)
            return e.matmul(banks[0:32, bk2, 0:P], Ms[:, 1, :], ones, start=False, stop=True)
        t2 = put("pe", counts, bank_free[bk2])
        t = vec(lambda e: e.tensor_scalar(overT[0:32, :], banks[0:32, bk2, 0:P], float(P), None, ALU.is_gt), t2)
        bank_free[bk2] = t
        bk3 = bank()
        t3 = put("pe", lambda e: e.matmul(banks[:, bk3, 0:32], overT[0:32, :], tri32[0:32, :], start=True, stop=True),
                 t, t_tri32, bank_free[bk3])
        t = vec(lambda e: e.tensor_copy(rks, banks[:, bk, 0:96]), t1)
        bank_free[bk] = t
        for c in range(2):
            for k in range(2):
                t = vec(lambda e, c=c, k=k: e.tensor_tensor_reduce(
                    jk, oh[:, c, k, :], rks[:, 32 * c:32 * c + 32], 1.0, 0.0, ALU.mult, ALU.add,
                    rk[:, 2 * c + k:2 * c + k + 1]), t)
        t = vec(lambda e: e.tensor_scalar(over, rks[:, 64:96], float(P), None, ALU.is_gt), t)
        t = vec(lambda e: e.tensor_copy(oo, banks[:, bk3, 0:32]), t3)
        bank_free[bk3] = t
        for c in range(2):
            for k in range(2):
                t = vec(lambda e, c=c, k=k: e.tensor_tensor_reduce(
                    jk, oh[:, c, k, :], oo, 1.0, 0.0, ALU.mult, ALU.add, ok[:, 2 * c + k:2 * c + k + 1]), t)
        t = vec(lambda e: e.tensor_scalar(fk, rk, float(P), None, ALU.is_ge), t)
        t = vec(lambda e: e.scalar_tensor_tensor(rk, fk, -float(P), rk, ALU.mult, ALU.add), t)
        t = vec(lambda e: e.tensor_tensor(ok, ok, ek, ALU.subtract), t)
        t = vec(lambda e: e.scalar_tensor_tensor(ok, ok, 32.0, fk, ALU.add, ALU.mult), t)
        t = vec(lambda e: e.tensor_tensor(ok, ok, ek, ALU.add), t)
        for m in range(4):
            t = vec(lambda e, m=m: e.tensor_scalar(rowhot[:, P * m:P * (m + 1)], iota128, rk[:, m:m + 1], None,
                                                   ALU.is_equal), t)
            t = vec(lambda e, m=m: e.tensor_scalar(tilehot[:, 36 * m:36 * (m + 1)], iota32, ok[:, m:m + 1],
                                                   ids[:, m:m + 1], ALU.is_equal, ALU.mult), t, t_ids)
        bs = bank()

        def table(e):
            for m in range(4):
                r = e.matmul(banks[:, bs, 0:NTW], rowhot[:, P * m:P * (m + 1)], tilehot[:, 36 * m:36 * (m + 1)],
                             start=(m == 0), stop=(m == 3))
            return r
        t = put("pe", table, t, bank_free[bs])
        t_tab = vec(lambda e: e.tensor_scalar(tab_r, banks[:, bs, 0:NTW], NONE, None, ALU.add), t)
        bank_free[bs] = t_tab
        t_tabg = vec(lambda e: e.tensor_scalar(tab_g, tab_r, 1, None, ALU.logical_shift_right), t_tab)
        t = vec(lambda e: e.tensor_tensor(oi, over, i32, ALU.mult))
        for o in range(3):
            t = vec(lambda e, o=o: e.tensor_scalar(eqo, oo, float(o), None, ALU.is_equal), t)
            t = vec(lambda e, o=o: e.tensor_tensor_reduce(jk, eqo, oi, 1.0, 0.0, ALU.mult, ALU.add, eo[:, o:o + 1]), t)
        t = vec(lambda e: e.tensor_reduce(eo[:, 3:4], over, X, ALU.add), t)
        t_eo = vec(lambda e: e.tensor_copy(eo_u, eo), t)
        for c in range(2):
            g8, v8, u8, w1, w8 = g8s[c], v8s[c], u8s[c], w1s[c], w8s[c]
            t = vec(lambda e, v8=v8, w1=w1: e.tensor_scalar(w1[:, 0:1], v8[:, 0:1], -1.0, None, ALU.mult), t)
            t = vec(lambda e, u8=u8, w1=w1: e.tensor_scalar(w1[:, 3:4], u8[:, 0:1], -1.0, None, ALU.mult), t)
            scal(lambda e, g8=g8, w1=w1, w8=w8: e.activation(w8[:, 0:4], g8[:, 0:4], ACT.Exp, bias=w1[:, 0:1],
                                                             accum_out=w1[:, 1:2]), t)
            ta = scal(lambda e, u8=u8, w1=w1, w8=w8: e.activation(w8[:, 0:2], u8[:, 0:2], ACT.Exp,
                                                                  bias=w1[:, 3:4], accum_out=w1[:, 6:7]), t)
            t = vec(lambda e, w1=w1: e.tensor_scalar(w1[:, 6:7], w1[:, 6:7], w1[:, 1:2], None, ALU.mult), ta)
            t = vec(lambda e, w1=w1: e.reciprocal(w1[:, 6:7], w1[:, 6:7]), t)
            t = t_wk = vec(lambda e, c=c, w1=w1, w8=w8: e.tensor_scalar(
                wk[:, 2 * c:2 * c + 2], w8[:, 0:2], w1[:, 6:7], None, ALU.mult), t)
        second = {}

        def read_expert(o):
            def go(e):
                second[o] = e.value_load(eo_u[0:1, o:o + 1], min_val=0, max_val=31)
            q.step("sp", go, t_eo)

        xg_sems = [sem(f"s_xg{i}") for i in range(4)]
        ys_sems = [sem(f"s_ys{i}") for i in range(3)]
        xg_free = [t_xg] * 4
        ys_free = [t_fence] * 3
        gT_free, he_free, heT_free = [t_fence] * 3, [t_fence] * 2, [t_fence] * 2
        xg_tok = {}
        last = [0]

        def rows_in(n):
            i = n % 4
            xg_tok[n] = dma("pool", lambda e: e.indirect_dma_start(
                xg[:, i, :], None, h_rows, bass.IndirectOffsetOnAxis(ap=tab_g[:, n:n + 1], axis=0),
                bounds_check=T - 1, oob_is_err=False), xg_sems[i], xg_free[i], t_tabg, t_hr, t_xg)

        def expert(w, n):
            if n < 32:
                return w[0][n]
            return w[0][bass.ds(second[n - 32], 1)].rearrange("a r c -> (a r) c")

        def load_pair(n, kk):
            s = slot_next[0] % NSLOT
            slot_next[0] += 1
            dst = ring[:, s, :].rearrange("p (k g c) -> p k g c", k=4, g=2)
            for g_, w in enumerate((a["w_gate"], a["w_up"])):
                t = dma("sp", lambda e, g_=g_, w=w: e.dma_start(
                    dst[:, :, g_, :], expert(w, n).rearrange("(k p) n -> p k n", p=P)[:, kk:kk + 4, :]),
                    slot_sem[s], slot_free[s])
            return s, dst.rearrange("p k g c -> p k (g c)"), t

        def turn_rows(n):
            if n + 3 < last[0]:
                rows_in(n + 3)
            i = n % 4
            t = transposes([(gT[:, n % 3, k:k + 4, :],
                             [xg[:, i, (k + r_) * P:(k + r_ + 1) * P] for r_ in range(4)])
                            for k in (0, 4)], xg_tok[n], gT_free[n % 3])
            xg_free[i] = q_pe()
            return t

        def up(n, tt):
            if n >= 32:
                read_expert(n - 32)
            j = n % 2
            b = bank(hold=True)
            for kk in (0, 4):
                s, wt, t_w = load_pair(n, kk)

                def go(e, kk=kk, wt=wt):
                    for k in range(4):
                        r = e.matmul(banks[:, b, :], gT[:, n % 3, kk + k, :], wt[:, k, :],
                                     start=(kk + k == 0), stop=(kk + k == 7))
                    return r
                t = put("pe", go, t_w, tt, bank_free[b])
                slot_free[s] = t
            gT_free[n % 3] = t
            hv = he[:, j, :]
            t = put("act", lambda e: e.activation(hv, banks[:, b, 0:256], ACT.Silu), t, he_free[j])
            t = put("dve", lambda e: e.tensor_tensor(hv, hv, banks[:, b, 256:512], ALU.mult), t)
            bank_free[b] = t
            held.discard(b)
            return t

        def turn_he(n, t_he):
            j = n % 2
            tt = transposes([(heT[:, j, :, :], [he[:, j, f * P:(f + 1) * P] for f in range(2)])], t_he, heT_free[j],
                            eng="act")
            he_free[j] = q_pe()
            return tt

        def down(n, tt):
            j = n % 2
            i = n % 3
            s = slot_next[0] % NSLOT
            slot_next[0] += 1
            wt = ring[:, s, :].rearrange("p (k c) -> p k c", k=2)
            t_w = dma("sp", lambda e: e.dma_start(
                wt, expert(a["w_down"], n).rearrange("(k p) n -> p k n", p=P)), slot_sem[s], slot_free[s])
            tc = []
            for hf in range(2):
                b = bank()

                def go(e, hf=hf, b=b):
                    for f in range(2):
                        r = e.matmul(banks[:, b, :], heT[:, j, f, :], wt[:, f, hf * 512:(hf + 1) * 512],
                                     start=(f == 0), stop=(f == 1))
                    return r
                t = put("pe", go, t_w, tt, bank_free[b])
                bank_free[b] = t2 = evac(ys[:, i, hf * 512:(hf + 1) * 512], banks[:, b, :], t, ys_free[i])
                tc.append(t2)
            slot_free[s] = heT_free[j] = t
            ys_free[i] = dma("pool", lambda e: e.indirect_dma_start(
                y_rows, bass.IndirectOffsetOnAxis(ap=tab_r[:, n:n + 1], axis=0), ys[:, i, :], None,
                bounds_check=2 * T - 1, oob_is_err=False), ys_sems[i], tc)

        def tiles(lo, hi):
            last[0] = hi
            for n in range(lo, min(lo + 3, hi)):
                rows_in(n)
            tts = {lo: turn_rows(lo), lo + 1: turn_rows(lo + 1)}
            pend = up(lo, tts[lo])
            for n in range(lo, hi):
                if n + 2 < hi:
                    tts[n + 2] = turn_rows(n + 2)
                th = turn_he(n, pend)
                if n + 1 < hi:
                    pend = up(n + 1, tts[n + 1])
                down(n, th)

        tiles(0, 32)
        q.begin_if(eo_u[0:1, 3:4], t_eo)
        ys_main = list(ys_free)
        xg_sems, ys_sems = [sem(f"s_xh{i}") for i in range(4)], [sem(f"s_yh{i}") for i in range(3)]
        tiles(32, NT)
        t_over = put("pool", lambda e: e.memset(gone[0:1, 0:1], 0.0), ys_free)
        q.end_if({s_.name for s_ in xg_sems + ys_sems})
        ys_free = ys_main + [t_over]
        y_view = y_rows.rearrange("(c p k) d -> p c k d", p=P, k=2)
        t_yb = [fetch(yb[:, c], y_view[:, c], ys_free) for c in range(2)]
        load_wait[0] = [(1, t_yb)]
        g_mix0 = load_gain(a["norm_mix_2"][0])
        ss_mix, t_free, t_n = sm(2), q_pe(), []
        t_r = []
        for c in range(2):
            for k in range(2):
                t = vec(lambda e, c=c, k=k: e.scalar_tensor_tensor(
                    x[:, c, :], yb[:, c, k, :], wk[:, 2 * c + k:2 * c + k + 1], x[:, c, :], ALU.mult, ALU.add),
                    t_yb[c], t_wk)
            t_r.append(t)
            t_n.append(norm_chunk(c, g_mix0, ss_mix, t, t_free))

        P2 = arena[:, 0:7168].rearrange("p (c n) -> p c n", c=2)
        q2 = arena[:, 7168:7168 + 4096].rearrange("p (j t) -> p j t", t=T)
        dec = arena[:, 11264:11264 + 1536].rearrange("p (h n) -> p h n", h=4)
        tab = arena[:, 12800:13056].rearrange("p (s c n) -> p s c n", s=2, c=2)
        RT = arena[:, 13056:13056 + 768].rearrange("p (i n) -> p i n", i=2)
        tmp2 = arena[:, 14000:14000 + 2048]
        cat = arena[:, 16384:16384 + 2048].rearrange("p (c n) -> p c n", c=2)
        t_fence = q.all_done()
        t_dec = fetch(dec, a["c_decay"], t_fence)
        t_tab = fetch(tab, a["c_rope2"], t_fence)
        t_h = [turn_chunk(c, t_n[c]) for c in range(2)]
        t_P.clear()
        w_e = kview(a["even_w_in_2"][0])

        def sink_P2(c0):
            def go(c, ps, t):
                v = P2[:, c, c0:c0 + 512]
                if c0 == 3072:
                    t = scal(lambda e: e.activation(v, ps, ACT.Silu), t, t_fence)
                else:
                    t = evac(v, ps, t, t_fence)
                t_P[(c0, c)] = t
                return t
            return go
        for j in (0, 1):
            project(w_e, 512 * j, 512, sink_P2(512 * j), t_h)
        filler.extend(project_steps(w_e, 512 * j, 512, sink_P2(512 * j), t_h) for j in (2, 3, 4, 5, 6))

        def need2(c0, c):
            while (c0, c) not in t_P:
                fill()
            return t_P[(c0, c)]

        t_kinds = {}

        def rope_pair(lo):
            for c in range(2):
                v = P2[:, c, lo:lo + 1024].rearrange("p (h n) -> p h n", h=8)
                t_kinds[(lo, c)] = rope(v, tab[:, 0, c, :], tab[:, 1, c, :], 64, tmp2,
                                        need2(lo, c), need2(lo + 512, c), t_tab)

        t_T = {}

        def turn_kinds(kinds):
            for kind in kinds:
                lo = (0, 512, 1536, 2048)[kind]
                t_T[kind] = []
                for c in range(2):
                    t_T[kind] += transposes([(q2[:, 4 * kind:4 * kind + 4, c * P:(c + 1) * P],
                                              [P2[:, c, lo + i * P:lo + (i + 1) * P] for i in range(4)])],
                                            t_kinds[(0 if lo < 1024 else 1536, c)])

        rope_pair(0)
        fill(2)
        turn_kinds((0, 1))
        jobs = []
        for c in range(2):
            ob = bank(hold=True)
            for h in range(4):
                parts = [causal_part(c, q2[:, h, c * P:(c + 1) * P], lambda lo, hi, h=h: q2[:, 4 + h, lo:hi])]
                jobs.append((c, parts, 128 ** -0.5, [P2[:, kc, 1024 + P * h:1024 + P * (h + 1)] for kc in range(c + 1)],
                             ob, P * h, P, 8 * c + h, [t_T[0], t_T[1], need2(1024, 0), need2(1024, 1)]))
        t_cat = []
        for c, ob, t in attend(jobs, lambda n: 1):
            t_cat.append(normalise(c, ob, cat[:, c, 0:512], 4, 128, t))
            if c == 0:
                rope_pair(1536)
        turn_kinds((2, 3))
        while filler:
            fill()
        rt_free = [None, None]
        t_f = q_pe()
        t_hT = []
        steps = [(c, h) for c in range(2) for h in range(4)]
        t_rt, ret_bank = {}, {}

        def ret_scores(m):
            c, h = steps[m]
            i, w_, b = m % 2, P * (c + 1), bank()

            def go(e):
                for kc in range(c + 1):
                    r = e.matmul(banks[:, b, P * kc:P * (kc + 1)], q2[:, 12 + h, P * kc:P * (kc + 1)],
                                 q2[:, 8 + h, P * c:P * (c + 1)], start=True, stop=True)
                return r
            t = put("pe", go, t_T[2], t_T[3], bank_free[b])
            bank_free[b] = t_rt[m] = put("dve", lambda e: e.tensor_tensor(
                RT[:, i, 0:w_], banks[:, b, 0:w_], dec[:, h, P * c:P * c + w_], ALU.mult), t, t_dec, rt_free[i])

        def ret_values(m):
            c, h = steps[m]
            i = m % 2
            if h == 0:
                ret_bank[c] = bank(hold=True)
            ob = ret_bank[c]

            def go(e):
                for kc in range(c + 1):
                    r = e.matmul(banks[:, ob, P * h:P * (h + 1)], RT[:, i, P * kc:P * (kc + 1)],
                                 P2[:, kc, 2560 + P * h:2560 + P * (h + 1)], start=(kc == 0), stop=(kc == c))
                return r
            t = put("pe", go, t_rt[m], t_P[(2560, 0)], t_P[(2560, 1)], bank_free[ob] if h == 0 else None)
            rt_free[i] = t
            return t
        ret_scores(0)
        for c in range(2):
            for m in range(4 * c, 4 * c + 4):
                if m < 7:
                    ret_scores(m + 1)
                t = ret_values(m)
            ob = ret_bank[c]
            cv = cat[:, c, 512:1024]
            cv3 = cv.rearrange("p (h n) -> p h n", h=4)
            sq = tmp2[:, 0:512].rearrange("p (h n) -> p h n", h=4)
            ss = ssq[:, 0, 0:4]
            t = vec(lambda e, cv=cv, ob=ob: e.tensor_copy(cv, banks[:, ob, :]), t)
            bank_free[ob] = t
            held.discard(ob)
            t = scal(lambda e, cv3=cv3: e.activation(sq, cv3, ACT.Square), t, dve_now())
            t = vec(lambda e: e.tensor_reduce(ss, sq, X, ALU.add), t)
            t_s = rsqrt(ss, ss, 128, t)
            t = vec(lambda e, cv=cv, c=c: e.tensor_tensor(cv, cv, P2[:, c, 3072:3584], ALU.mult),
                    t, t_P[(3072, c)])
            t = vec(lambda e, cv3=cv3: e.tensor_tensor(
                cv3, cv3, ss.unsqueeze(2).to_broadcast([P, 4, P]), ALU.mult), t_s)
            t_hT.append((c, t))
        t_done = t_hT
        t_hT = [transposes([(hT[:, k:k + 4, c * P:(c + 1) * P],
                             [cat[:, c, (k + i) * P:(k + i + 1) * P] for i in range(4)])
                            for k in (0, 4)], t, t_cat, t_f) for c, t in t_done]
        g = load_gain(a["norm_ffn_2"][0])
        early = q.all_done()
        g_mix1 = load_gain(a["norm_mix_2"][1])
        def even_out(mid):
            return residual_norm(kview(a["even_w_out_2"][0]), hT, t_hT, g, mid)

        iota16 = sm(16)
        t_i16 = put("pool", lambda e: e.iota(iota16, [[1, 16]], base=0, channel_multiplier=0,
                                             allow_small_or_imprecise_dtypes=True))
        g_sems = [sem(f"s_g{i}") for i in range(NG)]
        rows_free = [None] * NG
        rows_n = [0]
        tops = sm(2, 128)
        hid = sm(2, 128)
        top3 = tops.rearrange("p c (h k) -> p c h k", h=8)
        hid3 = hid.rearrange("p c (h k) -> p c h k", h=8)
        gz = sm(4)

        def peer(layer, into, t_early):
            at = [0]

            def take(n):
                v = arena[:, at[0]:at[0] + n]
                at[0] += n
                assert at[0] <= AR
                return v
            rows = take(NG * D).rearrange("p (i d) -> p i d", i=NG)
            qp = [take(512) for _ in range(2)]
            sc = [take(512).rearrange("p (j n) -> p j n", j=4) for _ in range(2)]
            cand = take(512).rearrange("p (c n) -> p c n", c=2)
            eq = take(512)
            diag = take(512).rearrange("p (i n) -> p i n", i=4)
            vals = take(64).rearrange("p (j n) -> p j n", j=4)
            ti = take(64)
            iu = take(64).bitcast(U32)
            pu = take(96).bitcast(U32)
            eix = take(256).bitcast(U32).rearrange("p (c n) -> p c n", c=2)
            af = take(32)
            e12 = take(64).rearrange("p (s n) -> p s n", s=2)
            table_u = a["peer_u_2"].rearrange("l e d -> (l e) d")
            table_v = a["peer_v_2"].rearrange("l e d -> (l e) d")
            w = kview(a["peer_w_q_2"][layer])
            kt = take(2048).rearrange("p (j n) -> p j n", j=16)
            t_kt = fetch(kt, a["c_keys"][layer], t_early)
            qp_free, sc_free = [t_early, t_early], [t_early, t_early]
            t_sc = {}
            acc = [[bank(hold=True), bank(hold=True)], [bank(hold=True), bank(hold=True)]]

            w0 = []

            def score(h, cs, t_h):
                if not w0:
                    w0.append(load(w[:, :, 256 * h:256 * (h + 1)], 8))
                s, wt, t_w = w0[0]
                b = bank()
                lo, hi = P * cs[0], P * (cs[-1] + 1)

                def go(e):
                    for f in range(2):
                        for k in range(8):
                            r = e.matmul(banks[:, b, f * T + lo:f * T + hi], wt[:, k, f * P:(f + 1) * P],
                                         hT[:, k, lo:hi], start=(k == 0), stop=(k == 7))
                    return r
                t = put("pe", go, t_w, t_h, bank_free[b])
                if cs[-1] == 1:
                    slot_free[s] = t
                    w0.clear()
                qv = qp[h % 2]
                bank_free[b] = t = put("act", lambda e: e.copy(
                    qv.rearrange("p (f t) -> p f t", f=2)[:, :, lo:hi],
                    banks[:, b, :].rearrange("p (f t) -> p f t", f=2)[:, :, lo:hi]), t, qp_free[h % 2])
                b2 = bank()

                def go2(e):
                    for c in cs:
                        for f in range(2):
                            r = e.matmul(banks[:, b2, (2 * c + f) * P:(2 * c + f + 1) * P],
                                         qv[:, f * T + c * P:f * T + (c + 1) * P], kt[:, 2 * h + f, :],
                                         start=True, stop=True)
                    return r
                t_q = put("pe", go2, t, t_kt, bank_free[b2])
                bank_free[b2] = t = put("act", lambda e: e.copy(
                    sc[h % 2].rearrange("p j n -> p (j n)")[:, 2 * lo:2 * hi], banks[:, b2, 2 * lo:2 * hi]),
                    t_q, sc_free[h % 2])
                for c in cs:
                    t_sc[(h, c)] = t
                if cs[-1] == 1:
                    qp_free[h % 2] = t_q

            t_sel = {}

            def select(h, cs):
                t_cell = [[t_sc[(h, c)] for c in cs] + [t_early]]
                n = len(cs)
                lo, hi = 16 * cs[0], 16 * (cs[-1] + 1)
                c_ = slice(cs[0], cs[-1] + 1)

                def step(fn, *after):
                    t_cell[0] = put("dve", fn, t_cell[0], (q.sems["dve"], q.count["dve"]), *after)
                    return t_cell[0]

                def top16(v, vout, iout):
                    step(lambda e: e.max(vout[:, 0:8], v))
                    yield
                    step(lambda e: e.max_index(iout[:, 0:8], vout[:, 0:8], v))
                    yield
                    step(lambda e: e.match_replace(v, vout[:, 0:8], v, -3e38))
                    yield
                    step(lambda e: e.max(vout[:, 8:16], v))
                    yield
                    step(lambda e: e.max_index(iout[:, 8:16], vout[:, 8:16], v))
                    yield

                for j in range(2 * cs[0], 2 * cs[-1] + 2):
                    yield from top16(sc[h % 2][:, j, :], vals[:, j, :], iu[:, 16 * j:16 * j + 16])
                sc_free[h % 2] = t_cell[0]
                step(lambda e: e.tensor_copy(ti[:, 2 * lo:2 * hi], iu[:, 2 * lo:2 * hi]))
                yield
                for c in cs:
                    step(lambda e, c=c: e.tensor_tensor(
                        cand[:, c, :].rearrange("p (i j) -> p i j", i=16),
                        vals[:, 2 * c, :].unsqueeze(2).to_broadcast([P, 16, 16]),
                        vals[:, 2 * c + 1, :].unsqueeze(1).to_broadcast([P, 16, 16]), ALU.add))
                    yield
                for c in cs:
                    yield from top16(cand[:, c, :], top3[:, c, h, :], pu[:, 16 * c:16 * c + 16])
                e3 = e12[:, 0, :].rearrange("p (c k) -> p c k", c=2)[:, c_]
                tv = top3[:, c_, h, :]
                t_x = step(lambda e: e.tensor_tensor(e3, tv, tv[:, :, 0:1].to_broadcast([P, n, 16]), ALU.subtract))
                t_x = put("act", lambda e: e.activation(tv, e3, ACT.Exp), t_x)
                yield
                step(lambda e: e.tensor_scalar(pu[:, 32 + lo:32 + hi], pu[:, lo:hi], 4, None, ALU.logical_shift_right))
                yield
                step(lambda e: e.tensor_scalar(pu[:, 64 + lo:64 + hi], pu[:, lo:hi], 15, None, ALU.bitwise_and))
                yield
                eqv = eq[:, 16 * lo:16 * hi]
                for s_, o in ((0, 32), (1, 64)):
                    step(lambda e, o=o: e.tensor_copy(af[:, lo:hi], pu[:, o + lo:o + hi]))
                    yield
                    step(lambda e: e.tensor_tensor(
                        eqv.rearrange("p (m j) -> p m j", j=16), iota16.unsqueeze(1).to_broadcast([P, 16 * n, 16]),
                        af[:, lo:hi].unsqueeze(2).to_broadcast([P, 16 * n, 16]), ALU.is_equal), t_i16)
                    yield
                    step(lambda e, s_=s_: e.tensor_tensor(
                        eqv.rearrange("p (c k j) -> p c k j", c=n, k=16), eqv.rearrange("p (c k j) -> p c k j", c=n, k=16),
                        ti.rearrange("p (c s j) -> p s c j", c=2, s=2)[:, s_, c_].unsqueeze(2).to_broadcast([P, n, 16, 16]),
                        ALU.mult))
                    yield
                    step(lambda e, s_=s_: e.tensor_reduce(
                        e12[:, s_, lo:hi], eqv.rearrange("p (m j) -> p m j", j=16), X, ALU.add), t_x)
                    yield
                step(lambda e: e.scalar_tensor_tensor(e12[:, 0, lo:hi], e12[:, 0, lo:hi], 128.0, e12[:, 1, lo:hi],
                                                      ALU.mult, ALU.add))
                yield
                t_e = step(lambda e: e.tensor_scalar(
                    eix[:, c_, 16 * h:16 * h + 16], e12[:, 0, lo:hi].rearrange("p (c k) -> p c k", c=n),
                    float(128 * 128 * layer), None, ALU.add))
                for c in cs:
                    t_sel[(h, c)] = t_e
                yield
                gs, gr = gz[:, cs[0]:cs[-1] + 1], gz[:, 2 + cs[0]:3 + cs[-1]]
                step(lambda e: e.tensor_reduce(gs, tv, X, ALU.add))
                yield
                step(lambda e: e.reciprocal(gr, gs))
                yield
                t_gate[h] = step(lambda e: e.tensor_tensor(tv, tv, gr.unsqueeze(2).to_broadcast([P, n, 16]), ALU.mult))

            t_gate = {}

            def gather(table, h, c, k):
                i = rows_n[0] % NG
                rows_n[0] += 1
                t = dma("pool", lambda e: e.indirect_dma_start(
                    rows[:, i, :], None, table,
                    bass.IndirectOffsetOnAxis(ap=eix[:, c, 16 * h + k:16 * h + k + 1], axis=0)),
                    g_sems[i], rows_free[i], t_sel[(h, c)])
                return i, t

            def u_step(h, c, k):
                i, t = early_rows.pop(0) if early_rows else gather(table_u, h, c, k)
                rows_free[i] = put("dve", lambda e: e.tensor_tensor_reduce(
                    rows[:, i, :], rows[:, i, :], xn[:, c, :], 1.0, 0.0, ALU.mult, ALU.add,
                    hid3[:, c, h, k:k + 1]), t, t_n[c])
                return rows_free[i]

            d_free = [None] * 4
            d_n = [0]
            on_pe = {}

            def v_step(h, c, k, tail):
                t_w = t_ws[h]
                i, t = gather(table_v, h, c, k)
                if tail and k % 3 == 2:
                    rows_free[i] = acc_tok[c] = put("dve", lambda e: e.scalar_tensor_tensor(
                        x[:, c, :], rows[:, i, :], hid3[:, c, h, k:k + 1], x[:, c, :], ALU.mult, ALU.add),
                        t, t_w, acc_tok[c])
                    return
                d = d_n[0] % 4
                d_n[0] += 1
                td = put("act", lambda e: e.activation(diag[:, d, :], ident[:, :], ACT.Copy,
                                                       scale=hid3[:, c, h, k:k + 1]), t_w, t_id, d_free[d])
                first, last = c not in on_pe, (h == 7 and k == 15)

                def go(e):
                    for hf in range(2):
                        r = e.matmul(banks[:, acc[c][hf], :], diag[:, d, :], rows[:, i, hf * 512:(hf + 1) * 512],
                                     start=first, stop=last)
                    return r
                d_free[d] = rows_free[i] = on_pe[c] = put(
                    "pe", go, t, td, [bank_free[acc[c][0]], bank_free[acc[c][1]]] if first else None)

            early_rows = []

            def first_chunk(t_x0, t_n0):
                for i in range(NG):
                    rows_free[i] = q.all_done()
                for _ in select(0, (0,)):
                    pass
                early_rows.extend(gather(table_u, 0, 0, k) for k in range(3))
            t_x, t_n, t_t = into((lambda t: score(0, (0,), t), first_chunk))
            acc_tok = list(t_x)
            score(0, (1,), t_t[1])
            score(1, (0, 1), t_t)

            def chain(*its):
                for it in its:
                    yield from it

            t_ws = {}
            us = [(0, c, k) for c in range(2) for k in range(16)]
            us += [(h, c, k) for h in range(1, 8) for k in range(16) for c in range(2)]
            vs = [(h, c, k) for h in range(8) for k in range(16) for c in range(2)]
            LEAD = 40
            due = []
            nxt = None
            for n in range(len(us) + LEAD):
                if n < len(us):
                    h, c, k = us[n]
                    if n % 32 == 0:
                        if 0 < h < 6:
                            score(h + 2, (0, 1), t_t)
                        nxt = select(h + 1, (0, 1)) if h + 1 < 8 else iter(())
                        if h == 0:
                            nxt = chain(select(0, (1,)), nxt)
                    if h == 0:
                        while (h, c) not in t_sel:
                            next(nxt, None)
                    if n == 16:
                        score(2, (0, 1), t_t)
                    t_u = u_step(h, c, k)
                    for _ in range(6 if h == 0 else 2):
                        next(nxt, None)
                    if n % 32 == 31:
                        for _ in nxt:
                            pass
                        hv = hid3[:, :, h, :]
                        t = put("act", lambda e, hv=hv: e.activation(hv, hv, ACT.Gelu), t_u)
                        due.append((min(n + 3, len(us) - 1), h, hv, t))
                if due and (n >= due[0][0]):
                    _, h, hv, t = due.pop()
                    t_ws[h] = put("dve", lambda e, hv=hv, h=h: e.tensor_tensor(hv, hv, top3[:, :, h, :], ALU.mult),
                                  t, t_gate[h])
                if n >= LEAD:
                    v_step(*vs[n - LEAD], n >= len(us))
            ts = [[], []]
            for c in range(2):
                for hf in range(2):
                    v = x[:, c, hf * 512:(hf + 1) * 512]
                    t = vec(lambda e, v=v, b=acc[c][hf]: e.tensor_tensor(v, v, banks[:, b, :], ALU.add),
                            on_pe[c], acc_tok[c])
                    bank_free[acc[c][hf]] = t
                    held.discard(acc[c][hf])
                    ts[c].append(t)
            return ts

        t_r = peer(0, even_out, early)

        t_fence = q.all_done()
        _, t_h = rmsnorm(g_mix1, t_r, q_pe())
        cw = sm(24)
        t_cw = fetch(cw, a["c_conv"])
        bgT = arena[:, 0:2048].rearrange("p (k t) -> p k t", k=8)
        hxT = arena[:, 2048:4096].rearrange("p (k t) -> p k t", k=8)
        uT = arena[:, 4096:4096 + 8 * 258].rearrange("p (k t) -> p k t", k=8)
        yT = arena[:, 6400:6400 + 2048].rearrange("p (k t) -> p k t", k=8)
        cgT = arena[:, 8448:8448 + 2048].rearrange("p (k t) -> p k t", k=8)
        w = kview(a["odd_w_in_2"][0])
        t_z = put("pool", lambda e: e.memset(uT[:, :, 0:2], 0.0), t_fence)
        t_b = {}
        t_y = []

        def conv(k):
            t = vec(lambda e, k=k: e.tensor_tensor(uT[:, k, 2:258], cgT[:, k, :], hxT[:, k, :], ALU.mult),
                    t_b[4 + k // 2], t_b[8 + k // 2], t_z)
            t = vec(lambda e, k=k: e.tensor_scalar(yT[:, k, :], uT[:, k, 0:256], cw[:, k:k + 1], None,
                                                          ALU.mult), t, t_cw)
            for i in (1, 2):
                t = vec(lambda e, k=k, i=i: e.scalar_tensor_tensor(
                    yT[:, k, :], uT[:, k, i:i + 256], cw[:, 8 * i + k:8 * i + k + 1], yT[:, k, :],
                    ALU.mult, ALU.add), t)
            t = vec(lambda e, k=k: e.tensor_tensor(yT[:, k, :], yT[:, k, :], bgT[:, k, :], ALU.mult), t,
                    t_b[k // 2])
            t_y.append(t)

        for jj in range(12):
            s, wt, t_w = load(w[:, :, 256 * jj:256 * (jj + 1)], 8)
            b = bank()

            def go(e, wt=wt, b=b):
                for f in range(2):
                    for k in range(8):
                        r = e.matmul(banks[:, b, f * T:(f + 1) * T], wt[:, k, f * P:(f + 1) * P], hT[:, k, :],
                                     start=(k == 0), stop=(k == 7))
                return r
            t = put("pe", go, t_w, t_h, bank_free[b])
            slot_free[s] = t
            kd_, k0 = jj // 4, 2 * (jj % 4)
            dst = (bgT, cgT, hxT)[kd_]
            t = evac(dst[:, k0:k0 + 2, :].rearrange("p j t -> p (j t)"), banks[:, b, :], t, t_fence)
            bank_free[b] = t
            t_b[jj] = t
            for k in range(2 * (jj - 8), 2 * (jj - 7)) if jj >= 8 else ():
                conv(k)
        g = load_gain(a["norm_ffn_2"][1])
        early = q.all_done()
        g_fin = load_gain(a["final_norm_2"])

        def odd_out(mid):
            return residual_norm(kview(a["odd_w_out_2"][0]), yT, [t_y, t_y], g, mid)
        t_r = peer(1, odd_out, early)
        toks, _ = rmsnorm(g_fin, t_r, q.all_done(), to_T=False)
        return wrap(nc, ctx, q, finish, xn, toks)


def wrap(nc, ctx, q, finish, src, t):
    finish(src[:, :, :], t)
    block = ctx.enter_context(nc.Block())

    @block.sync
    def _(e):
        q.emit("sp", e)

    @block.tensor
    def _(e):
        q.emit("pe", e)

    @block.vector
    def _(e):
        q.emit("dve", e)

    @block.scalar
    def _(e):
        q.emit("act", e)

    @block.gpsimd
    def _(e):
        q.emit("pool", e)


def constants():
    c = {}
    c["c_ident"] = np.eye(P, dtype=np.float32)
    qi = np.arange(T)[:, None]
    ki = np.arange(T)[None, :]
    d = qi - ki
    band = []
    for dil in (1, 4, 16):
        ok = (d >= 0) & (d % dil == 0) & (d <= 128 * dil)
        band.append(np.where(ok, d, 1e30).astype(np.float32))
    c["c_band"] = np.concatenate([b[0:P, 0:P] for b in band] + [b[P:T] for b in band], axis=1)
    cm = np.where(d >= 0, 0.0, NEG).astype(np.float32)
    c["c_causal"] = np.concatenate([cm[0:P, 0:P], cm[P:T]], axis=1)
    f = (np.float32(10000.0) ** (-np.arange(16, dtype=np.float32) / np.float32(16))).astype(np.float32)
    c["c_freq"] = np.repeat(f[None, :], P, axis=0)
    inv = (np.float32(10000.0) ** (-np.arange(64, dtype=np.float32) / np.float32(64))).astype(np.float32)
    ang = (np.arange(T, dtype=np.float32)[:, None] * inv[None, :]).astype(np.float64)
    tab = np.stack([np.cos(ang), np.sin(ang)]).astype(np.float32)
    c["c_tri"] = np.triu(np.ones((P, P), np.float32), 1)
    c["c_rope2"] = np.ascontiguousarray(tab.reshape(2, 2, P, 64).transpose(2, 0, 1, 3))
    dec = []
    for h in range(4):
        lg = np.log(1.0 - 2.0 ** (-5.0 - h))
        m = np.where(d.T <= 0, np.exp(lg * np.abs(d.T)), 0.0) * 0 + np.where(
            (ki - qi) >= 0, np.exp(lg * np.maximum(ki - qi, 0)), 0.0)
        m = (m * 128 ** -0.5).astype(np.float32)
        dec.append(np.concatenate([m[0:P, :], m[P:T, P:T]], axis=1))
    c["c_decay"] = np.ascontiguousarray(np.stack(dec, axis=1))
    return c


_OUTS = [((1, 256, 1024), "float32")]


def kernel(**inputs):
    import concourse.bacc as _bacc
    from concourse.bass_utils import run_bass_kernel_spmd as _run

    nc = _bacc.Bacc("TRN2", target_bir_lowering=False, num_devices=1)
    data = {k: np.ascontiguousarray(v) for k, v in inputs.items() if k != "peer_sub_keys_2"}
    data.update(constants())
    keys = np.asarray(inputs["peer_sub_keys_2"])
    data["c_keys"] = np.ascontiguousarray(keys.transpose(0, 4, 1, 2, 3).reshape(2, P, 16, P))
    data["c_conv"] = np.ascontiguousarray(data.pop("odd_conv_2")[0].reshape(3, 8, P).transpose(2, 0, 1).reshape(P, 24))
    data["c_pos"] = np.ascontiguousarray(data.pop("positions").reshape(2, P).T)
    arrays, args = {}, {}
    for name, v in data.items():
        arrays[f"in_{name}_dram"] = v
        args[name] = nc.dram_tensor(f"in_{name}_dram", v.shape, mybir.dt.from_np(v.dtype),
                                    kind="ExternalInput").ap()
    outs = [nc.dram_tensor(f"out_{i}_dram", shape, mybir.dt.from_np(np.dtype(dt)), kind="ExternalOutput").ap()
            for i, (shape, dt) in enumerate(_OUTS)]
    build(nc, args, outs[0])
    r = _run(nc, [arrays], core_ids=[0])
    return r.results[0]["out_0_dram"]
```
